# Optimizing a Trainium2 kernel written in Bass

```python
import math, functools
import jax, jax.numpy as jnp
from jax import lax
import numpy as np
import math

D_MODEL = 1024
BATCH = 1
SEQ = 256
DEPTH = 2

GRID_W = 64
CTX_LEN = 256
N_MIXERS = 2
N_A_LAYERS = (DEPTH + 1) // 2
N_B_LAYERS = DEPTH // 2
D_FF = 2816
N_MOD = 9
EPS = 1e-6
ROPE_BASE = 10000.0
Q_BLOCK = 128
NEG_INF = -1e30

A_HEADS = 8
A_HEAD_DIM = 64
A_V_DIM = 2 * A_HEAD_DIM
A_QKV_COLS = 3 * A_HEADS * A_V_DIM
A_WIDTH = A_HEADS * A_V_DIM

B_Q_HEADS = 16
B_KV_HEADS = 4
B_HEAD_DIM = 64
B_GROUP = B_Q_HEADS // B_KV_HEADS
B_QKV_COLS = (B_Q_HEADS + 2 * B_KV_HEADS) * B_HEAD_DIM
B_WIDTH = B_Q_HEADS * B_HEAD_DIM
WINDOW = 128
BAND_BLOCK = 128


def rms(x):
    xf = x.astype(jnp.float32)
    return (xf * lax.rsqrt(jnp.mean(xf * xf, axis=-1, keepdims=True) + EPS)).astype(x.dtype)

def rms_gain(x, g):
    return rms(x) * g

def modulate(h, shift, scale):
    return h * (1 + scale) + shift

def swiglu(h, wi, wo):
    g, u = jnp.split(h @ wi, 2, axis=-1)
    return (jax.nn.silu(g) * u) @ wo

def axial_rope_tables(rows, head_dim):
    nf = head_dim // 4
    inv = ROPE_BASE ** (-jnp.arange(nf, dtype=jnp.float32) / nf)
    row = jnp.broadcast_to(jnp.arange(rows, dtype=jnp.float32)[:, None], (rows, GRID_W)).reshape(-1)
    col = jnp.broadcast_to(jnp.arange(GRID_W, dtype=jnp.float32)[None, :], (rows, GRID_W)).reshape(-1)
    ang = jnp.stack([row[:, None] * inv, col[:, None] * inv], axis=1)
    ang = jnp.stack([ang, ang], axis=2).reshape(rows * GRID_W, head_dim)
    return jnp.cos(ang), jnp.sin(ang)

def apply_rope(x, cos, sin):
    dh = x.shape[-1]
    xr = x.reshape(x.shape[:-1] + (2, 2, dh // 4))
    rot = jnp.stack([-xr[..., 1, :], xr[..., 0, :]], axis=-2).reshape(x.shape)
    return (x * cos + rot * sin).astype(x.dtype)

def diff_attention(h_lat, h_ctx, w_qkv, w_o, q_gain, k_gain, lam_vec, subln_gain, lam_init, cos, sin, ctx_out):
    B, L, _ = h_lat.shape

    def project(h):
        q, k, v = jnp.split(h @ w_qkv, [A_WIDTH, 2 * A_WIDTH], axis=-1)
        q = rms_gain(q.reshape(B, -1, A_HEADS, 2, A_HEAD_DIM), q_gain)
        k = rms_gain(k.reshape(B, -1, A_HEADS, 2, A_HEAD_DIM), k_gain)
        return q, k, v.reshape(B, -1, A_HEADS, A_V_DIM)

    q_l, k_l, v_l = project(h_lat)
    q_c, k_c, v_c = project(h_ctx)
    rc, rs = cos[:, None, None, :], sin[:, None, None, :]
    q_l, k_l = apply_rope(q_l, rc, rs), apply_rope(k_l, rc, rs)

    lv = lam_vec.astype(jnp.float32)
    lam = jnp.exp(jnp.sum(lv[0] * lv[1])) - jnp.exp(jnp.sum(lv[2] * lv[3])) + lam_init
    scale = A_HEAD_DIM ** -0.5

    def attend(q, k, v):
        s = jnp.einsum('bqhcd,bkhcd->bhcqk', q, k).astype(jnp.float32) * scale
        p = jax.nn.softmax(s, axis=-1)
        a = (p[:, :, 0] - lam * p[:, :, 1]).astype(v.dtype)
        return jnp.einsum('bhqk,bkhe->bqhe', a, v)

    def finish(o):
        o = rms_gain(o, subln_gain) * (1.0 - lam_init)
        return o.reshape(o.shape[0], o.shape[1], A_WIDTH) @ w_o

    k_all = jnp.concatenate([k_l, k_c], axis=1)
    v_all = jnp.concatenate([v_l, v_c], axis=1)
    nb = L // Q_BLOCK
    qb = q_l.reshape(B, nb, Q_BLOCK, A_HEADS, 2, A_HEAD_DIM).transpose(1, 0, 2, 3, 4, 5)
    o_l = lax.map(lambda qblk: attend(qblk, k_all, v_all), qb)
    o_l = o_l.transpose(1, 0, 2, 3, 4).reshape(B, L, A_HEADS, A_V_DIM)
    out_l = finish(o_l)
    out_c = finish(attend(q_c, k_c, v_c)) if ctx_out else None
    return out_l, out_c

def window_gqa(h_lat, h_ctx, w_qkv, w_o, q_gain, k_gain, sink, cos, sin, ctx_out):
    B, L, _ = h_lat.shape
    nb = L // BAND_BLOCK
    BB = BAND_BLOCK

    def project(h):
        q, k, v = jnp.split(h @ w_qkv, [B_WIDTH, B_WIDTH + B_KV_HEADS * B_HEAD_DIM], axis=-1)
        q = rms_gain(q.reshape(B, -1, B_KV_HEADS, B_GROUP, B_HEAD_DIM), q_gain)
        k = rms_gain(k.reshape(B, -1, B_KV_HEADS, B_HEAD_DIM), k_gain)
        return q, k, v.reshape(B, -1, B_KV_HEADS, B_HEAD_DIM)

    q_l, k_l, v_l = project(h_lat)
    q_c, k_c, v_c = project(h_ctx)
    q_l = apply_rope(q_l, cos[:, None, None, :], sin[:, None, None, :])
    k_l = apply_rope(k_l, cos[:, None, :], sin[:, None, :])
    scale = B_HEAD_DIM ** -0.5
    sink_f = sink.astype(jnp.float32).reshape(B_KV_HEADS, B_GROUP)

    def band(t):
        tb = jnp.pad(t, ((0, 0), (BB, BB), (0, 0), (0, 0))).reshape(B, nb + 2, BB, B_KV_HEADS, B_HEAD_DIM)
        return jnp.concatenate([tb[:, :-2], tb[:, 1:-1], tb[:, 2:]], axis=2)

    k_w, v_w = band(k_l), band(v_l)
    qb = q_l.reshape(B, nb, BB, B_KV_HEADS, B_GROUP, B_HEAD_DIM)
    s_w = jnp.einsum('bnqhgd,bnkhd->bnhgqk', qb, k_w).astype(jnp.float32) * scale
    s_c = jnp.einsum('bnqhgd,bkhd->bnhgqk', qb, k_c).astype(jnp.float32) * scale
    qi = jnp.arange(BB)
    kj = jnp.arange(3 * BB)
    rel = kj[None, :] - BB - qi[:, None]
    kpos = jnp.arange(nb)[:, None] * BB - BB + kj[None, :]
    valid = (jnp.abs(rel) <= WINDOW)[None] & ((kpos >= 0) & (kpos < L))[:, None, :]
    s_w = jnp.where(valid[None, :, None, None], s_w, NEG_INF)
    sink_b = jnp.broadcast_to(sink_f[None, None, :, :, None, None], s_w.shape[:-1] + (1,))
    n_ctx = k_c.shape[1]
    p = jax.nn.softmax(jnp.concatenate([s_w, s_c, sink_b], axis=-1), axis=-1)
    p_w = p[..., :3 * BB].astype(v_w.dtype)
    p_c = p[..., 3 * BB:3 * BB + n_ctx].astype(v_c.dtype)
    o = jnp.einsum('bnhgqk,bnkhd->bnqhgd', p_w, v_w) + jnp.einsum('bnhgqk,bkhd->bnqhgd', p_c, v_c)
    out_l = o.reshape(B, L, B_WIDTH) @ w_o
    out_c = None
    if ctx_out:
        s = jnp.einsum('bqhgd,bkhd->bhgqk', q_c, k_c).astype(jnp.float32) * scale
        sb = jnp.broadcast_to(sink_f[None, :, :, None, None], s.shape[:-1] + (1,))
        pc = jax.nn.softmax(jnp.concatenate([s, sb], axis=-1), axis=-1)[..., :n_ctx].astype(v_c.dtype)
        oc = jnp.einsum('bhgqk,bkhd->bqhgd', pc, v_c)
        out_c = oc.reshape(B, n_ctx, B_WIDTH) @ w_o
    return out_l, out_c

def layer(x, xc, mod_l, mod_c, pre_wi, pre_wo, post_wi, post_wo, mixer, ctx_out):
    sh1, sc1, g1, sh2, sc2, g2, sh3, sc3, g3 = jnp.split(mod_l, N_MOD, axis=-1)
    ch1, cc1, cg1, ch2, cc2, cg2, ch3, cc3, cg3 = jnp.split(mod_c, N_MOD, axis=-1)

    def ffn_step(t, sh, sc, g, wi, wo):
        return t + 0.5 * g * swiglu(modulate(rms(t), sh, sc), wi, wo)

    x = ffn_step(x, sh1, sc1, g1, pre_wi, pre_wo)
    xc = ffn_step(xc, ch1, cc1, cg1, pre_wi, pre_wo)
    o_l, o_c = mixer(h_lat=modulate(rms(x), sh2, sc2), h_ctx=modulate(rms(xc), ch2, cc2), ctx_out=ctx_out)
    x = x + g2 * o_l
    x = ffn_step(x, sh3, sc3, g3, post_wi, post_wo)
    if ctx_out:
        xc = xc + cg2 * o_c
        xc = ffn_step(xc, ch3, cc3, cg3, post_wi, post_wo)
    return x, xc

def first_inputs(seed: int = 0) -> dict:
    key = jax.random.key(seed)
    ks = jax.random.split(key, 24)
    f32 = jnp.float32
    D = D_MODEL

    def nrm(k, shape, s):
        return jax.random.normal(k, shape, f32) * s

    return {
        "x": nrm(ks[0], (BATCH, SEQ, D), 1.0),
        "c": nrm(ks[1], (BATCH, D), 1.0),
        "ctx": nrm(ks[2], (BATCH, CTX_LEN, D), 1.0),
        "c_ctx": nrm(ks[3], (D,), 1.0),
        "ada_w": nrm(ks[4], (DEPTH, D, N_MOD * D), 0.5 * D ** -0.5),
        "ada_b": nrm(ks[5], (DEPTH, N_MOD * D), 0.02),
        "ffn_pre_wi": nrm(ks[6], (DEPTH, D, 2 * D_FF), D ** -0.5),
        "ffn_pre_wo": nrm(ks[7], (DEPTH, D_FF, D), D_FF ** -0.5),
        "ffn_post_wi": nrm(ks[8], (DEPTH, D, 2 * D_FF), D ** -0.5),
        "ffn_post_wo": nrm(ks[9], (DEPTH, D_FF, D), D_FF ** -0.5),
        "a_w_qkv": nrm(ks[10], (N_A_LAYERS, D, A_QKV_COLS), D ** -0.5),
        "a_w_o": nrm(ks[11], (N_A_LAYERS, A_WIDTH, D), A_WIDTH ** -0.5),
        "a_q_gain": 1.0 + nrm(ks[12], (N_A_LAYERS, A_HEAD_DIM), 0.1),
        "a_k_gain": 1.0 + nrm(ks[13], (N_A_LAYERS, A_HEAD_DIM), 0.1),
        "a_lambda": nrm(ks[14], (N_A_LAYERS, 4, A_HEAD_DIM), 0.1),
        "a_subln_gain": 1.0 + nrm(ks[15], (N_A_LAYERS, A_V_DIM), 0.1),
        "b_w_qkv": nrm(ks[16], (N_B_LAYERS, D, B_QKV_COLS), D ** -0.5),
        "b_w_o": nrm(ks[17], (N_B_LAYERS, B_WIDTH, D), B_WIDTH ** -0.5),
        "b_q_gain": 1.0 + nrm(ks[18], (N_B_LAYERS, B_HEAD_DIM), 0.1),
        "b_k_gain": 1.0 + nrm(ks[19], (N_B_LAYERS, B_HEAD_DIM), 0.1),
        "b_sink": nrm(ks[20], (N_B_LAYERS, B_Q_HEADS), 0.5),
    }

def first_block(x, c, ctx, c_ctx, ada_w, ada_b, ffn_pre_wi, ffn_pre_wo, ffn_post_wi, ffn_post_wo,
              a_w_qkv, a_w_o, a_q_gain, a_k_gain, a_lambda, a_subln_gain,
              b_w_qkv, b_w_o, b_q_gain, b_k_gain, b_sink):
    n_tok = x.shape[1]
    rows = n_tok // GRID_W
    cos, sin = axial_rope_tables(rows, A_HEAD_DIM)
    xc = ctx
    for i in range(DEPTH):
        mod_l = (jax.nn.silu(c) @ ada_w[i] + ada_b[i])[:, None, :]
        mod_c = jax.nn.silu(c_ctx) @ ada_w[i] + ada_b[i]
        ctx_out = i < DEPTH - 1
        j = i // N_MIXERS
        if i % N_MIXERS == 0:
            mixer = functools.partial(diff_attention, w_qkv=a_w_qkv[j], w_o=a_w_o[j], q_gain=a_q_gain[j],
                                      k_gain=a_k_gain[j], lam_vec=a_lambda[j], subln_gain=a_subln_gain[j],
                                      lam_init=0.8 - 0.6 * math.exp(-0.3 * i), cos=cos, sin=sin)
        else:
            mixer = functools.partial(window_gqa, w_qkv=b_w_qkv[j], w_o=b_w_o[j], q_gain=b_q_gain[j],
                                      k_gain=b_k_gain[j], sink=b_sink[j], cos=cos, sin=sin)
        x, xc = layer(x, xc, mod_l, mod_c, ffn_pre_wi[i], ffn_pre_wo[i], ffn_post_wi[i], ffn_post_wo[i],
                      mixer, ctx_out)
    return x


HEAD_DIM = 64
NORM_EPS = 1e-6

RWKV_HEADS = 8
RWKV_WIDTH = RWKV_HEADS * HEAD_DIM
RWKV_DECAY_RANK = 64
RWKV_ICLR_RANK = 64
RWKV_GATE_RANK = 128
RWKV_GN_EPS = 64e-5

NSA_Q_HEADS = 8
NSA_KV_GROUPS = 2
NSA_CMP_LEN = 32
NSA_CMP_STRIDE = 16
NSA_CMP_HIDDEN = 256
NSA_SEL_BLOCK = 64
NSA_SEL_TOPN = 16
NSA_WINDOW = 512
NSA_FORCE_SCORE = 1e9

SWA_Q_HEADS = 8
SWA_KV_HEADS = 2
SWA_WINDOW = 128

REL_BUCKETS = 32
REL_MAX_DIST = 128

PEER_HEADS = 8
PEER_NKEYS = 128
PEER_EXPERTS = PEER_NKEYS * PEER_NKEYS
PEER_QDIM = 256
PEER_TOPK = 16
PEER_TOK_BLOCK = 128

RWKV_SPLITS = (RWKV_WIDTH, RWKV_WIDTH, RWKV_WIDTH, RWKV_DECAY_RANK, RWKV_ICLR_RANK, RWKV_GATE_RANK)
NSA_SPLITS = (NSA_Q_HEADS * HEAD_DIM,) + (NSA_KV_GROUPS * HEAD_DIM,) * 6 + (NSA_Q_HEADS * 3,)
SWA_SPLITS = (SWA_Q_HEADS * HEAD_DIM, SWA_KV_HEADS * HEAD_DIM, SWA_KV_HEADS * HEAD_DIM)
GATE_SPLITS = (D_MODEL, D_MODEL, D_MODEL)
RWKV_COLS = sum(RWKV_SPLITS)
IN_SPLITS = RWKV_SPLITS + NSA_SPLITS + SWA_SPLITS + GATE_SPLITS
IN_COLS = sum(IN_SPLITS)


def split_cols(z, sizes):
    cuts = [int(c) for c in np.cumsum(sizes)[:-1]]
    return jnp.split(z, cuts, axis=-1)

def rmsnorm(x, w):
    xf = x.astype(jnp.float32)
    y = xf * lax.rsqrt(jnp.mean(xf * xf, axis=-1, keepdims=True) + NORM_EPS)
    return (y * w.astype(jnp.float32)).astype(x.dtype)

def token_shift(z, mu):
    z_prev = jnp.pad(z, ((0, 0), (1, 0), (0, 0)))[:, :-1]
    return z + mu * (z_prev - z)

def t5_bucket(dist):
    n = jnp.maximum(dist, 0)
    max_exact = REL_BUCKETS // 2
    nf = jnp.maximum(n, max_exact).astype(jnp.float32)
    large = max_exact + (jnp.log(nf / max_exact) / math.log(REL_MAX_DIST / max_exact)
                         * (REL_BUCKETS - max_exact)).astype(jnp.int32)
    large = jnp.minimum(large, REL_BUCKETS - 1)
    return jnp.where(n < max_exact, n, large)

def masked_softmax(s, mask):
    s = jnp.where(mask, s.astype(jnp.float32), -jnp.inf)
    m = jnp.max(s, axis=-1, keepdims=True)
    m = jnp.where(jnp.isfinite(m), m, 0.0)
    e = jnp.exp(s - m)
    return e / jnp.maximum(jnp.sum(e, axis=-1, keepdims=True), 1e-30)

def sink_softmax(s, mask, sink):
    s = jnp.where(mask, s.astype(jnp.float32), -jnp.inf)
    sink = sink.astype(jnp.float32)[None, :, :, None, None]
    m = jnp.maximum(jnp.max(s, axis=-1, keepdims=True), sink)
    e = jnp.exp(s - m)
    return e / (jnp.sum(e, axis=-1, keepdims=True) + jnp.exp(sink - m))

def rwkv7_mixer(zr, zk, zv, zw, za, zg, w0, w2, a0, a2, g2, k_k, k_a, r_k, ln_w, ln_b):
    B, S, C = zr.shape
    H, N = RWKV_HEADS, HEAD_DIM
    f32 = jnp.float32
    log_w = -jax.nn.softplus(-(w0 + jnp.tanh(zw) @ w2)) - 0.5
    decay = jnp.exp(-jnp.exp(log_w.astype(f32)))
    a = jax.nn.sigmoid(a0 + za @ a2)
    g = jax.nn.sigmoid(zg) @ g2
    kk = (zk * k_k).reshape(B, S, H, N).astype(f32)
    kk = kk * lax.rsqrt(jnp.maximum(jnp.sum(kk * kk, axis=-1, keepdims=True), 1e-12))
    k = zk * (1.0 + (a - 1.0) * k_a)
    hd = lambda z: z.reshape(B, S, H, N).astype(f32)
    r_h, k_h, v_h, a_h, w_h = hd(zr), hd(k), hd(zv), hd(a), hd(decay)
    tm = lambda z: jnp.swapaxes(z, 0, 1)

    def step(state, inp):
        r_t, w_t, k_t, v_t, kk_t, a_t = inp
        sa = jnp.einsum('bhij,bhj->bhi', state, -kk_t)
        state = (state * w_t[:, :, None, :] + sa[..., None] * (kk_t * a_t)[:, :, None, :]
                 + v_t[..., None] * k_t[:, :, None, :])
        return state, jnp.einsum('bhij,bhj->bhi', state, r_t)

    s0 = jnp.zeros((B, H, N, N), f32)
    _, y = lax.scan(step, s0, (tm(r_h), tm(w_h), tm(k_h), tm(v_h), tm(kk), tm(a_h)))
    y = tm(y)
    mu = jnp.mean(y, axis=-1, keepdims=True)
    var = jnp.mean(jnp.square(y - mu), axis=-1, keepdims=True)
    y = ((y - mu) * lax.rsqrt(var + RWKV_GN_EPS)).reshape(B, S, C) * ln_w + ln_b
    bonus = jnp.sum(r_h * k_h * r_k, axis=-1, keepdims=True) * v_h
    out = (y + bonus.reshape(B, S, C)) * g
    return out.astype(zr.dtype)

def nsa_compress(z, pe, w1, w2):
    B, S, G, dh = z.shape
    n_sub = NSA_CMP_LEN // NSA_CMP_STRIDE
    chunks = z.reshape(B, S // NSA_CMP_STRIDE, NSA_CMP_STRIDE, G, dh)
    n_cmp = S // NSA_CMP_STRIDE - n_sub + 1
    blocks = jnp.concatenate([chunks[:, j:j + n_cmp] for j in range(n_sub)], axis=2)
    blocks = blocks + pe[None, None, :, None, :]
    flat = blocks.transpose(0, 3, 1, 2, 4).reshape(B, G, n_cmp, NSA_CMP_LEN * dh)
    return jax.nn.gelu(flat @ w1, approximate=False) @ w2

def nsa_mixer(q, kc, vc, ks, vs, kw, vw, gates, pe_k, pe_v, ck_w1, ck_w2, cv_w1, cv_w2, bias_tbl):
    B, S, _ = q.shape
    G, Hg, dh = NSA_KV_GROUPS, NSA_Q_HEADS // NSA_KV_GROUPS, HEAD_DIM
    scale = dh ** -0.5
    heads = lambda z: z.reshape(B, S, G, dh)
    kv_t = lambda z: heads(z).transpose(0, 2, 1, 3)
    qh = q.reshape(B, S, G, Hg, dh).transpose(0, 2, 3, 1, 4)
    gh = jax.nn.sigmoid(gates.reshape(B, S, G, Hg, 3)).transpose(0, 2, 3, 1, 4)

    k_cmp = nsa_compress(heads(kc), pe_k, ck_w1, ck_w2)
    v_cmp = nsa_compress(heads(vc), pe_v, cv_w1, cv_w2)
    n_cmp = k_cmp.shape[2]
    cmp_start = jnp.arange(n_cmp) * NSA_CMP_STRIDE
    cmp_end = cmp_start + NSA_CMP_LEN - 1
    n_sel = S // NSA_SEL_BLOCK
    sel_start = jnp.arange(n_sel) * NSA_SEL_BLOCK
    overlap = ((cmp_end[:, None] >= sel_start[None, :])
               & (cmp_start[:, None] <= sel_start[None, :] + NSA_SEL_BLOCK - 1)).astype(jnp.float32)
    ks_blk = kv_t(ks).reshape(B, G, n_sel, NSA_SEL_BLOCK, dh)
    vs_blk = kv_t(vs).reshape(B, G, n_sel, NSA_SEL_BLOCK, dh)
    pad = ((0, 0), (0, 0), (NSA_WINDOW, 0), (0, 0))
    kw_pad = jnp.pad(kv_t(kw), pad)
    vw_pad = jnp.pad(kv_t(vw), pad)

    tbl = bias_tbl.T.reshape(G, Hg, REL_BUCKETS)
    win_len = NSA_WINDOW + Q_BLOCK
    rel = jnp.arange(Q_BLOCK)[:, None] + NSA_WINDOW - jnp.arange(win_len)[None, :]
    win_bias = tbl[:, :, t5_bucket(rel)]
    win_rel_mask = (rel >= 0) & (rel < NSA_WINDOW)
    top_n = min(NSA_SEL_TOPN, n_sel)
    b_ix = jnp.arange(B)[:, None, None, None]
    g_ix = jnp.arange(G)[None, :, None, None]
    g_ix5 = jnp.arange(G)[None, :, None, None, None]
    h_ix5 = jnp.arange(Hg)[None, None, :, None, None]
    blk = jnp.arange(n_sel)

    def block(i):
        s0 = i * Q_BLOCK
        t = s0 + jnp.arange(Q_BLOCK)
        qb = lax.dynamic_slice_in_dim(qh, s0, Q_BLOCK, axis=3)
        gb = lax.dynamic_slice_in_dim(gh, s0, Q_BLOCK, axis=3)
        sc = jnp.einsum('bghqd,bgcd->bghqc', qb, k_cmp) * scale
        pc = masked_softmax(sc, cmp_end[None, :] <= t[:, None])
        o_cmp = jnp.einsum('bghqc,bgcd->bghqd', pc.astype(v_cmp.dtype), v_cmp)
        imp = jnp.einsum('bghqc,cn->bgqn', pc, overlap)
        cur = t // NSA_SEL_BLOCK
        forced = (blk[None, :] == 0) | (blk[None, :] == cur[:, None]) | (blk[None, :] == cur[:, None] - 1)
        valid = blk[None, :] <= cur[:, None]
        imp = jnp.where(forced, NSA_FORCE_SCORE, jnp.where(valid, imp, -1.0))
        _, sel = lax.top_k(imp, top_n)
        k_sel = ks_blk[b_ix, g_ix, sel].reshape(B, G, Q_BLOCK, top_n * NSA_SEL_BLOCK, dh)
        v_sel = vs_blk[b_ix, g_ix, sel].reshape(B, G, Q_BLOCK, top_n * NSA_SEL_BLOCK, dh)
        pos = (sel[..., None] * NSA_SEL_BLOCK + jnp.arange(NSA_SEL_BLOCK)).reshape(B, G, Q_BLOCK, top_n * NSA_SEL_BLOCK)
        dist = t[:, None] - pos
        bias = tbl[g_ix5, h_ix5, t5_bucket(dist)[:, :, None]]
        ss = jnp.einsum('bghqd,bgqkd->bghqk', qb, k_sel) * scale + bias
        ps = masked_softmax(ss, (dist >= 0)[:, :, None])
        o_sel = jnp.einsum('bghqk,bgqkd->bghqd', ps.astype(v_sel.dtype), v_sel)
        k_win = lax.dynamic_slice_in_dim(kw_pad, s0, win_len, axis=2)
        v_win = lax.dynamic_slice_in_dim(vw_pad, s0, win_len, axis=2)
        kpos = s0 - NSA_WINDOW + jnp.arange(win_len)
        sw = jnp.einsum('bghqd,bgkd->bghqk', qb, k_win) * scale + win_bias
        pw = masked_softmax(sw, win_rel_mask & (kpos >= 0)[None, :])
        o_win = jnp.einsum('bghqk,bgkd->bghqd', pw.astype(v_win.dtype), v_win)
        return gb[..., 0:1] * o_cmp + gb[..., 1:2] * o_sel + gb[..., 2:3] * o_win

    out = lax.map(block, jnp.arange(S // Q_BLOCK))
    return out.transpose(1, 0, 4, 2, 3, 5).reshape(B, S, G * Hg * dh)

def swa_sink_mixer(q, k, v, sinks, bias_tbl):
    B, S, _ = q.shape
    G, Hg, dh = SWA_KV_HEADS, SWA_Q_HEADS // SWA_KV_HEADS, HEAD_DIM
    scale = dh ** -0.5
    qh = q.reshape(B, S, G, Hg, dh).transpose(0, 2, 3, 1, 4)
    pad = ((0, 0), (0, 0), (SWA_WINDOW, 0), (0, 0))
    k_pad = jnp.pad(k.reshape(B, S, G, dh).transpose(0, 2, 1, 3), pad)
    v_pad = jnp.pad(v.reshape(B, S, G, dh).transpose(0, 2, 1, 3), pad)
    win_len = SWA_WINDOW + Q_BLOCK
    rel = jnp.arange(Q_BLOCK)[:, None] + SWA_WINDOW - jnp.arange(win_len)[None, :]
    bias = bias_tbl.T.reshape(G, Hg, REL_BUCKETS)[:, :, t5_bucket(rel)]
    rel_mask = (rel >= 0) & (rel < SWA_WINDOW)
    sink = sinks.reshape(G, Hg)

    def block(i):
        s0 = i * Q_BLOCK
        qb = lax.dynamic_slice_in_dim(qh, s0, Q_BLOCK, axis=3)
        kb = lax.dynamic_slice_in_dim(k_pad, s0, win_len, axis=2)
        vb = lax.dynamic_slice_in_dim(v_pad, s0, win_len, axis=2)
        kpos = s0 - SWA_WINDOW + jnp.arange(win_len)
        s = jnp.einsum('bghqd,bgkd->bghqk', qb, kb) * scale + bias
        p = sink_softmax(s, rel_mask & (kpos >= 0)[None, :], sink)
        return jnp.einsum('bghqk,bgkd->bghqd', p.astype(vb.dtype), vb)

    out = lax.map(block, jnp.arange(S // Q_BLOCK))
    return out.transpose(1, 0, 4, 2, 3, 5).reshape(B, S, G * Hg * dh)

def peer_ffn(z, wq, subkeys, u_tab, v_tab):
    B, S, D = z.shape
    Hp, K, half = PEER_HEADS, PEER_TOPK, PEER_QDIM // 2
    zt = z.reshape(B * S // PEER_TOK_BLOCK, PEER_TOK_BLOCK, D)

    def block(zb):
        q = (zb @ wq).reshape(PEER_TOK_BLOCK, Hp, 2, half)
        s = jnp.einsum('thpd,hpnd->thpn', q, subkeys).astype(jnp.float32)
        s_top, i_top = lax.top_k(s, K)
        cand = (s_top[:, :, 0, :, None] + s_top[:, :, 1, None, :]).reshape(PEER_TOK_BLOCK, Hp, K * K)
        score, flat = lax.top_k(cand, K)
        i1 = jnp.take_along_axis(i_top[:, :, 0], flat // K, axis=-1)
        i2 = jnp.take_along_axis(i_top[:, :, 1], flat % K, axis=-1)
        expert = i1 * PEER_NKEYS + i2
        gate = jax.nn.softmax(score, axis=-1)
        h = jnp.einsum('thkd,td->thk', u_tab[expert], zb).astype(jnp.float32)
        act = (gate * jax.nn.gelu(h, approximate=False)).astype(zb.dtype)
        return jnp.einsum('thk,thkd->td', act, v_tab[expert])

    return lax.map(block, zt).reshape(B, S, D)

def second_inputs(seed: int = 0) -> dict:
    key = jax.random.key(seed)
    keys = iter(jax.random.split(key, 40))
    L, D = DEPTH, D_MODEL

    def nrm(shape, scale):
        return jax.random.normal(next(keys), shape, jnp.float32) * scale

    def unif(shape, lo, hi):
        return jax.random.uniform(next(keys), shape, jnp.float32, lo, hi)

    cmp_in = NSA_CMP_LEN * HEAD_DIM
    return {
        'x': nrm((BATCH, SEQ, D), 1.0),
        'ln1_w': 1.0 + nrm((L, D), 0.02),
        'ln2_w': 1.0 + nrm((L, D), 0.02),
        'lnf_w': 1.0 + nrm((D,), 0.02),
        'rel_bias': nrm((REL_BUCKETS, NSA_Q_HEADS + SWA_Q_HEADS), 0.3),
        'w_in': nrm((L, D, IN_COLS), D ** -0.5),
        'rwkv_mu': unif((L, RWKV_COLS), 0.0, 1.0),
        'rwkv_w0': -0.5 + nrm((L, RWKV_WIDTH), 0.5),
        'rwkv_w2': nrm((L, RWKV_DECAY_RANK, RWKV_WIDTH), 0.1),
        'rwkv_a0': nrm((L, RWKV_WIDTH), 0.3),
        'rwkv_a2': nrm((L, RWKV_ICLR_RANK, RWKV_WIDTH), 0.1),
        'rwkv_g2': nrm((L, RWKV_GATE_RANK, RWKV_WIDTH), RWKV_GATE_RANK ** -0.5),
        'rwkv_k_k': 0.85 + nrm((L, RWKV_WIDTH), 0.05),
        'rwkv_k_a': 1.0 + nrm((L, RWKV_WIDTH), 0.05),
        'rwkv_r_k': nrm((L, RWKV_HEADS, HEAD_DIM), 0.1),
        'rwkv_ln_w': 1.0 + nrm((L, RWKV_WIDTH), 0.02),
        'rwkv_ln_b': nrm((L, RWKV_WIDTH), 0.02),
        'nsa_pe_k': nrm((L, NSA_CMP_LEN, HEAD_DIM), 0.1),
        'nsa_pe_v': nrm((L, NSA_CMP_LEN, HEAD_DIM), 0.1),
        'nsa_ck_w1': nrm((L, cmp_in, NSA_CMP_HIDDEN), cmp_in ** -0.5),
        'nsa_ck_w2': nrm((L, NSA_CMP_HIDDEN, HEAD_DIM), NSA_CMP_HIDDEN ** -0.5),
        'nsa_cv_w1': nrm((L, cmp_in, NSA_CMP_HIDDEN), cmp_in ** -0.5),
        'nsa_cv_w2': nrm((L, NSA_CMP_HIDDEN, HEAD_DIM), NSA_CMP_HIDDEN ** -0.5),
        'swa_sinks': nrm((L, SWA_Q_HEADS), 0.5),
        'w_br_a': nrm((L, RWKV_WIDTH, D), RWKV_WIDTH ** -0.5),
        'w_br_b': nrm((L, NSA_Q_HEADS * HEAD_DIM, D), (NSA_Q_HEADS * HEAD_DIM) ** -0.5),
        'w_br_c': nrm((L, SWA_Q_HEADS * HEAD_DIM, D), (SWA_Q_HEADS * HEAD_DIM) ** -0.5),
        'w_out': nrm((L, D, D), D ** -0.5),
        'peer_wq': nrm((L, D, PEER_HEADS * PEER_QDIM), D ** -0.5),
        'peer_subkeys': nrm((L, PEER_HEADS, 2, PEER_NKEYS, PEER_QDIM // 2), (PEER_QDIM // 2) ** -0.5),
        'peer_u': nrm((L, PEER_EXPERTS, D), D ** -0.5),
        'peer_v': nrm((L, PEER_EXPERTS, D), 0.5 * PEER_HEADS ** -0.5),
    }

def second_block(x, ln1_w, ln2_w, lnf_w, rel_bias, w_in, rwkv_mu, rwkv_w0, rwkv_w2, rwkv_a0, rwkv_a2,
              rwkv_g2, rwkv_k_k, rwkv_k_a, rwkv_r_k, rwkv_ln_w, rwkv_ln_b, nsa_pe_k, nsa_pe_v,
              nsa_ck_w1, nsa_ck_w2, nsa_cv_w1, nsa_cv_w2, swa_sinks, w_br_a, w_br_b, w_br_c, w_out,
              peer_wq, peer_subkeys, peer_u, peer_v):
    nsa_tbl = rel_bias[:, :NSA_Q_HEADS]
    swa_tbl = rel_bias[:, NSA_Q_HEADS:]
    for l in range(DEPTH):
        u = rmsnorm(x, ln1_w[l])
        proj = u @ w_in[l]
        rw = token_shift(proj[..., :RWKV_COLS], rwkv_mu[l])
        zr, zk, zv, zw, za, zg = split_cols(rw, RWKV_SPLITS)
        cols = split_cols(proj[..., RWKV_COLS:], NSA_SPLITS + SWA_SPLITS + GATE_SPLITS)
        nq, nkc, nvc, nks, nvs, nkw, nvw, ngate = cols[:8]
        sq, sk, sv = cols[8:11]
        g_a, g_b, g_c = [jax.nn.sigmoid(c) for c in cols[11:14]]
        o_a = rwkv7_mixer(zr, zk, zv, zw, za, zg, rwkv_w0[l], rwkv_w2[l], rwkv_a0[l], rwkv_a2[l],
                          rwkv_g2[l], rwkv_k_k[l], rwkv_k_a[l], rwkv_r_k[l], rwkv_ln_w[l], rwkv_ln_b[l])
        o_b = nsa_mixer(nq, nkc, nvc, nks, nvs, nkw, nvw, ngate, nsa_pe_k[l], nsa_pe_v[l],
                        nsa_ck_w1[l], nsa_ck_w2[l], nsa_cv_w1[l], nsa_cv_w2[l], nsa_tbl)
        o_c = swa_sink_mixer(sq, sk, sv, swa_sinks[l], swa_tbl)
        merged = g_a * (o_a @ w_br_a[l]) + g_b * (o_b @ w_br_b[l]) + g_c * (o_c @ w_br_c[l])
        x = x + merged @ w_out[l]
        x = x + peer_ffn(rmsnorm(x, ln2_w[l]), peer_wq[l], peer_subkeys[l], peer_u[l], peer_v[l])
    return rmsnorm(x, lnf_w)


def setup_inputs(seed=0):
    out = dict(first_inputs(seed))
    for name, value in second_inputs(seed + 1).items():
        if name != "x":
            out[name + "_2"] = value
    return out


def reference(
    x, c, ctx, c_ctx, ada_w, ada_b, ffn_pre_wi, ffn_pre_wo, ffn_post_wi, ffn_post_wo, a_w_qkv,
    a_w_o, a_q_gain, a_k_gain, a_lambda, a_subln_gain, b_w_qkv, b_w_o, b_q_gain, b_k_gain,
    b_sink, ln1_w_2, ln2_w_2, lnf_w_2, rel_bias_2, w_in_2, rwkv_mu_2, rwkv_w0_2, rwkv_w2_2,
    rwkv_a0_2, rwkv_a2_2, rwkv_g2_2, rwkv_k_k_2, rwkv_k_a_2, rwkv_r_k_2, rwkv_ln_w_2,
    rwkv_ln_b_2, nsa_pe_k_2, nsa_pe_v_2, nsa_ck_w1_2, nsa_ck_w2_2, nsa_cv_w1_2, nsa_cv_w2_2,
    swa_sinks_2, w_br_a_2, w_br_b_2, w_br_c_2, w_out_2, peer_wq_2, peer_subkeys_2, peer_u_2,
    peer_v_2,
):
    x = first_block(
        x, c, ctx, c_ctx, ada_w, ada_b, ffn_pre_wi, ffn_pre_wo, ffn_post_wi, ffn_post_wo,
        a_w_qkv, a_w_o, a_q_gain, a_k_gain, a_lambda, a_subln_gain, b_w_qkv, b_w_o, b_q_gain,
        b_k_gain, b_sink,
    )
    return second_block(
        x, ln1_w_2, ln2_w_2, lnf_w_2, rel_bias_2, w_in_2, rwkv_mu_2, rwkv_w0_2, rwkv_w2_2,
        rwkv_a0_2, rwkv_a2_2, rwkv_g2_2, rwkv_k_k_2, rwkv_k_a_2, rwkv_r_k_2, rwkv_ln_w_2,
        rwkv_ln_b_2, nsa_pe_k_2, nsa_pe_v_2, nsa_ck_w1_2, nsa_ck_w2_2, nsa_cv_w1_2, nsa_cv_w2_2,
        swa_sinks_2, w_br_a_2, w_br_b_2, w_br_c_2, w_out_2, peer_wq_2, peer_subkeys_2, peer_u_2,
        peer_v_2,
    )


_drawn_inputs = setup_inputs


def setup_inputs(seed=0):
    import zlib

    import numpy as np

    out = dict(_drawn_inputs(seed))
    spreads = {}
    factors = {'b_q_gain': 6.371,
     'b_k_gain': 6.087,
     'b_sink': 8.0,
     'ln2_w_2': 3.203,
     'lnf_w_2': 2.844,
     'rwkv_k_k_2': 4.841,
     'rwkv_ln_w_2': 4.67,
     'rwkv_ln_b_2': 4.17,
     'nsa_pe_k_2': 7.796,
     'swa_sinks_2': 7.122}
    for name, (base, spread) in spreads.items():
        noise = np.random.default_rng([zlib.crc32(name.encode()), seed]).standard_normal(out[name].shape)
        drawn = base * np.exp(spread * noise) if base else spread * noise
        out[name] = __import__('jax').numpy.asarray(drawn.astype(out[name].dtype))
    for name, factor in factors.items():
        out[name] = (out[name] * factor).astype(out[name].dtype)
    return out
```

```python
import math
from contextlib import ExitStack

import numpy as np
import concourse.bass as bass
from concourse import mybir

P = 128
F32 = mybir.dt.float32
U32 = mybir.dt.uint32
I32 = mybir.dt.int32
ALU = mybir.AluOpType
ACT = mybir.ActivationFunctionType
AX = mybir.AxisListType.X

D = 1024
DC = D // P
LAT, CTX = 256, 256
TOK = LAT + CTX
FF = 2816
FC = FF // P
NMOD = 9
EPS = 1e-6
HD = 64
SCALE = HD ** -0.5
NEG = -1e30
A_HEADS = 8
LAM_INIT = 0.8 - 0.6 * math.exp(0.0)
B_HEADS, B_KV = 16, 4
B_WINDOW = 128
RW = 512
RC = RW // P
CH = 64
GN_EPS = 64e-5
DECAY = -math.exp(-0.5)
N_CMP, CMP_LEN, CMP_STRIDE = 15, 32, 16
PEER_H, PEER_K, NKEYS = 8, 16, 128
EXPERTS = NKEYS * NKEYS
SLOTS = PEER_H * PEER_K
QT = LAT // P
W_TILE = 16
W_SLOTS = 6

IN = dict(rw=0, nq=1792, nkc=2304, nvc=2432, nks=2560, nvs=2688, nkw=2816, nvw=2944, ngate=3072,
          sq=3096, sk=3608, sv=3736, gates=3864)


def weight_plan():
    plan = []

    def add(name, layer, row, col, width=1):
        if len(plan) % W_TILE + width > W_TILE:
            while len(plan) % W_TILE:
                plan.append(None)
        plan.append((name, layer, row, col, width))
        plan.extend(["+"] * (width - 1))

    def ffn(which, layer):
        for j in range(FC):
            for half in range(2):
                for k in range(DC):
                    add(f"ffn_{which}_wi", layer, k * P, half * FF + j * P)
        for m in range(DC):
            for f in range(FC):
                add(f"ffn_{which}_wo", layer, f * P, m * P)

    def square(name, layer, cols, rows=D):
        for c in cols:
            for k in range(rows // P):
                add(name, layer, k * P, c)

    def ada(layer):
        for c in range(0, NMOD * D, 4 * 512):
            for k in range(DC):
                for q in range(c, min(c + 4 * 512, NMOD * D), 512):
                    add("ada_w", layer, k * P, q, 4)

    ada(0)
    ffn("pre", 0)
    square("a_w_qkv", 0, range(0, 2 * D, P))
    for half in range(2):
        for k in range(DC):
            add("a_w_qkv", 0, k * P, 2 * D + half * 512, 4)
    square("a_w_o", 0, range(0, D, P))
    ffn("post", 0)
    ada(1)
    ffn("pre", 1)
    square("b_w_qkv", 0, range(0, D + 256, P))
    for k in range(DC):
        add("b_w_qkv", 0, k * P, D + 256, 2)
    square("b_w_o", 0, range(0, D, P))
    ffn("post", 1)
    for l in range(2):
        square("w_in", l, range(0, IN["nq"], P))
        add("rwkv_wa", l, 0, 0, 4)
        add("rwkv_g2", l, 0, 0, 4)
        square("w_in", l, [*range(IN["nq"], IN["nvs"], P), IN["nkw"]])
        for c, width in ((IN["nvs"], 1), (IN["nvw"], 2)):
            for k in range(DC):
                add("w_in", l, k * P, c, width)
        for name in ("nsa_ck", "nsa_cv"):
            for h in range(2):
                for k in range(16):
                    add(name + "_w1", l, k * P, h * P)
            for k in range(2):
                add(name + "_w2", l, k * P, 0)
        square("w_in", l, range(IN["sq"], IN["sv"], P))
        square("w_in", l, [IN["sv"]])
        for m in range(DC):
            for i, name in enumerate(("w_br_a", "w_br_b", "w_br_c")):
                square("w_in", l, [IN["gates"] + i * D + m * P])
                square(name, l, [m * P], RW)
        square("w_out", l, range(0, D, P))
        for i in range(2 * PEER_H):
            square("peer_wq", l, [i * P])
            add("peer_subkeys", l, 0, i * P)
    while len(plan) % W_TILE:
        plan.append(None)
    return plan


PLAN = weight_plan()
W_TILES = len(PLAN) // W_TILE


def columns(widths):
    at, out = 0, {}
    for name, w in widths:
        out[name] = (at, w)
        at += w
    return out, at


VEC_AT, N_VEC = columns([
    ("c", DC * 2), ("ada_b", 2 * NMOD * DC), ("a_q_gain", 1), ("a_k_gain", 1), ("a_subln", 1), ("b_q_gain", 1),
    ("b_k_gain", 1), ("ln1", 2 * DC), ("ln2", 2 * DC), ("lnf", DC), ("mu", 2 * 14), ("w0", 2 * RC), ("a0", 2 * RC),
    ("k_k", 2 * RC), ("k_a", 2 * RC), ("r_k", 2 * RC), ("ln_w", 2 * RC), ("ln_b", 2 * RC), ("pe_k", 2 * 16),
    ("pe_v", 2 * 16), ("b_sink", B_HEADS), ("swa_sink", 2 * 8), ("lambda", 4 * HD), ("rel", 16)])
LEVELS = 6
CONST_AT, N_CONST = columns([
    ("ident", P), ("ones", P), ("bones", P), ("rot", P), ("sel", 2 * P), ("cos", LAT), ("sin", LAT),
    ("level", LEVELS * P), ("before", P), ("upto", P), ("window", QT * TOK), ("cmp", QT * N_CMP),
    ("iota", PEER_K), ("carry", LAT), ("flip", P), ("eps", 1), ("gn_eps", 1)])
OH = 512
OH_AT, N_OH = columns([("nsa", OH), ("swa", OH)])


def t5_bucket(dist):
    n = np.maximum(dist, 0)
    nf = np.maximum(n, 16).astype(np.float32)
    large = 16 + (np.log(nf / 16) / math.log(128 / 16) * 16).astype(np.int32)
    return np.where(n < 16, n, np.minimum(large, 31))


def constants():
    c = np.zeros((P, N_CONST), np.float32)

    def put(name, a):
        at, w = CONST_AT[name]
        c[:, at:at + w] = np.asarray(a, np.float32).reshape(P, w)

    i, j = np.arange(P)[:, None], np.arange(P)[None, :]
    put("ident", i == j)
    put("ones", np.ones((P, P)))
    put("bones", i // HD == j // HD)
    rot = np.zeros((P, P))
    for m in range(P):
        if m % 32 < 16:
            rot[m + 16, m] = -1
        else:
            rot[m - 16, m] = 1
    put("rot", rot)
    put("sel", np.stack([(i == g * HD + j % HD) for g in range(2)], 1))
    inv = (10000.0 ** (-np.arange(16, dtype=np.float32) / 16)).astype(np.float32)
    t = np.arange(LAT)
    pos = np.stack([t // 64, t % 64]).astype(np.float32)
    d = np.arange(P) % HD
    ang = (pos[(d // 32)][:, :] * inv[d % 16][:, None]).astype(np.float32)
    put("cos", np.cos(ang))
    put("sin", np.sin(ang))
    put("level", np.stack([(i // (2 << k) == j // (2 << k)) & (i % (2 << k) < (1 << k)) & (j % (2 << k) >= (1 << k))
                           for k in range(LEVELS)], 1))
    put("before", (i // CH == j // CH) & (i < j))
    put("upto", (i // CH == j // CH) & (i <= j))
    w = np.zeros((P, QT, TOK))
    for q in range(QT):
        w[:, q, :LAT] = np.where(np.abs(np.arange(LAT)[None, :] - (q * P + i)) <= B_WINDOW, 0, NEG)
    put("window", w)
    end = np.arange(N_CMP) * CMP_STRIDE + CMP_LEN - 1
    put("cmp", np.stack([np.where(end[None, :] <= q * P + i, 0, NEG) for q in range(QT)], 1))
    put("iota", np.tile(np.arange(PEER_K), (P, 1)))
    put("carry", np.tile(np.arange(LAT) % CH != 0, (P, 1)))
    put("flip", i + j == P - 1)
    put("eps", np.full((P, 1), EPS))
    put("gn_eps", np.full((P, 1), GN_EPS))
    oh = np.zeros((33, 2, OH), np.float32)
    dist = 255 - np.arange(OH)
    for n, last in enumerate((256, 128)):
        oh[t5_bucket(dist), n, np.arange(OH)] = 1
        oh[32, n] = np.where((dist >= 0) & (dist < last), 0, NEG)
    return c, oh.reshape(33, N_OH)


ARENA = 26624


class Signal:

    def __init__(self, sem, unit=1):
        self.sem, self.unit, self.seen = sem, unit, {}

    def due(self, eng, n=1):
        self.seen[id(eng)] = self.seen.get(id(eng), 0) + n
        return self.unit * self.seen[id(eng)]


class Ring:

    def __init__(self, full, free, bufs):
        self.full, self.free, self.bufs = full, free, bufs
        self.claimed, self.taken = 0, 0

    def given_back(self, n=1):
        return max(self.claimed + n - len(self.bufs), 0)

    def filled(self, n=1):
        return self.taken + n

    def claim(self):
        self.claimed += 1
        return self.bufs[(self.claimed - 1) % len(self.bufs)]

    def take(self):
        self.taken += 1
        return self.bufs[(self.taken - 1) % len(self.bufs)]


def model_kernel(nc, wstream, vecs, consts, onehots, tokens, peer_u, peer_v, out, until=99):
    ctx = ExitStack()
    with ctx:
        def sem(name):
            return ctx.enter_context(nc.semaphore(name))

        def sb(name, shape, dt=F32):
            return ctx.enter_context(nc.sbuf_tensor(name, shape, dt))

        def signal(name, unit=1):
            return Signal(sem(name), unit)

        def ring(name, bufs):
            return Ring(sem(name + "_full"), sem(name + "_free"), bufs)

        xT = sb("xT", [P, DC, TOK])
        hT = sb("hT", [P, DC, TOK])
        wt = sb("wt", [P, W_SLOTS, W_TILE * P])
        cst = sb("cst", [P, N_CONST])
        vec = sb("vec", [P, N_VEC])
        mod = sb("mod", [P, 2, NMOD * DC, 2])
        silu_cc = sb("silu_cc", [P, DC, 2])
        rstd = sb("rstd", [P, TOK])
        small = sb("small", [P, 64])
        mini = sb("mini", [P, 784])
        arena = sb("arena", [P, ARENA])
        ps = ctx.enter_context(nc.psum_tensor("ps", [P, 8, 512], F32))

        def const(name, i=0, w=None):
            at, width = CONST_AT[name]
            w = w or width
            return cst[:, at + i * w:at + (i + 1) * w]

        def v(name, i=0, w=1):
            at = VEC_AT[name][0] + i
            return vec[:, at:at + w]

        ident, ones, bones = const("ident"), const("ones"), const("bones")
        eps = const("eps")

        class Carve:

            def __init__(self, at=0):
                self.at = at

            def __call__(self, *shape):
                n = int(np.prod(shape))
                a = arena[:, self.at:self.at + n]
                self.at += n
                assert self.at <= ARENA, self.at
                if len(shape) == 1:
                    return a
                names = "abcd"[:len(shape)]
                return a.rearrange(f"p ({' '.join(names)}) -> p {' '.join(names)}",
                                   **dict(zip(names[1:], shape[1:])))

        scratch = nc.dram_tensor("bias_by_distance", (16, OH), F32, kind="Internal").ap()

        loaded = signal("loaded", 16)
        w_full = [sem(f"w_full{i}") for i in range(W_SLOTS)]
        w_free = sem("w_free")
        phase_done = sem("phase_done")
        silu_done = signal("silu_done")
        sq_ready = signal("sq_ready")
        rstd_ready = signal("rstd_ready")
        xn_ready = signal("xn_ready")
        h_ready = signal("h_ready")
        hid_ready = signal("hid_ready")
        act_chain, dve_chain, pool_chain = sem("act_chain"), sem("dve_chain"), sem("pool_chain")
        D_ = ring("psd", [ps[:, i, :] for i in range(4)])
        A_ = ring("psa", [ps[:, 4 + i, :] for i in range(4)])

        phases = {}

        def end_phase(eng):
            n = phases[id(eng)] = phases.get(id(eng), 0) + 1
            eng.drain().then_inc(phase_done, 1)
            eng.wait_ge(phase_done, 4 * n)

        class Stepper:

            def __init__(self, eng, chain):
                self.eng, self.chain, self.n = eng, chain, 0

            def __call__(self, ins):
                self.n += 1
                ins.then_inc(self.chain, 1)
                self.eng.wait_ge(self.chain, self.n)

        class Weights:

            def __init__(self, pe):
                self.pe, self.at, self.owed = pe, 0, 0

            def next(self, *key, width=1):
                while PLAN[self.at] in (None, "+"):
                    self.at += 1
                assert PLAN[self.at] == (*key, width), (PLAN[self.at], key, width)
                tile, b = divmod(self.at, W_TILE)
                if tile != (self.at - 1) // W_TILE or self.at == 0 or self.tile != tile:
                    self.pe.wait_ge(w_full[tile % W_SLOTS], 16 * (tile // W_SLOTS + 1))
                    if tile:
                        self.owed += 1
                    self.tile = tile
                self.at += 1
                return wt[:, tile % W_SLOTS, b * P:(b + width) * P]

        def make_mm(pe, W):
            def mm(o, lhsT, rhs, start=True, stop=True, inc=None, **kw):
                ins = pe.matmul(o, lhsT, rhs, start=start, stop=stop, **kw)
                if inc is not None:
                    ins.then_inc(inc, 1)
                elif W.owed and not start:
                    ins.then_inc(w_free, 1)
                    W.owed -= 1
                return ins
            return mm

        def pe_project(pe, W, mm, name, l, cols, T, ring_of, src):
            for n, c in enumerate(cols):
                r = ring_of(n)
                pe.wait_ge(r.free, r.given_back())
                bank = r.claim()
                for k in range(DC):
                    mm(bank[:, 0:T], W.next(name, l, k * P, c), src[:, k, 0:T], k == 0, k == DC - 1,
                       r.full if k == DC - 1 else None)

        def pe_norm(pe, mm, T):
            pe.wait_ge(A_.free, A_.given_back())
            bank = A_.claim()
            for k in range(DC):
                pe.wait_ge(sq_ready.sem, sq_ready.due(pe))
                mm(bank[:, 0:T], ones, hT[:, k, 0:T], k == 0, k == DC - 1, A_.full if k == DC - 1 else None)

        def act_rsqrt(act, step, out_, in_, scale, bias):
            step(act.activation(out_, in_, ACT.Ln, bias=bias, scale=scale))
            step(act.activation(out_, out_, ACT.Exp, scale=-0.5))

        def act_norm(act, step, T, affine):
            for k in range(DC):
                act.activation(hT[:, k, 0:T], xT[:, k, 0:T], ACT.Square).then_inc(sq_ready.sem, 1)
            act.wait_ge(A_.full, A_.filled())
            bank = A_.take()
            act_rsqrt(act, step, rstd[:, 0:T], bank[:, 0:T], 1.0 / D, eps)
            act.sem_inc(A_.free, 1)
            act.sem_inc(rstd_ready.sem, 1)
            for k in range(DC):
                act.wait_ge(xn_ready.sem, xn_ready.due(act))
                affine(k)

        def dve_norm(dve, T):
            dve.wait_ge(rstd_ready.sem, rstd_ready.due(dve))
            for k in range(DC):
                dve.tensor_tensor(hT[:, k, 0:T], xT[:, k, 0:T], rstd[:, 0:T], ALU.mult).then_inc(xn_ready.sem, 1)

        def modulated(act, l, which, T):
            def affine(k):
                for r in range(T // LAT):
                    seg = hT[:, k, r * LAT:(r + 1) * LAT]
                    ins = act.activation(seg, seg, ACT.Identity, bias=mod[:, l, 3 * which * DC + k, r:r + 1],
                                         scale=mod[:, l, (3 * which + 1) * DC + k, r:r + 1])
                ins.then_inc(h_ready.sem, 1)
            return affine

        def dve_residual(dve, bank, m, l, which, T):
            for r in range(T // LAT):
                seg = xT[:, m, r * LAT:(r + 1) * LAT]
                ins = dve.scalar_tensor_tensor(out=seg, in0=bank[:, r * LAT:(r + 1) * LAT],
                                               scalar=mod[:, l, (3 * which + 2) * DC + m, r:r + 1], in1=seg,
                                               op0=ALU.mult, op1=ALU.add)
            ins.then_inc(D_.free, 1)

        arow = Carve()(NMOD * D)
        arow_ready = signal("arow_ready")

        def pe_ada(pe, W, mm, l):
            if l == 0:
                pe.wait_ge(silu_done.sem, silu_done.due(pe))
            for c in range(0, NMOD * D, 4 * 512):
                cols = range(c, min(c + 4 * 512, NMOD * D), 512)
                pe.wait_ge(D_.free, D_.given_back())
                bank = D_.claim()
                for k in range(DC):
                    for i, q in enumerate(cols):
                        last = k == DC - 1 and i == len(cols) - 1
                        mm(bank[32 * i:32 * i + 2, :], silu_cc[:, k, :], W.next("ada_w", l, k * P, q, width=4),
                           k == 0, k == DC - 1, D_.full if last else None)
            pe.wait_ge(arow_ready.sem, arow_ready.due(pe))
            pe.wait_ge(D_.free, D_.given_back())
            bank = D_.claim()
            for j in range(NMOD * DC):
                ins = pe.transpose(bank[:, 2 * j:2 * j + 2], arow[0:2, j * P:(j + 1) * P], ident[0:2, 0:2])
            ins.then_inc(D_.full, 1)

        def dve_ada(dve, step, l):
            for c in range(0, NMOD * D, 4 * 512):
                dve.wait_ge(D_.full, D_.filled())
                bank = D_.take()
                for i, q in enumerate(range(c, min(c + 4 * 512, NMOD * D), 512)):
                    step(dve.tensor_copy(arow[0:2, q:q + 512], bank[32 * i:32 * i + 2, :]))
                dve.sem_inc(D_.free, 1)
            dve.sem_inc(arow_ready.sem, 1)
            dve.wait_ge(D_.full, D_.filled())
            bank = D_.take()
            n = NMOD * DC
            bias = v("ada_b", l * n, n).unsqueeze(2).to_broadcast([P, n, 2])
            step(dve.tensor_tensor(mod[:, l], bank[:, 0:2 * n].rearrange("p (n c) -> p n c", c=2), bias, ALU.add))
            dve.sem_inc(D_.free, 1)
            for i in (1, 4, 7):
                a = mod[:, l, i * DC:(i + 1) * DC, :]
                step(dve.tensor_scalar(a, a, 1.0, None, ALU.add))
            for i in (2, 8):
                a = mod[:, l, i * DC:(i + 1) * DC, :]
                step(dve.tensor_scalar(a, a, 0.5, None, ALU.mult))

        F = Carve()
        hid = F(FC, TOK)
        silu_ring = ring("silu", [F(TOK) for _ in range(3)])

        def pe_ffn(pe, W, mm, which, l, T):
            pe_norm(pe, mm, T)
            pe.wait_ge(h_ready.sem, h_ready.due(pe, DC))
            for j in range(FC):
                for half, r in ((0, A_), (1, D_)):
                    pe.wait_ge(r.free, r.given_back())
                    bank = r.claim()
                    for k in range(DC):
                        mm(bank[:, 0:T], W.next(f"ffn_{which}_wi", l, k * P, half * FF + j * P), hT[:, k, 0:T],
                           k == 0, k == DC - 1, r.full if k == DC - 1 else None)
            for m in range(DC):
                pe.wait_ge(D_.free, D_.given_back())
                bank = D_.claim()
                for f in range(FC):
                    if m == 0:
                        pe.wait_ge(hid_ready.sem, hid_ready.due(pe))
                    mm(bank[:, 0:T], W.next(f"ffn_{which}_wo", l, f * P, m * P), hid[:, f, 0:T], f == 0, f == FC - 1,
                       D_.full if f == FC - 1 else None)

        def act_ffn(act, step, l, sub, T):
            act_norm(act, step, T, modulated(act, l, sub, T))
            for j in range(FC):
                act.wait_ge(A_.full, A_.filled())
                bank = A_.take()
                act.wait_ge(silu_ring.free, silu_ring.given_back())
                s = silu_ring.claim()
                step(act.activation(s[:, 0:T], bank[:, 0:T], ACT.Silu))
                act.sem_inc(A_.free, 1)
                act.sem_inc(silu_ring.full, 1)

        def dve_ffn(dve, step, l, sub, T):
            dve_norm(dve, T)
            for j in range(FC):
                dve.wait_ge(silu_ring.full, silu_ring.filled())
                s = silu_ring.take()
                dve.wait_ge(D_.full, D_.filled())
                bank = D_.take()
                step(dve.tensor_tensor(hid[:, j, 0:T], s[:, 0:T], bank[:, 0:T], ALU.mult))
                dve.sem_inc(silu_ring.free, 1)
                dve.sem_inc(D_.free, 1)
                dve.sem_inc(hid_ready.sem, 1)
            for m in range(DC):
                dve.wait_ge(D_.full, D_.filled())
                dve_residual(dve, D_.take(), m, l, sub, T)

        M = Carve()
        qT, kT = M(8, TOK), M(8, TOK)
        vA = M(4, D)
        oT = M(8, TOK)
        S = Carve(M.at)
        raw_ring = ring("raw", [S(TOK) for _ in range(2)])
        sqh_ring = ring("sqh", [S(TOK) for _ in range(2)])
        rs_ring = ring("rs", [S(TOK) for _ in range(2)])
        qn_ring = ring("qn", [S(LAT) for _ in range(2)])
        tmp_a, tmp_b = S(TOK), S(TOK)
        assert S.at <= ARENA

        def pe_heads(pe, W, mm, name, cols):
            n = len(cols)
            for i in range(n + 2):
                if i < n:
                    pe_project(pe, W, mm, name, 0, [cols[i]], TOK, lambda _: A_, hT)
                if 1 <= i <= n:
                    pe.wait_ge(sqh_ring.full, sqh_ring.filled())
                    sq = sqh_ring.take()
                    pe.wait_ge(A_.free, A_.given_back())
                    mm(A_.claim(), bones, sq).then_inc(A_.full, 1)
                if i >= 2:
                    pe.wait_ge(qn_ring.full, qn_ring.filled())
                    qn = qn_ring.take()
                    pe.wait_ge(D_.free, D_.given_back())
                    mm(D_.claim()[:, 0:LAT], const("rot"), qn).then_inc(D_.full, 1)

        def act_heads(act, step, n):
            for i in range(n + 1):
                if i < n:
                    act.wait_ge(A_.full, A_.filled())
                    bank = A_.take()
                    act.wait_ge(raw_ring.free, raw_ring.given_back())
                    act.wait_ge(sqh_ring.free, sqh_ring.given_back())
                    raw, sq = raw_ring.claim(), sqh_ring.claim()
                    act.activation(raw, bank, ACT.Copy).then_inc(raw_ring.full, 1)
                    step(act.activation(sq, bank, ACT.Square))
                    act.sem_inc(sqh_ring.full, 1)
                    act.sem_inc(A_.free, 1)
                if i >= 1:
                    act.wait_ge(A_.full, A_.filled())
                    bank = A_.take()
                    act.wait_ge(rs_ring.free, rs_ring.given_back())
                    r = rs_ring.claim()
                    act_rsqrt(act, step, r, bank, 1.0 / HD, eps)
                    act.sem_inc(sqh_ring.free, 1)
                    act.sem_inc(A_.free, 1)
                    act.sem_inc(rs_ring.full, 1)

        def dve_heads(dve, step, outs, gains):
            n = len(outs)
            for i in range(n + 1):
                if i < n:
                    dve.wait_ge(raw_ring.full, raw_ring.filled())
                    dve.wait_ge(rs_ring.full, rs_ring.filled())
                    dve.wait_ge(qn_ring.free, qn_ring.given_back())
                    raw, r, qn = raw_ring.take(), rs_ring.take(), qn_ring.claim()
                    step(dve.scalar_tensor_tensor(out=outs[i][:, LAT:TOK], in0=raw[:, LAT:TOK], scalar=gains[i],
                                                  in1=r[:, LAT:TOK], op0=ALU.mult, op1=ALU.mult))
                    step(dve.scalar_tensor_tensor(out=qn, in0=raw[:, 0:LAT], scalar=gains[i],
                                                  in1=r[:, 0:LAT], op0=ALU.mult, op1=ALU.mult))
                    dve.sem_inc(raw_ring.free, 1)
                    dve.sem_inc(rs_ring.free, 1)
                    step(dve.tensor_tensor(outs[i][:, 0:LAT], qn, const("cos"), ALU.mult))
                    dve.sem_inc(qn_ring.full, 1)
                if i >= 1:
                    dve.wait_ge(D_.full, D_.filled())
                    bank = D_.take()
                    o = outs[i - 1][:, 0:LAT]
                    step(dve.tensor_tensor(tmp_a[:, 0:LAT], bank[:, 0:LAT], const("sin"), ALU.mult))
                    dve.sem_inc(qn_ring.free, 1)
                    dve.sem_inc(D_.free, 1)
                    step(dve.tensor_tensor(o, o, tmp_a[:, 0:LAT], ALU.add))

        def pe_a_qkv(pe, W, mm):
            pe_norm(pe, mm, TOK)
            pe.wait_ge(h_ready.sem, h_ready.due(pe, DC))
            pe_heads(pe, W, mm, "a_w_qkv", range(0, 2 * D, P))
            for half in range(2):
                pe.wait_ge(D_.free, D_.given_back(4))
                banks = [D_.claim() for _ in range(4)]
                for k in range(DC):
                    w = W.next("a_w_qkv", 0, k * P, 2 * D + half * 512, width=4)
                    for t in range(4):
                        mm(banks[t], hT[:, k, t * P:(t + 1) * P], w, k == 0, k == DC - 1,
                           D_.full if k == DC - 1 else None)

        def act_a_qkv(act, step):
            act_norm(act, step, TOK, modulated(act, 0, 1, TOK))
            act_heads(act, step, 16)

        def dve_a_qkv(dve, step):
            dve_norm(dve, TOK)
            dve_heads(dve, step, [qT[:, i] for i in range(8)] + [kT[:, i] for i in range(8)],
                      [v("a_q_gain")] * 8 + [v("a_k_gain")] * 8)
            for half in range(2):
                for t in range(4):
                    dve.wait_ge(D_.full, D_.filled())
                    bank = D_.take()
                    dve.tensor_copy(vA[:, t, half * 512:(half + 1) * 512], bank).then_inc(D_.free, 1)
            prod = tmp_b[:, 0:2 * HD]
            lam4 = v("lambda", 0, 4 * HD).rearrange("p (a b d) -> p a b d", a=2, b=2)
            step(dve.tensor_tensor(prod.rearrange("p (a d) -> p a d", a=2), lam4[:, :, 0, :], lam4[:, :, 1, :], ALU.mult))
            step(dve.tensor_reduce(small[:, 2:4], prod.rearrange("p (a d) -> p a d", a=2), AX, ALU.add))
            dve.sem_inc(lam_sum.sem, 1)
            dve.wait_ge(lam_exp.sem, lam_exp.due(dve))
            step(dve.tensor_scalar(small[:, 0:1], small[:, 5:6], small[:, 4:5], -LAM_INIT, ALU.subtract, ALU.add))

        lam_sum, lam_exp = signal("lam_sum"), signal("lam_exp")

        def act_lambda(act, step):
            act.wait_ge(lam_sum.sem, lam_sum.due(act))
            step(act.activation(small[:, 4:6], small[:, 2:4], ACT.Exp))
            act.sem_inc(lam_exp.sem, 1)

        A_UNITS = [(h, q) for h in range(A_HEADS) for q in range(4)]
        U = Carve(M.at)
        p_bufs = [U(2, TOK) for _ in range(2)]
        a_ring = ring("aprob", [U(TOK) for _ in range(2)])
        t_ring = ring("at", [U(4, P) for _ in range(2)])
        nmax = U(8, 2)
        rsum = U(8, 2)
        assert U.at <= ARENA
        s_pair = ring("spair", [ps[:, 0:2], ps[:, 2:4]])
        p_ring = ring("prob", p_bufs)
        nm_ready = signal("nm_ready")
        ot_ring = ring("ot", [ps[:, 6], ps[:, 7]])
        tpr = ring("tpr", [ps[:, 4], ps[:, 5]])

        def keys_of(q):
            return (0, TOK) if q < QT else (LAT, TOK)

        def pe_a_attend(pe, W, mm):
            n = len(A_UNITS)
            for i in range(n + 3):
                if i < n:
                    h, q = A_UNITS[i]
                    k0, k1 = keys_of(q)
                    pe.wait_ge(s_pair.free, s_pair.given_back())
                    s = s_pair.claim()
                    for c in range(2):
                        r = slice(c * HD, (c + 1) * HD)
                        mm(s[:, c, 0:k1 - k0], qT[r, h, q * P:(q + 1) * P], kT[r, h, k0:k1],
                           inc=s_pair.full if c else None)
                if 2 <= i < n + 2:
                    h, q = A_UNITS[i - 2]
                    k0, k1 = keys_of(q)
                    pe.wait_ge(a_ring.full, a_ring.filled())
                    pe.wait_ge(tpr.free, tpr.given_back())
                    a, t = a_ring.take(), tpr.claim()
                    for j in range((k1 - k0) // P):
                        ins = pe.transpose(t[:, j * P:(j + 1) * P], a[:, j * P:(j + 1) * P], ident)
                    ins.then_inc(tpr.full, 1)
                if i >= 3:
                    h, q = A_UNITS[i - 3]
                    k0, k1 = keys_of(q)
                    pe.wait_ge(t_ring.full, t_ring.filled())
                    pe.wait_ge(ot_ring.free, ot_ring.given_back())
                    t, o = t_ring.take(), ot_ring.claim()
                    nk = (k1 - k0) // P
                    for j in range(nk):
                        mm(o[:, 0:P], vA[:, k0 // P + j, h * P:(h + 1) * P], t[:, j, :], j == 0, j == nk - 1,
                           ot_ring.full if j == nk - 1 else None)

        def act_a_attend(act, step):
            n = len(A_UNITS)
            for i in range(n + 2):
                if i < n:
                    h, q = A_UNITS[i]
                    k0, k1 = keys_of(q)
                    w = k1 - k0
                    act.wait_ge(nm_ready.sem, nm_ready.due(act))
                    act.wait_ge(p_ring.free, p_ring.given_back())
                    p = p_ring.claim()
                    s = s_pair.bufs[i % 2]
                    for c in range(2):
                        step(act.activation(p[:, c, 0:w], s[:, c, 0:w], ACT.Exp, bias=nmax[:, i % 8, c:c + 1],
                                            scale=SCALE, accum_out=rsum[:, i % 8, c:c + 1]))
                    act.sem_inc(s_pair.free, 1)
                    act.sem_inc(p_ring.full, 1)
                if i >= 2:
                    h, q = A_UNITS[i - 2]
                    k0, k1 = keys_of(q)
                    w = k1 - k0
                    act.wait_ge(tpr.full, tpr.filled())
                    act.wait_ge(t_ring.free, t_ring.given_back())
                    tp, t = tpr.take(), t_ring.claim()
                    act.sem_inc(a_ring.free, 1)
                    step(act.activation(t[:, 0:w // P, :], tp[:, 0:w].rearrange("p (a b) -> p a b", b=P), ACT.Copy))
                    act.sem_inc(tpr.free, 1)
                    act.sem_inc(t_ring.full, 1)

        def dve_a_attend(dve, step):
            n = len(A_UNITS)
            for i in range(n + 4):
                if i < n:
                    h, q = A_UNITS[i]
                    k0, k1 = keys_of(q)
                    dve.wait_ge(s_pair.full, s_pair.filled())
                    s = s_pair.take()
                    step(dve.tensor_reduce(nmax[:, i % 8, :], s[:, :, 0:k1 - k0], AX, ALU.max))
                    step(dve.tensor_scalar(nmax[:, i % 8, :], nmax[:, i % 8, :], -SCALE, None, ALU.mult))
                    dve.sem_inc(nm_ready.sem, 1)
                if 1 <= i < n + 1:
                    j = i - 1
                    h, q = A_UNITS[j]
                    k0, k1 = keys_of(q)
                    w = k1 - k0
                    dve.wait_ge(p_ring.full, p_ring.filled())
                    p = p_ring.take()
                    dve.wait_ge(a_ring.free, a_ring.given_back())
                    a = a_ring.claim()
                    rs = rsum[:, j % 8, :]
                    step(dve.reciprocal(rs, rs))
                    step(dve.tensor_scalar(p[:, 1, 0:w], p[:, 1, 0:w], rs[:, 1:2], small[:, 0:1], ALU.mult, ALU.mult))
                    step(dve.scalar_tensor_tensor(out=a[:, 0:w], in0=p[:, 0, 0:w], scalar=rs[:, 0:1], in1=p[:, 1, 0:w],
                                                  op0=ALU.mult, op1=ALU.add))
                    dve.sem_inc(p_ring.free, 1)
                    dve.sem_inc(a_ring.full, 1)
                if i >= 4:
                    h, q = A_UNITS[i - 4]
                    dve.wait_ge(ot_ring.full, ot_ring.filled())
                    o = ot_ring.take()
                    step(dve.tensor_copy(oT[:, h, q * P:(q + 1) * P], o[:, 0:P]))
                    dve.sem_inc(ot_ring.free, 1)
                    dve.sem_inc(t_ring.free, 1)

        def pe_a_out(pe, W, mm):
            for h in range(A_HEADS):
                pe.wait_ge(A_.free, A_.given_back())
                pe.wait_ge(sqh_ring.full, sqh_ring.filled())
                mm(A_.claim(), ones, sqh_ring.take()).then_inc(A_.full, 1)
            pe.wait_ge(h_ready.sem, h_ready.due(pe, A_HEADS))
            pe_project(pe, W, mm, "a_w_o", 0, range(0, D, P), TOK, lambda _: D_, oT)

        def act_a_out(act, step):
            for h in range(A_HEADS + 1):
                if h < A_HEADS:
                    act.wait_ge(sqh_ring.free, sqh_ring.given_back())
                    sq = sqh_ring.claim()
                    step(act.activation(sq, oT[:, h, :], ACT.Square))
                    act.sem_inc(sqh_ring.full, 1)
                if h >= 1:
                    act.wait_ge(A_.full, A_.filled())
                    act.wait_ge(rs_ring.free, rs_ring.given_back())
                    bank, r = A_.take(), rs_ring.claim()
                    act_rsqrt(act, step, r, bank, 1.0 / P, eps)
                    act.sem_inc(sqh_ring.free, 1)
                    act.sem_inc(A_.free, 1)
                    act.sem_inc(rs_ring.full, 1)

        def dve_a_out(dve, step):
            step(dve.tensor_scalar(small[:, 1:2], v("a_subln"), 1.0 - LAM_INIT, None, ALU.mult))
            for h in range(A_HEADS):
                dve.wait_ge(rs_ring.full, rs_ring.filled())
                r = rs_ring.take()
                step(dve.scalar_tensor_tensor(out=oT[:, h, :], in0=oT[:, h, :], scalar=small[:, 1:2], in1=r,
                                              op0=ALU.mult, op1=ALU.mult))
                dve.sem_inc(rs_ring.free, 1)
                dve.sem_inc(h_ready.sem, 1)
            for m in range(DC):
                dve.wait_ge(D_.full, D_.filled())
                dve_residual(dve, D_.take(), m, 0, 1, TOK)

        MB = Carve()
        qB = MB(8, TOK)
        kB = MB(2, TOK)
        kD = MB(B_KV, TOK)
        vB = MB(4, 256)
        oB = MB(8, LAT)
        N = Carve(MB.at)
        sm_ring_b = ring("sm", [N(TOK) for _ in range(2)])
        pb_ring = ring("pb", [N(TOK) for _ in range(2)])
        sinkv = N(8, 4)
        B_UNITS = [(h, q) for h in range(B_HEADS) for q in range(QT)]

        def pe_b_qkv(pe, W, mm):
            pe_norm(pe, mm, TOK)
            pe.wait_ge(h_ready.sem, h_ready.due(pe, DC))
            pe_heads(pe, W, mm, "b_w_qkv", range(0, D + 256, P))
            pe.wait_ge(D_.free, D_.given_back(4))
            banks = [D_.claim() for _ in range(4)]
            for k in range(DC):
                w = W.next("b_w_qkv", 0, k * P, D + 256, width=2)
                for t in range(4):
                    mm(banks[t][:, 0:256], hT[:, k, t * P:(t + 1) * P], w, k == 0, k == DC - 1,
                       D_.full if k == DC - 1 else None)
            pe.wait_ge(kb_ready.sem, kb_ready.due(pe))
            for g in range(B_KV):
                pe.wait_ge(D_.free, D_.given_back())
                mm(D_.claim(), const("sel", g % 2, P), kB[:, g // 2, :]).then_inc(D_.full, 1)

        kb_ready = signal("kb_ready")

        def dve_b_qkv(dve, step):
            dve_norm(dve, TOK)
            dve_heads(dve, step, [qB[:, i] for i in range(8)] + [kB[:, i] for i in range(2)],
                      [v("b_q_gain")] * 8 + [v("b_k_gain")] * 2)
            dve.sem_inc(kb_ready.sem, 1)
            for t in range(4):
                dve.wait_ge(D_.full, D_.filled())
                bank = D_.take()
                dve.tensor_copy(vB[:, t, :], bank[:, 0:256]).then_inc(D_.free, 1)
            for g in range(B_KV):
                dve.wait_ge(D_.full, D_.filled())
                bank = D_.take()
                dve.tensor_copy(kD[:, g, :], bank).then_inc(D_.free, 1)

        def act_b_qkv(act, step):
            act_norm(act, step, TOK, modulated(act, 1, 1, TOK))
            act_heads(act, step, 10)

        def pe_b_attend(pe, W, mm):
            n = len(B_UNITS)
            for i in range(n + 3):
                if i < n:
                    h, q = B_UNITS[i]
                    r = slice((h % 2) * HD, (h % 2 + 1) * HD)
                    pe.wait_ge(D_.free, D_.given_back())
                    mm(D_.claim(), qB[r, h // 2, q * P:(q + 1) * P], kD[r, h // 4, :]).then_inc(D_.full, 1)
                if 2 <= i < n + 2:
                    pe.wait_ge(a_ring.full, a_ring.filled())
                    pe.wait_ge(tpr.free, tpr.given_back())
                    a, t = a_ring.take(), tpr.claim()
                    for j in range(4):
                        ins = pe.transpose(t[:, j * P:(j + 1) * P], a[:, j * P:(j + 1) * P], ident)
                    ins.then_inc(tpr.full, 1)
                if i >= 3:
                    h, q = B_UNITS[i - 3]
                    g = h // 4
                    r = slice((h % 2) * HD, (h % 2 + 1) * HD)
                    pe.wait_ge(t_ring.full, t_ring.filled())
                    pe.wait_ge(ot_ring.free, ot_ring.given_back())
                    t, o = t_ring.take(), ot_ring.claim()
                    for j in range(4):
                        mm(o[r, 0:P], vB[:, j, g * HD:(g + 1) * HD], t[:, j, :], j == 0, j == 3,
                           ot_ring.full if j == 3 else None)

        def act_b_attend(act, step):
            n = len(B_UNITS)
            for i in range(n + 2):
                if i < n:
                    h, q = B_UNITS[i]
                    act.wait_ge(sm_ring_b.full, sm_ring_b.filled())
                    act.wait_ge(pb_ring.free, pb_ring.given_back())
                    s, p = sm_ring_b.take(), pb_ring.claim()
                    sv = sinkv[:, i % 8, :]
                    step(act.activation(p, s, ACT.Exp, bias=sv[:, 0:1], accum_out=sv[:, 1:2]))
                    act.sem_inc(sm_ring_b.free, 1)
                    step(act.activation(sv[:, 2:3], v("b_sink", h), ACT.Exp, bias=sv[:, 0:1]))
                    act.sem_inc(pb_ring.full, 1)
                if i >= 2:
                    act.wait_ge(tpr.full, tpr.filled())
                    act.wait_ge(t_ring.free, t_ring.given_back())
                    tp, t = tpr.take(), t_ring.claim()
                    act.sem_inc(a_ring.free, 1)
                    step(act.activation(t, tp.rearrange("p (a b) -> p a b", b=P), ACT.Copy))
                    act.sem_inc(tpr.free, 1)
                    act.sem_inc(t_ring.full, 1)

        def dve_b_attend(dve, step):
            n = len(B_UNITS)
            for i in range(n + 4):
                if i < n:
                    h, q = B_UNITS[i]
                    dve.wait_ge(D_.full, D_.filled())
                    dve.wait_ge(sm_ring_b.free, sm_ring_b.given_back())
                    bank, s = D_.take(), sm_ring_b.claim()
                    sv = sinkv[:, i % 8, :]
                    step(dve.scalar_tensor_tensor(out=s, in0=bank, scalar=SCALE, in1=const("window", q, TOK),
                                                  op0=ALU.mult, op1=ALU.add))
                    dve.sem_inc(D_.free, 1)
                    step(dve.tensor_reduce(sv[:, 0:1], s, AX, ALU.max))
                    step(dve.tensor_scalar(sv[:, 0:1], sv[:, 0:1], v("b_sink", h), -1.0, ALU.max, ALU.mult))
                    dve.sem_inc(sm_ring_b.full, 1)
                if 1 <= i < n + 1:
                    dve.wait_ge(pb_ring.full, pb_ring.filled())
                    dve.wait_ge(a_ring.free, a_ring.given_back())
                    p, a = pb_ring.take(), a_ring.claim()
                    sv = sinkv[:, (i - 1) % 8, :]
                    step(dve.tensor_tensor(sv[:, 3:4], sv[:, 1:2], sv[:, 2:3], ALU.add))
                    step(dve.reciprocal(sv[:, 3:4], sv[:, 3:4]))
                    step(dve.tensor_scalar(a, p, sv[:, 3:4], None, ALU.mult))
                    dve.sem_inc(pb_ring.free, 1)
                    dve.sem_inc(a_ring.full, 1)
                if i >= 4:
                    h, q = B_UNITS[i - 4]
                    r = slice((h % 2) * HD, (h % 2 + 1) * HD)
                    dve.wait_ge(ot_ring.full, ot_ring.filled())
                    o = ot_ring.take()
                    step(dve.tensor_copy(oB[r, h // 2, q * P:(q + 1) * P], o[r, 0:P]))
                    dve.sem_inc(ot_ring.free, 1)
                    dve.sem_inc(t_ring.free, 1)
            dve.sem_inc(h_ready.sem, 1)

        biasT = Carve()(16, 3 * P)
        B0 = 16 * 3 * P
        xU, hU = xT[:, :, LAT:TOK], hT[:, :, LAT:TOK]
        oa, ob, oc = xU[:, 0:4], xU[:, 4:8], hU[:, 0:4]

        X_ = Carve(B0)
        oh_sb = X_(N_OH)
        f_sb = X_(2 * OH)
        toep = X_(16, 3 * P)
        oh_loaded, f_ready, f_stored, toep_loaded = (signal(n, u) for n, u in (
            ("oh_loaded", 16), ("f_ready", 1), ("f_stored", 16), ("toep_loaded", 16)))

        def pe_bias(pe, W, mm):
            pe.wait_ge(oh_loaded.sem, oh_loaded.due(pe))
            for i in range(2):
                pe.wait_ge(D_.free, D_.given_back())
                mm(D_.claim()[0:8, 0:OH], v("rel", i * 8, 8)[0:33, :], oh_sb[0:33, i * OH:(i + 1) * OH]).then_inc(D_.full, 1)
            pe.wait_ge(toep_loaded.sem, toep_loaded.due(pe))
            for h in range(16):
                pe.wait_ge(D_.free, D_.given_back())
                mm(D_.claim()[:, 0:3 * P], const("flip"), toep[:, h, :]).then_inc(D_.full, 1)

        def dve_bias(dve, step):
            for i in range(2):
                dve.wait_ge(D_.full, D_.filled())
                bank = D_.take()
                step(dve.tensor_copy(f_sb[0:8, i * OH:(i + 1) * OH], bank[0:8, 0:OH]))
                dve.sem_inc(D_.free, 1)
            dve.sem_inc(f_ready.sem, 1)
            for h in range(16):
                dve.wait_ge(D_.full, D_.filled())
                bank = D_.take()
                step(dve.tensor_copy(biasT[:, h, :], bank[:, 0:3 * P]))
                dve.sem_inc(D_.free, 1)

        def dma_bias(act):
            act.dma_start(oh_sb[0:33, :], onehots).then_inc(oh_loaded.sem, 16)
            act.wait_ge(f_ready.sem, f_ready.due(act))
            act.dma_start(scratch.rearrange("(i h) x -> h i x", i=2),
                         f_sb[0:8, :].rearrange("p (i x) -> p i x", i=2)).then_inc(f_stored.sem, 16)
            act.wait_ge(f_stored.sem, f_stored.due(act))
            shifted = bass.AP(scratch.tensor, 0, [[1, P], [OH, 16], [1, 3 * P]])
            act.dma_start(toep, shifted).then_inc(toep_loaded.sem, 16)

        def gained(act, name, l):
            def affine(k):
                act.activation(hT[:, k, 0:LAT], hT[:, k, 0:LAT], ACT.Copy,
                               scale=v(name, l * DC + k)).then_inc(h_ready.sem, 1)
            return affine

        def copy_out(dve, dst, w):
            dve.wait_ge(D_.full, D_.filled())
            bank = D_.take()
            dve.tensor_copy(dst, bank[:, 0:w]).then_inc(D_.free, 1)

        def slot(n, k=1):
            return arena[:, B0 + n * 1024:B0 + (n + k) * 1024]

        def fm(n):
            return slot(n).rearrange("p (m t) -> p m t", t=LAT)

        zraw = arena[:, B0:B0 + 14 * (LAT + 1)].rearrange("p (m t) -> p m t", t=LAT + 1)
        zs = arena[:, B0 + 4096:B0 + 4096 + 14 * LAT].rearrange("p (m t) -> p m t", t=LAT)
        zr, zk, zv = zs[:, 0:4], zs[:, 4:8], zs[:, 8:12]
        ld, lcum, pcum, pinv = fm(0), fm(1), fm(2), fm(3)
        pprev, iclr, gate, kk, bonus, sqk, kmod = fm(8), fm(9), fm(10), fm(11), fm(12), fm(13), fm(14)
        rt, kt, at_, bt = pcum, pinv, pprev, iclr
        vtok, atok, btok, ktok = (slot(n).rearrange("p (t f) -> p t f", t=2) for n in (15, 11, 0, 1))
        utok = slot(7).rearrange("p (t f) -> p t f", t=2)
        xat = slot(4).rearrange("p (m t f) -> p m t f", m=4, t=2)
        lrb, lrk = (slot(n, 2).rearrange("p (t h f) -> p t h f", t=2, h=8) for n in (5, 13))
        B4 = [slot(16 + n // 2)[:, (n % 2) * 512:(n % 2 + 1) * 512].rearrange("p (a b) -> p a b", b=P)
              for n in range(8)]
        B4 += [u[:, 4:8, i * P:(i + 1) * P] for u in (xU, hU) for i in range(2)]
        LT, LAK, X, XT, LTL, Y = (B4[2 * i:2 * i + 2] for i in range(6))
        W1 = [a[:, :, 0:HD] for a in LTL]
        state = [mini[:, c * 256:(c + 1) * 256].rearrange("p (m i) -> p m i", i=HD) for c in range(3)]
        p_end = mini[:, 768:784].rearrange("p (m c) -> p m c", c=4)
        y_ = at_
        mix_ready = signal("mix_ready")
        act_ready = signal("act_ready")
        to_act = signal("to_act")
        to_dve = signal("to_dve")

        def by_group(tok, t):
            return tok[:, t].rearrange("p (u g f) -> p u g f", g=2, f=HD)

        def pe_rwkv_in(pe, W, mm, l):
            pe_norm(pe, mm, LAT)
            pe.wait_ge(h_ready.sem, h_ready.due(pe, DC))
            pe_project(pe, W, mm, "w_in", l, range(0, IN["nq"], P), LAT, lambda _: D_, hT)
            pe.wait_ge(act_ready.sem, act_ready.due(pe))
            w = W.next("rwkv_wa", l, 0, 0, width=4)
            for m in range(RC):
                pe.wait_ge(A_.free, A_.given_back())
                mm(A_.claim()[:, 0:LAT], w[0:64, m * P:(m + 1) * P], zs[0:64, 12, :]).then_inc(A_.full, 1)
            for m in range(RC):
                pe.wait_ge(A_.free, A_.given_back())
                mm(A_.claim()[:, 0:LAT], w[64:128, m * P:(m + 1) * P], zs[64:128, 12, :]).then_inc(A_.full, 1)
            w = W.next("rwkv_g2", l, 0, 0, width=4)
            for m in range(RC):
                pe.wait_ge(A_.free, A_.given_back())
                mm(A_.claim()[:, 0:LAT], w[:, m * P:(m + 1) * P], zs[:, 13, :]).then_inc(A_.full, 1)
            pe.wait_ge(mix_ready.sem, mix_ready.due(pe))
            for m in range(RC):
                pe.wait_ge(A_.free, A_.given_back())
                mm(A_.claim()[:, 0:LAT], bones, sqk[:, m]).then_inc(A_.full, 1)
            pe.wait_ge(mix_ready.sem, mix_ready.due(pe))
            for m in range(RC):
                pe.wait_ge(D_.free, D_.given_back())
                mm(D_.claim()[:, 0:LAT], bones, sqk[:, m]).then_inc(D_.full, 1)

        def act_rwkv_in(act, step, l):
            act_norm(act, step, LAT, gained(act, "ln1", l))
            act.wait_ge(to_act.sem, to_act.due(act))
            step(act.activation(zs[0:64, 12, :], zs[0:64, 12, :], ACT.Tanh))
            step(act.activation(zs[:, 13, :], zs[:, 13, :], ACT.Sigmoid))
            act.sem_inc(act_ready.sem, 1)
            for m in range(RC):
                act.wait_ge(A_.full, A_.filled())
                bank = A_.take()
                act.activation(ld[:, m], bank[:, 0:LAT], ACT.Sigmoid, bias=v("w0", l * RC + m)).then_inc(A_.free, 1)
            for m in range(RC):
                act.wait_ge(A_.full, A_.filled())
                bank = A_.take()
                act.activation(iclr[:, m], bank[:, 0:LAT], ACT.Sigmoid, bias=v("a0", l * RC + m)).then_inc(A_.free, 1)
            for m in range(RC):
                act.wait_ge(A_.full, A_.filled())
                bank = A_.take()
                act.activation(gate[:, m], bank[:, 0:LAT], ACT.Copy).then_inc(A_.free, 1)
            act.drain().then_inc(to_dve.sem, 1)
            act.wait_ge(to_act.sem, to_act.due(act))
            act.activation(pprev, pprev, ACT.Exp)
            act.activation(pcum, lcum, ACT.Exp)
            step(act.activation(pinv, lcum, ACT.Exp, scale=-1.0))
            act.sem_inc(to_dve.sem, 1)
            for m in range(RC):
                act.wait_ge(A_.full, A_.filled())
                bank = A_.take()
                step(act.activation(lcum[:, m], bank[:, 0:LAT], ACT.Copy))
                act.sem_inc(A_.free, 1)
            act.sem_inc(to_dve.sem, 1)
            act.wait_ge(to_act.sem, to_act.due(act))
            act_rsqrt(act, step, lcum, lcum, 1.0, 0.0)
            act.sem_inc(to_dve.sem, 1)

        def dve_rwkv_in(dve, step, l):
            dve_norm(dve, LAT)
            step(dve.memset(zraw[:, :, 0:1], 0.0))
            for n in [*range(14)]:
                dve.wait_ge(D_.full, D_.filled())
                bank = D_.take()
                step(dve.tensor_copy(zraw[:, n, 1:], bank[:, 0:LAT]))
                dve.sem_inc(D_.free, 1)
                z = zs[:, n, :]
                step(dve.tensor_tensor(z, zraw[:, n, 0:LAT], zraw[:, n, 1:], ALU.subtract))
                step(dve.scalar_tensor_tensor(out=z, in0=z, scalar=v("mu", l * 14 + n), in1=zraw[:, n, 1:],
                                              op0=ALU.mult, op1=ALU.add))
            dve.sem_inc(to_act.sem, 1)
            for m in range(RC):
                step(dve.tensor_scalar(kk[:, m], zk[:, m], v("k_k", l * RC + m), None, ALU.mult))
            step(dve.tensor_tensor(sqk, kk, kk, ALU.mult))
            dve.sem_inc(mix_ready.sem, 1)
            dve.wait_ge(to_dve.sem, to_dve.due(dve))
            step(dve.tensor_scalar(ld, ld, DECAY, None, ALU.mult))
            for m in range(RC):
                step(dve.tensor_tensor_scan(lcum[:, m], const("carry"), ld[:, m], 0.0, ALU.mult, ALU.add))
            step(dve.tensor_tensor(pprev, lcum, ld, ALU.subtract))
            dve.sem_inc(to_act.sem, 1)
            for m in range(RC):
                step(dve.tensor_scalar(kmod[:, m], iclr[:, m], -1.0, v("k_a", l * RC + m), ALU.add, ALU.mult))
            step(dve.scalar_tensor_tensor(out=kmod, in0=kmod, scalar=1.0, in1=zk, op0=ALU.add, op1=ALU.mult))
            dve.wait_ge(to_dve.sem, to_dve.due(dve))
            dve.wait_ge(to_dve.sem, to_dve.due(dve))
            step(dve.tensor_scalar(lcum, lcum, 1e-12, None, ALU.max))
            dve.sem_inc(to_act.sem, 1)
            for m in range(RC):
                step(dve.scalar_tensor_tensor(out=sqk[:, m], in0=zr[:, m], scalar=v("r_k", l * RC + m), in1=kmod[:, m],
                                              op0=ALU.mult, op1=ALU.mult))
            dve.sem_inc(mix_ready.sem, 1)
            dve.wait_ge(to_dve.sem, to_dve.due(dve))
            step(dve.tensor_tensor(kk, kk, lcum, ALU.mult))
            step(dve.tensor_tensor(iclr, iclr, kk, ALU.mult))
            step(dve.tensor_tensor(bt, iclr, pinv, ALU.mult))
            step(dve.scalar_tensor_tensor(out=at_, in0=kk, scalar=-1.0, in1=pprev, op0=ALU.mult, op1=ALU.mult))
            step(dve.tensor_tensor(kt, kmod, pinv, ALU.mult))
            step(dve.tensor_copy(p_end, pcum[:, :, CH - 1::CH]))
            step(dve.tensor_tensor(rt, zr, pcum, ALU.mult))
            for m in range(RC):
                dve.wait_ge(D_.full, D_.filled())
                bank = D_.take()
                dve.tensor_tensor(bonus[:, m], bank[:, 0:LAT], zv[:, m], ALU.mult).then_inc(D_.free, 1)

        def pe_rwkv_core(pe, W, mm, l):
            for src in (zv, at_, bt, kt):
                for t in range(2):
                    pe.wait_ge(A_.free, A_.given_back())
                    bank = A_.claim()
                    for m in range(RC):
                        ins = pe.transpose(bank[:, m * P:(m + 1) * P], src[:, m, t * P:(t + 1) * P], ident)
                    ins.then_inc(A_.full, 1)

            def gram(t, g, a, b):
                pe.wait_ge(D_.free, D_.given_back())
                bank = D_.claim()
                r = slice(g * HD, (g + 1) * HD)
                for u in range(4):
                    mm(bank[:, u * P:(u + 1) * P], a[r, u, t * P:(t + 1) * P], b[r, u, t * P:(t + 1) * P],
                       inc=D_.full if u == 3 else None)

            for t in range(2):
                for g in range(2):
                    gram(t, g, bt, at_)
                for g in range(2):
                    gram(t, g, kt, at_)
                for g in range(2):
                    gram(t, g, bt, rt)
                    gram(t, g, kt, rt)
                for g in range(2):
                    pe.wait_ge(mix_ready.sem, mix_ready.due(pe))
                    pe.wait_ge(A_.free, A_.given_back())
                    bank = A_.claim()
                    for u in range(4):
                        mm(bank[:, u * P:(u + 1) * P], LTL[g][:, u, :], ident, inc=A_.full if u == 3 else None)
                for level in range(1, LEVELS):
                    for g in range(2):
                        pe.wait_ge(mix_ready.sem, mix_ready.due(pe))
                        pe.wait_ge(A_.free, A_.given_back())
                        bank = A_.claim()
                        for u in range(4):
                            mm(bank[:, u * P:(u + 1) * P], LTL[g][:, u, :], X[g][:, u, :],
                               inc=A_.full if u == 3 else None)
                    for g in range(2):
                        pe.wait_ge(act_ready.sem, act_ready.due(pe))
                        for a, b in (((XT, Y), (Y, XT)) if level < LEVELS - 1 else ((Y, XT),)):
                            pe.wait_ge(D_.free, D_.given_back())
                            bank = D_.claim()
                            for u in range(4):
                                mm(bank[:, u * P:(u + 1) * P], a[g][:, u, :], b[g][:, u, :],
                                   inc=D_.full if u == 3 else None)
                for g in range(2):
                    pe.wait_ge(mix_ready.sem, mix_ready.due(pe))
                    pe.wait_ge(A_.free, A_.given_back())
                    bank = A_.claim()
                    for u in range(4):
                        h = 2 * u + g
                        mm(bank[:, u * HD:(u + 1) * HD], LAK[g][:, u, :], vtok[:, t, h * HD:(h + 1) * HD],
                           inc=A_.full if u == 3 else None)
                    pe.wait_ge(A_.free, A_.given_back())
                    bank = A_.claim()
                    for u in range(4):
                        h = 2 * u + g
                        mm(bank[g * HD:(g + 1) * HD, u * P:(u + 1) * P], atok[:, t, h * HD:(h + 1) * HD], XT[g][:, u, :],
                           inc=A_.full if u == 3 else None)
                    pe.wait_ge(act_ready.sem, act_ready.due(pe))
                    pe.wait_ge(A_.free, A_.given_back())
                    bank = A_.claim()
                    for u in range(4):
                        mm(bank[:, u * HD:(u + 1) * HD], XT[g][:, u, :], W1[g][:, u, :], inc=A_.full if u == 3 else None)

        def act_rwkv_core(act, step, l):
            for dst in (vtok, atok, btok, ktok):
                for t in range(2):
                    act.wait_ge(A_.full, A_.filled())
                    bank = A_.take()
                    act.activation(dst[:, t], bank, ACT.Copy).then_inc(A_.free, 1)
            for t in range(2):
                for g in range(2):
                    act.wait_ge(A_.full, A_.filled())
                    bank = A_.take()
                    step(act.activation(X[g], bank.rearrange("p (a b) -> p a b", b=P), ACT.Copy))
                    act.sem_inc(A_.free, 1)
                    act.sem_inc(to_dve.sem, 1)
                for level in range(1, LEVELS):
                    for g in range(2):
                        act.wait_ge(A_.full, A_.filled())
                        bank = A_.take()
                        step(act.activation(Y[g], bank.rearrange("p (a b) -> p a b", b=P), ACT.Copy))
                        act.sem_inc(A_.free, 1)
                        act.sem_inc(act_ready.sem, 1)
                for g in range(2):
                    act.wait_ge(A_.full, A_.filled())
                    bank = A_.take()
                    step(act.activation(W1[g], bank[:, 0:4 * HD].rearrange("p (a b) -> p a b", b=HD), ACT.Copy))
                    act.sem_inc(A_.free, 1)
                    act.sem_inc(act_ready.sem, 1)
                    act.wait_ge(A_.full, A_.filled())
                    bank = A_.take()
                    r = slice(g * HD, (g + 1) * HD)
                    act.activation(xat[r, :, t, :], bank[r, :].rearrange("p (a b) -> p a b", b=P),
                                   ACT.Copy).then_inc(A_.free, 1)
                    act.wait_ge(A_.full, A_.filled())
                    bank = A_.take()
                    act.activation(by_group(utok, t)[:, :, g, :], bank[:, 0:256].rearrange("p (a b) -> p a b", b=HD),
                                   ACT.Copy).then_inc(A_.free, 1)

        def dve_rwkv_core(dve, step, l):
            def four(ap):
                return ap.unsqueeze(1).to_broadcast([P, 4, P])

            def bank4(bank):
                return bank.rearrange("p (a b) -> p a b", b=P)

            for t in range(2):
                for dst, mask in ((LT, "before"), (LAK, "before")):
                    for g in range(2):
                        dve.wait_ge(D_.full, D_.filled())
                        bank = D_.take()
                        step(dve.tensor_tensor(dst[g], bank4(bank), four(const(mask)), ALU.mult))
                        dve.sem_inc(D_.free, 1)
                for g in range(2):
                    for dst in (lrb, lrk):
                        dve.wait_ge(D_.full, D_.filled())
                        bank = D_.take()
                        dve.tensor_tensor(dst[:, t, g::2], bank4(bank), four(const("upto")),
                                          ALU.mult).then_inc(D_.free, 1)
                for g in range(2):
                    step(dve.tensor_tensor(LTL[g], LT[g], four(const("level", 0, P)), ALU.mult))
                    dve.sem_inc(mix_ready.sem, 1)
                    step(dve.tensor_tensor(XT[g], LTL[g], four(ident), ALU.add))
                for g in range(2):
                    dve.wait_ge(to_dve.sem, to_dve.due(dve))
                    step(dve.tensor_tensor(X[g], X[g], four(ident), ALU.add))
                    step(dve.tensor_tensor(LTL[g], LT[g], four(const("level", 1, P)), ALU.mult))
                    dve.sem_inc(mix_ready.sem, 1)
                for level in range(1, LEVELS):
                    for g in range(2):
                        if level < LEVELS - 1:
                            dve.wait_ge(D_.full, D_.filled())
                            bank = D_.take()
                            step(dve.tensor_tensor(X[g], X[g], bank4(bank), ALU.add))
                            dve.sem_inc(D_.free, 1)
                        dve.wait_ge(D_.full, D_.filled())
                        bank = D_.take()
                        step(dve.tensor_tensor(XT[g], XT[g], bank4(bank), ALU.add))
                        dve.sem_inc(D_.free, 1)
                        if level < LEVELS - 1:
                            step(dve.tensor_tensor(LTL[g], LT[g], four(const("level", level + 1, P)), ALU.mult))
                        dve.sem_inc(mix_ready.sem, 1)

        def pe_rwkv_out(pe, W, mm, l):
            for c in range(LAT // CH):
                t, r = c // 2, slice((c % 2) * CH, (c % 2 + 1) * CH)
                if c:
                    pe.wait_ge(mix_ready.sem, mix_ready.due(pe))
                    for g in range(2):
                        pe.wait_ge(D_.free, D_.given_back())
                        bank = D_.claim()
                        q = slice(g * HD, (g + 1) * HD)
                        for u in range(4):
                            mm(bank[r, u * HD:(u + 1) * HD], xat[q, u, t, r], state[c - 1][q, u, :],
                               inc=D_.full if u == 3 else None)
                if c < LAT // CH - 1:
                    if c:
                        pe.wait_ge(mix_ready.sem, mix_ready.due(pe))
                    pe.wait_ge(D_.free, D_.given_back())
                    bank = D_.claim()
                    for h in range(8):
                        q = slice((h % 2) * HD, (h % 2 + 1) * HD)
                        o = bank[q, (h // 2) * HD:(h // 2 + 1) * HD]
                        f = slice(h * HD, (h + 1) * HD)
                        mm(o, btok[r, t, f], utok[r, t, f], True, False)
                        mm(o, ktok[r, t, f], vtok[r, t, f], False, True, D_.full if h == 7 else None)
            pe.wait_ge(mix_ready.sem, mix_ready.due(pe))
            for m in range(RC):
                for hh in range(2):
                    pe.wait_ge(D_.free, D_.given_back())
                    bank = D_.claim()
                    h = 2 * m + hh
                    q = slice(hh * HD, (hh + 1) * HD)
                    f = slice(h * HD, (h + 1) * HD)
                    for t in range(2):
                        o = bank[q, t * P:(t + 1) * P]
                        mm(o, vtok[:, t, f], lrk[:, t, h, :], True, False)
                        mm(o, utok[:, t, f], lrb[:, t, h, :], False, False)
                        for c in range(max(2 * t, 1), 2 * t + 2):
                            last = c == 2 * t + 1
                            mm(bank[q, c * CH:(c + 1) * CH], state[c - 1][q, m, :], rt[q, m, c * CH:(c + 1) * CH],
                               False, last, D_.full if last and t else None)
            pe.wait_ge(mix_ready.sem, mix_ready.due(pe))
            for m in range(RC):
                pe.wait_ge(D_.free, D_.given_back())
                mm(D_.claim()[:, 0:LAT], bones, y_[:, m]).then_inc(D_.full, 1)
            pe.wait_ge(act_ready.sem, act_ready.due(pe))
            for m in range(RC):
                pe.wait_ge(A_.free, A_.given_back())
                mm(A_.claim()[:, 0:LAT], bones, sqk_y[:, m]).then_inc(A_.full, 1)

        sqk_y = fm(8 + 1)
        rstd_y = fm(3)

        def dve_rwkv_out(dve, step, l):
            for c in range(LAT // CH):
                t, r = c // 2, slice((c % 2) * CH, (c % 2 + 1) * CH)
                if c:
                    for g in range(2):
                        dve.wait_ge(D_.full, D_.filled())
                        bank = D_.take()
                        o = by_group(utok, t)[r, :, g, :]
                        step(dve.tensor_tensor(o, o, bank[r, 0:256].rearrange("p (u f) -> p u f", f=HD), ALU.add))
                        dve.sem_inc(D_.free, 1)
                    dve.sem_inc(mix_ready.sem, 1)
                if c < LAT // CH - 1:
                    dve.wait_ge(D_.full, D_.filled())
                    bank = D_.take()
                    s = state[c]
                    pe_bc = p_end[:, :, c:c + 1].to_broadcast([P, RC, HD])
                    b4 = bank[:, 0:RC * HD].rearrange("p (m i) -> p m i", i=HD)
                    if c:
                        step(dve.tensor_tensor(s, state[c - 1], b4, ALU.add))
                        step(dve.tensor_tensor(s, s, pe_bc, ALU.mult))
                    else:
                        step(dve.tensor_tensor(s, b4, pe_bc, ALU.mult))
                    dve.sem_inc(D_.free, 1)
                    dve.sem_inc(mix_ready.sem, 1)
            for h in range(8):
                dve.wait_ge(D_.full, D_.filled())
                bank = D_.take()
                q = slice((h % 2) * HD, (h % 2 + 1) * HD)
                step(dve.tensor_copy(y_[q, h // 2], bank[q, 0:LAT]))
                dve.sem_inc(D_.free, 1)
            dve.sem_inc(mix_ready.sem, 1)
            for m in range(RC):
                dve.wait_ge(D_.full, D_.filled())
                bank = D_.take()
                step(dve.scalar_tensor_tensor(out=y_[:, m], in0=bank[:, 0:LAT], scalar=-1.0 / HD, in1=y_[:, m],
                                              op0=ALU.mult, op1=ALU.add))
                dve.sem_inc(D_.free, 1)
            dve.sem_inc(to_act.sem, 1)
            dve.wait_ge(to_dve.sem, to_dve.due(dve))
            step(dve.tensor_tensor(y_, y_, rstd_y, ALU.mult))
            for m in range(RC):
                step(dve.tensor_scalar(y_[:, m], y_[:, m], v("ln_w", l * RC + m), v("ln_b", l * RC + m),
                                       ALU.mult, ALU.add))
            step(dve.tensor_tensor(y_, y_, bonus, ALU.add))
            step(dve.tensor_tensor(oa, y_, gate, ALU.mult))

        def act_rwkv_out(act, step, l):
            act.wait_ge(to_act.sem, to_act.due(act))
            step(act.activation(sqk_y, y_, ACT.Square))
            act.sem_inc(act_ready.sem, 1)
            for m in range(RC):
                act.wait_ge(A_.full, A_.filled())
                bank = A_.take()
                act_rsqrt(act, step, rstd_y[:, m], bank[:, 0:LAT], 1.0 / HD, const("gn_eps"))
                act.sem_inc(A_.free, 1)
            act.sem_inc(to_dve.sem, 1)

        Q_ = Carve(B0)
        fN = Q_(8, LAT)
        dup = Q_(4, 2, LAT)
        vsw = Q_(2, 3, P)
        ngate = Q_(2, 24)
        zpe = Q_(2, 16, 2, 15)
        hidc = Q_(2, 2, 30)
        kcmp = Q_(30)
        vcmp = Q_(2, HD)
        sc = Q_(8, N_CMP)
        pcT = Q_(QT, 8, P)
        mx8 = Q_(8)
        fS = Q_(5, LAT)
        dupS = Q_(2, LAT)
        vS = Q_(2, P)
        s_ring = ring("s2", [Q_(2, LAT) for _ in range(3)])
        e_ring = ring("e2", [Q_(2, LAT) for _ in range(3)])
        n_ring = ring("n2", [Q_(2, LAT) for _ in range(2)])
        nt_ring = ring("nt2", [Q_(4, P) for _ in range(2)])
        st2 = Q_(8, 8)

        def pe_nsa_in(pe, W, mm, l):
            pe_project(pe, W, mm, "w_in", l, [*range(IN["nq"], IN["nvs"], P), IN["nkw"]], LAT, lambda _: D_, hT)
            for c, width in ((IN["nvs"], 1), (IN["nvw"], 2)):
                pe.wait_ge(D_.free, D_.given_back(2))
                banks = [D_.claim() for _ in range(2)]
                for k in range(DC):
                    w = W.next("w_in", l, k * P, c, width=width)
                    for t in range(2):
                        mm(banks[t][:, 0:width * P], hT[:, k, t * P:(t + 1) * P], w, k == 0, k == DC - 1,
                           D_.full if k == DC - 1 else None)
            pe.wait_ge(mix_ready.sem, mix_ready.due(pe))
            for i in range(4):
                for g in range(2):
                    pe.wait_ge(D_.free, D_.given_back())
                    mm(D_.claim()[:, 0:LAT], const("sel", g, P), fN[:, 4 + i, :]).then_inc(D_.full, 1)
            pe.wait_ge(mix_ready.sem, mix_ready.due(pe))
            for n, name in enumerate(("nsa_ck", "nsa_cv")):
                for h in range(2):
                    pe.wait_ge(A_.free, A_.given_back())
                    bank = A_.claim()
                    for k in range(16):
                        mm(bank[:, 0:30], W.next(name + "_w1", l, k * P, h * P),
                           zpe[:, n, k].rearrange("p g c -> p (g c)"), k == 0, k == 15, A_.full if k == 15 else None)
                pe.wait_ge(act_ready.sem, act_ready.due(pe))
                if n == 0:
                    pe.wait_ge(D_.free, D_.given_back())
                    bank = D_.claim()
                    for k in range(2):
                        w = W.next(name + "_w2", l, k * P, 0)
                        for half in range(2):
                            mm(bank[half * HD:(half + 1) * HD, 0:30], w[:, 0:HD], hidc[:, n, k, :], k == 0, k == 1,
                               D_.full if k and half else None)
                else:
                    pe.wait_ge(D_.free, D_.given_back(2))
                    banks = [D_.claim() for _ in range(2)]
                    for k in range(2):
                        w = W.next(name + "_w2", l, k * P, 0)
                        for g in range(2):
                            mm(banks[g][0:N_CMP, 0:HD], hidc[:, n, k, g * N_CMP:(g + 1) * N_CMP], w[:, 0:HD],
                               k == 0, k == 1, D_.full if k else None)

        def act_nsa_in(act, step, l):
            act.wait_ge(to_act.sem, to_act.due(act))
            step(act.activation(ngate, vsw[:, :, 2, 0:24], ACT.Sigmoid))
            for n in range(2):
                for h in range(2):
                    act.wait_ge(A_.full, A_.filled())
                    bank = A_.take()
                    step(act.activation(hidc[:, n, h, :], bank[:, 0:30], ACT.Gelu))
                    act.sem_inc(A_.free, 1)
                act.sem_inc(act_ready.sem, 1)

        def dve_nsa_in(dve, step, l):
            for i in range(8):
                copy_out(dve, fN[:, i, :], LAT)
            for t in range(2):
                copy_out(dve, vsw[:, t, 0, :], P)
            for t in range(2):
                copy_out(dve, vsw[:, t, 1:3, :].rearrange("p a b -> p (a b)"), 2 * P)
            dve.drain().then_inc(mix_ready.sem, 1)
            dve.sem_inc(to_act.sem, 1)
            for i in range(4):
                for g in range(2):
                    dve.wait_ge(D_.full, D_.filled())
                    bank = D_.take()
                    step(dve.tensor_copy(dup[:, i, g, :], bank[:, 0:LAT]))
                    dve.sem_inc(D_.free, 1)
            for n, name in enumerate(("pe_k", "pe_v")):
                for par in range(2):
                    r = slice(par * HD, (par + 1) * HD)
                    tokens16 = dup[r, n].rearrange("p g (c l x) -> p g c l x", l=8, x=2)
                    for a in range(2):
                        pos = v(name, l * 16 + a * 8, 8)[r, :]
                        for g in range(2):
                            o = zpe[r, n, a * 8:(a + 1) * 8, g, :].rearrange("p l c -> p c l")
                            step(dve.tensor_tensor(o, tokens16[:, g, a:a + N_CMP, :, par],
                                                   pos.unsqueeze(1).to_broadcast([HD, N_CMP, 8]), ALU.add))
            dve.sem_inc(mix_ready.sem, 1)
            dve.wait_ge(D_.full, D_.filled())
            bank = D_.take()
            dve.tensor_copy(kcmp, bank[:, 0:30]).then_inc(D_.free, 1)
            for g in range(2):
                dve.wait_ge(D_.full, D_.filled())
                bank = D_.take()
                dve.tensor_copy(vcmp[0:N_CMP, g, :], bank[0:N_CMP, 0:HD]).then_inc(D_.free, 1)

        def pe_nsa_cmp(pe, W, mm):
            for q in range(QT):
                for half in range(2):
                    pe.wait_ge(D_.free, D_.given_back())
                    bank = D_.claim()
                    r = slice(half * HD, (half + 1) * HD)
                    for u in range(4):
                        mm(bank[:, u * N_CMP:(u + 1) * N_CMP], fN[r, u, q * P:(q + 1) * P],
                           kcmp[r, (u // 2) * N_CMP:(u // 2 + 1) * N_CMP], inc=D_.full if u == 3 else None)
                pe.wait_ge(mix_ready.sem, mix_ready.due(pe))
                for half in range(2):
                    pe.wait_ge(A_.free, A_.given_back())
                    bank = A_.claim()
                    for u in range(4):
                        ins = pe.transpose(bank[0:N_CMP, u * P:(u + 1) * P], sc[:, 4 * half + u, :], ident)
                    ins.then_inc(A_.full, 1)

        def act_nsa_cmp(act, step):
            for q in range(QT):
                act.wait_ge(to_act.sem, to_act.due(act))
                step(act.activation(sc, sc, ACT.Exp))
                act.sem_inc(to_dve.sem, 1)
                for half in range(2):
                    act.wait_ge(A_.full, A_.filled())
                    bank = A_.take()
                    step(act.activation(pcT[0:N_CMP, q, 4 * half:4 * half + 4, :],
                                        bank[0:N_CMP, :].rearrange("p (a b) -> p a b", b=P), ACT.Copy))
                    act.sem_inc(A_.free, 1)
                act.sem_inc(to_dve.sem, 1)

        def dve_nsa_cmp(dve, step):
            def wide(a):
                return a.unsqueeze(2).to_broadcast([P, 8, N_CMP])

            for q in range(QT):
                mask = const("cmp", q, N_CMP).unsqueeze(1).to_broadcast([P, 4, N_CMP])
                for half in range(2):
                    dve.wait_ge(D_.full, D_.filled())
                    bank = D_.take()
                    step(dve.scalar_tensor_tensor(out=sc[:, half::2, :],
                                                  in0=bank[:, 0:4 * N_CMP].rearrange("p (a b) -> p a b", b=N_CMP),
                                                  scalar=SCALE, in1=mask, op0=ALU.mult, op1=ALU.add))
                    dve.sem_inc(D_.free, 1)
                step(dve.tensor_reduce(mx8, sc, AX, ALU.max))
                step(dve.tensor_scalar(mx8, mx8, NEG / 10, None, ALU.max))
                step(dve.tensor_tensor(sc, sc, wide(mx8), ALU.subtract))
                dve.sem_inc(to_act.sem, 1)
                dve.wait_ge(to_dve.sem, to_dve.due(dve))
                step(dve.tensor_reduce(mx8, sc, AX, ALU.add))
                step(dve.tensor_scalar(mx8, mx8, 1e-30, None, ALU.max))
                step(dve.reciprocal(mx8, mx8))
                step(dve.tensor_tensor(mx8, mx8, ngate[:, q].rearrange("p (h i) -> p h i", i=3)[:, :, 0], ALU.mult))
                step(dve.tensor_tensor(sc, sc, wide(mx8), ALU.mult))
                dve.sem_inc(mix_ready.sem, 1)
                dve.wait_ge(to_dve.sem, to_dve.due(dve))

        N_UNITS = [(h, q) for h in range(8) for q in range(QT)]

        def bias_of(base, h, q):
            return biasT[:, base + h, P * (1 - q):2 * P] if q == 0 else biasT[:, base + h, 0:2 * P]

        def pe_rel(pe, mm, qsrc, keys, values, cmp):
            n, parts = len(N_UNITS), len(keys)
            for i in range(n + 3):
                if i < n:
                    h, q = N_UNITS[i]
                    r = slice((h % 2) * HD, (h % 2 + 1) * HD)
                    nk = (q + 1) * P
                    pe.wait_ge(D_.free, D_.given_back())
                    bank = D_.claim()
                    for j, key in enumerate(keys):
                        mm(bank[:, j * LAT:j * LAT + nk], qsrc[r, h // 2, q * P:(q + 1) * P], key[r, h // 4, 0:nk],
                           inc=D_.full if j == parts - 1 else None)
                if 2 <= i < n + 2:
                    h, q = N_UNITS[i - 2]
                    pe.wait_ge(n_ring.full, n_ring.filled())
                    pe.wait_ge(tpr.free, tpr.given_back())
                    a, t = n_ring.take(), tpr.claim()
                    for j in range(parts):
                        for k in range(q + 1):
                            ins = pe.transpose(t[:, (2 * j + k) * P:(2 * j + k + 1) * P], a[:, j, k * P:(k + 1) * P], ident)
                    ins.then_inc(tpr.full, 1)
                if i >= 3:
                    h, q = N_UNITS[i - 3]
                    r = slice((h % 2) * HD, (h % 2 + 1) * HD)
                    f = slice((h // 4) * HD, (h // 4 + 1) * HD)
                    pe.wait_ge(nt_ring.full, nt_ring.filled())
                    pe.wait_ge(ot_ring.free, ot_ring.given_back())
                    t, o = nt_ring.take(), ot_ring.claim()
                    if cmp:
                        mm(o[r, 0:P], vcmp[0:N_CMP, h // 4, :], pcT[0:N_CMP, q, h, :], True, False)
                    steps = [(j, k) for j in range(parts) for k in range(q + 1)]
                    for x, (j, k) in enumerate(steps):
                        last = x == len(steps) - 1
                        mm(o[r, 0:P], values[j][:, k, f], t[:, 2 * j + k, :], not cmp and x == 0, last,
                           ot_ring.full if last else None)

        def act_rel(act, step, parts, sink):
            n = len(N_UNITS)
            for i in range(n + 2):
                if i < n:
                    h, q = N_UNITS[i]
                    nk = (q + 1) * P
                    act.wait_ge(s_ring.full, s_ring.filled())
                    act.wait_ge(e_ring.free, e_ring.given_back())
                    s, e, st = s_ring.take(), e_ring.claim(), st2[:, i % 8, :]
                    for j in range(parts):
                        step(act.activation(e[:, j, 0:nk], s[:, j, 0:nk], ACT.Exp, bias=st[:, j:j + 1],
                                            accum_out=st[:, 2 + j:3 + j]))
                    act.sem_inc(s_ring.free, 1)
                    if sink is not None:
                        step(act.activation(st[:, 6:7], sink(h), ACT.Exp, bias=st[:, 0:1]))
                    act.sem_inc(e_ring.full, 1)
                if i >= 2:
                    h, q = N_UNITS[i - 2]
                    act.wait_ge(tpr.full, tpr.filled())
                    act.wait_ge(nt_ring.free, nt_ring.given_back())
                    tp, t = tpr.take(), nt_ring.claim()
                    act.sem_inc(n_ring.free, 1)
                    src = tp.rearrange("p (j k b) -> p j k b", j=2, b=P)[:, 0:parts, 0:q + 1, :]
                    dst = t.rearrange("p (j k) b -> p j k b", j=2)[:, 0:parts, 0:q + 1, :]
                    step(act.activation(dst, src, ACT.Copy))
                    act.sem_inc(tpr.free, 1)
                    act.sem_inc(nt_ring.full, 1)

        def dve_rel(dve, step, parts, base, sink, gates, out_):
            n = len(N_UNITS)
            for i in range(n + 4):
                if i < n:
                    h, q = N_UNITS[i]
                    nk = (q + 1) * P
                    dve.wait_ge(D_.full, D_.filled())
                    dve.wait_ge(s_ring.free, s_ring.given_back())
                    bank, s, st = D_.take(), s_ring.claim(), st2[:, i % 8, :]
                    b = bank.rearrange("p (j k) -> p j k", j=2)[:, 0:parts, 0:nk]
                    bias = bias_of(base, h, q).unsqueeze(1).to_broadcast([P, parts, nk])
                    step(dve.scalar_tensor_tensor(out=s[:, 0:parts, 0:nk], in0=b, scalar=SCALE, in1=bias,
                                                  op0=ALU.mult, op1=ALU.add))
                    dve.sem_inc(D_.free, 1)
                    step(dve.tensor_reduce(st[:, 0:parts], s[:, 0:parts, 0:nk], AX, ALU.max))
                    if sink is not None:
                        step(dve.tensor_scalar(st[:, 0:1], st[:, 0:1], sink(h), -1.0, ALU.max, ALU.mult))
                    else:
                        step(dve.tensor_scalar(st[:, 0:parts], st[:, 0:parts], -1.0, None, ALU.mult))
                    dve.sem_inc(s_ring.full, 1)
                if 1 <= i < n + 1:
                    h, q = N_UNITS[i - 1]
                    nk = (q + 1) * P
                    dve.wait_ge(e_ring.full, e_ring.filled())
                    dve.wait_ge(n_ring.free, n_ring.given_back())
                    e, a, st = e_ring.take(), n_ring.claim(), st2[:, (i - 1) % 8, :]
                    if sink is not None:
                        step(dve.tensor_tensor(st[:, 2:3], st[:, 2:3], st[:, 6:7], ALU.add))
                    step(dve.reciprocal(st[:, 4:4 + parts], st[:, 2:2 + parts]))
                    if gates:
                        step(dve.tensor_tensor(st[:, 4:6], st[:, 4:6], ngate[:, q, 3 * h + 1:3 * h + 3], ALU.mult))
                    for j in range(parts):
                        step(dve.tensor_scalar(a[:, j, 0:nk], e[:, j, 0:nk], st[:, 4 + j:5 + j], None, ALU.mult))
                    dve.sem_inc(e_ring.free, 1)
                    dve.sem_inc(n_ring.full, 1)
                if i >= 4:
                    h, q = N_UNITS[i - 4]
                    r = slice((h % 2) * HD, (h % 2 + 1) * HD)
                    dve.wait_ge(ot_ring.full, ot_ring.filled())
                    o = ot_ring.take()
                    step(dve.tensor_copy(out_[r, h // 2, q * P:(q + 1) * P], o[r, 0:P]))
                    dve.sem_inc(ot_ring.free, 1)
                    dve.sem_inc(nt_ring.free, 1)

        def pe_nsa_attend(pe, W, mm):
            pe_rel(pe, mm, fN, [dup[:, 2], dup[:, 3]], [vsw[:, :, 0, :], vsw[:, :, 1, :]], True)

        def pe_swa_in(pe, W, mm, l):
            pe_project(pe, W, mm, "w_in", l, range(IN["sq"], IN["sv"], P), LAT, lambda _: D_, hT)
            pe.wait_ge(D_.free, D_.given_back(2))
            banks = [D_.claim() for _ in range(2)]
            for k in range(DC):
                w = W.next("w_in", l, k * P, IN["sv"])
                for t in range(2):
                    mm(banks[t][:, 0:P], hT[:, k, t * P:(t + 1) * P], w, k == 0, k == DC - 1,
                       D_.full if k == DC - 1 else None)
            pe.wait_ge(mix_ready.sem, mix_ready.due(pe))
            for g in range(2):
                pe.wait_ge(D_.free, D_.given_back())
                mm(D_.claim()[:, 0:LAT], const("sel", g, P), fS[:, 4, :]).then_inc(D_.full, 1)

        def dve_swa_in(dve, step, l):
            for i in range(5):
                copy_out(dve, fS[:, i, :], LAT)
            for t in range(2):
                copy_out(dve, vS[:, t, :], P)
            dve.drain().then_inc(mix_ready.sem, 1)
            for g in range(2):
                copy_out(dve, dupS[:, g, :], LAT)

        G_ = Carve(B0)
        merged = G_(DC, LAT)
        g_ring = ring("gate", [G_(LAT) for _ in range(3)])
        mtmp = G_(LAT)
        merged_ready = signal("merged_ready")

        def pe_merge(pe, W, mm, l):
            for m in range(DC):
                for i, (name, o) in enumerate((("w_br_a", oa), ("w_br_b", ob), ("w_br_c", oc))):
                    pe_project(pe, W, mm, "w_in", l, [IN["gates"] + i * D + m * P], LAT, lambda _: A_, hT)
                    pe.wait_ge(D_.free, D_.given_back())
                    bank = D_.claim()
                    for k in range(RC):
                        mm(bank[:, 0:LAT], W.next(name, l, k * P, m * P), o[:, k, :], k == 0, k == RC - 1,
                           D_.full if k == RC - 1 else None)
            pe.wait_ge(merged_ready.sem, merged_ready.due(pe, DC))
            pe_project(pe, W, mm, "w_out", l, range(0, D, P), LAT, lambda _: D_, merged)

        def act_merge(act, step):
            for n in range(3 * DC):
                act.wait_ge(A_.full, A_.filled())
                act.wait_ge(g_ring.free, g_ring.given_back())
                bank, g = A_.take(), g_ring.claim()
                step(act.activation(g, bank[:, 0:LAT], ACT.Sigmoid))
                act.sem_inc(A_.free, 1)
                act.sem_inc(g_ring.full, 1)

        def dve_merge(dve, step):
            for m in range(DC):
                for i in range(3):
                    dve.wait_ge(D_.full, D_.filled())
                    dve.wait_ge(g_ring.full, g_ring.filled())
                    bank, g = D_.take(), g_ring.take()
                    dst = mtmp if i else merged[:, m]
                    step(dve.tensor_tensor(dst, g, bank[:, 0:LAT], ALU.mult))
                    dve.sem_inc(D_.free, 1)
                    dve.sem_inc(g_ring.free, 1)
                    if i:
                        step(dve.tensor_tensor(merged[:, m], merged[:, m], mtmp, ALU.add))
                dve.sem_inc(merged_ready.sem, 1)
            for m in range(DC):
                dve.wait_ge(D_.full, D_.filled())
                bank = D_.take()
                step(dve.tensor_tensor(xT[:, m, 0:LAT], xT[:, m, 0:LAT], bank[:, 0:LAT], ALU.add))
                dve.sem_inc(D_.free, 1)

        E_ = Carve(B0)
        ztok = E_(QT, D)
        ytok = E_(QT, D)
        experts = E_(QT, SLOTS).bitcast(U32)
        gates_p = E_(QT, SLOTS)
        hbuf = E_(QT, SLOTS)
        subs = E_(QT, 2 * PEER_H, NKEYS)
        q_ring = ring("pq", [E_(LAT) for _ in range(2)])
        top_s = E_(2, PEER_K)
        top_i = E_(2, PEER_K)
        top_u = E_(2, PEER_K).bitcast(U32)
        cand = E_(PEER_K, PEER_K)
        pick = E_(2, PEER_K, PEER_K)
        best = E_(PEER_H, PEER_K)
        flat_u = E_(PEER_K).bitcast(U32)
        digit_u = E_(2, PEER_K).bitcast(U32)
        digit = E_(2, PEER_K)
        hsum = E_(PEER_H)
        GB = (ARENA - E_.at) // D
        rows = [E_(D) for _ in range(GB)]
        row_full = [sem(f"row_full{i}") for i in range(GB)]
        row_free = sem("row_free")
        ztok_ready = signal("ztok_ready")
        subs_ready = signal("subs_ready")
        experts_ready = signal("experts_ready")
        GATHERS = [(t, x, s) for t in range(QT) for x in range(2) for s in range(SLOTS)]

        def pe_peer(pe, W, mm, l):
            pe_norm(pe, mm, LAT)
            pe.wait_ge(h_ready.sem, h_ready.due(pe, DC))
            for t in range(QT):
                for half in range(2):
                    pe.wait_ge(A_.free, A_.given_back())
                    bank = A_.claim()
                    for k in range(4):
                        ins = pe.transpose(bank[:, k * P:(k + 1) * P], hT[:, 4 * half + k, t * P:(t + 1) * P], ident)
                    ins.then_inc(A_.full, 1)
            for i in range(2 * PEER_H):
                pe_project(pe, W, mm, "peer_wq", l, [i * P], LAT, lambda _: A_, hT)
                w = W.next("peer_subkeys", l, 0, i * P)
                pe.wait_ge(q_ring.full, q_ring.filled())
                qc = q_ring.take()
                pe.wait_ge(A_.free, A_.given_back())
                bank = A_.claim()
                for t in range(QT):
                    mm(bank[:, t * P:(t + 1) * P], qc[:, t * P:(t + 1) * P], w, inc=A_.full if t else None)

        def act_peer(act, step, l):
            act_norm(act, step, LAT, gained(act, "ln2", l))
            for t in range(QT):
                for half in range(2):
                    act.wait_ge(A_.full, A_.filled())
                    bank = A_.take()
                    step(act.activation(ztok[:, t, half * 512:(half + 1) * 512], bank, ACT.Copy))
                    act.sem_inc(A_.free, 1)
            act.sem_inc(ztok_ready.sem, 1)
            for i in range(2 * PEER_H):
                act.wait_ge(A_.full, A_.filled())
                bank = A_.take()
                act.wait_ge(q_ring.free, q_ring.given_back())
                qc = q_ring.claim()
                step(act.activation(qc, bank[:, 0:LAT], ACT.Copy))
                act.sem_inc(A_.free, 1)
                act.sem_inc(q_ring.full, 1)
                act.wait_ge(A_.full, A_.filled())
                bank = A_.take()
                act.sem_inc(q_ring.free, 1)
                step(act.activation(subs[:, :, i, :], bank[:, 0:2 * P].rearrange("p (t n) -> p t n", t=2), ACT.Copy))
                act.sem_inc(A_.free, 1)
                act.sem_inc(subs_ready.sem, 1)
            for t in range(QT):
                act.wait_ge(to_act.sem, to_act.due(act))
                step(act.activation(gates_p[:, t], gates_p[:, t], ACT.Exp))
                step(act.activation(hbuf[:, t], hbuf[:, t], ACT.Gelu))
                act.sem_inc(to_dve.sem, 1)

        def dve_top16(dve, step, src, vals, idx):
            step(dve.max(vals[:, 0:8], src))
            step(dve.max_index(idx[:, 0:8], vals[:, 0:8], src))
            step(dve.match_replace(src, vals[:, 0:8], src, -3.0e38))
            step(dve.max(vals[:, 8:16], src))
            step(dve.max_index(idx[:, 8:16], vals[:, 8:16], src))

        def dve_experts(dve, step, l, t, h):
            sq = [P, PEER_K, PEER_K]
            for x in range(2):
                if t == 0:
                    dve.wait_ge(subs_ready.sem, subs_ready.due(dve))
                dve_top16(dve, step, subs[:, t, 2 * h + x, :], top_s[:, x, :], top_u[:, x, :])
            step(dve.tensor_copy(top_i, top_u))
            step(dve.tensor_tensor(cand, top_s[:, 0, :].unsqueeze(2).to_broadcast(sq),
                                   top_s[:, 1, :].unsqueeze(1).to_broadcast(sq), ALU.add))
            dve_top16(dve, step, cand.rearrange("p a b -> p (a b)"), best[:, h, :], flat_u)
            dve.tensor_scalar(digit_u[:, 0], flat_u, 4, None, ALU.logical_shift_right)
            step(dve.tensor_scalar(digit_u[:, 1], flat_u, PEER_K - 1, None, ALU.bitwise_and))
            step(dve.tensor_copy(digit, digit_u))
            for x in range(2):
                step(dve.tensor_tensor(pick[:, x], digit[:, x].unsqueeze(2).to_broadcast(sq),
                                       const("iota").unsqueeze(1).to_broadcast(sq), ALU.is_equal))
                step(dve.tensor_tensor(pick[:, x], pick[:, x], top_i[:, x].unsqueeze(1).to_broadcast(sq), ALU.mult))
            step(dve.tensor_reduce(digit, pick, AX, ALU.add))
            step(dve.tensor_scalar(digit[:, 0], digit[:, 0], float(NKEYS), float(l * EXPERTS), ALU.mult, ALU.add))
            step(dve.tensor_tensor(experts[:, t, h * PEER_K:(h + 1) * PEER_K], digit[:, 0], digit[:, 1], ALU.add))
            dve.sem_inc(experts_ready.sem, 1)

        def pool_peer(pool, base):
            for n, (t, x, s) in enumerate(GATHERS):
                n += base
                if x == 0 and s % PEER_K == 0:
                    pool.wait_ge(experts_ready.sem, experts_ready.due(pool))
                if n >= GB:
                    pool.wait_ge(row_free, n - GB + 1)
                pool.indirect_dma_start(out=rows[n % GB], out_offset=None, in_=(peer_u, peer_v)[x],
                                        in_offset=bass.IndirectOffsetOnAxis(ap=experts[:, t, s:s + 1], axis=0)
                                        ).then_inc(row_full[n % GB], 16)

        def dve_peer(dve, step, l, base):
            dve_norm(dve, LAT)
            n = base
            for t in range(QT):
                dve_experts(dve, step, l, t, 0)
                if t == 0:
                    dve.wait_ge(ztok_ready.sem, ztok_ready.due(dve))
                for h in range(PEER_H):
                    if h + 1 < PEER_H:
                        dve_experts(dve, step, l, t, h + 1)
                    for s in range(h * PEER_K, (h + 1) * PEER_K):
                        r = rows[n % GB]
                        dve.wait_ge(row_full[n % GB], 16 * (n // GB + 1))
                        dve.tensor_tensor_reduce(r, r, ztok[:, t], 1.0, 0.0, ALU.mult, ALU.add,
                                                 hbuf[:, t, s:s + 1]).then_inc(row_free, 1)
                        n += 1
                gp = gates_p[:, t].rearrange("p (h j) -> p h j", h=PEER_H)
                dve.tensor_tensor(gp, best, best[:, :, 0:1].to_broadcast([P, PEER_H, PEER_K]), ALU.subtract)
                dve.drain().then_inc(to_act.sem, 1)
                dve.wait_ge(to_dve.sem, to_dve.due(dve))
                step(dve.tensor_reduce(hsum, gp, AX, ALU.add))
                step(dve.reciprocal(hsum, hsum))
                step(dve.tensor_tensor(gp, gp, hsum.unsqueeze(2).to_broadcast([P, PEER_H, PEER_K]), ALU.mult))
                step(dve.tensor_tensor(hbuf[:, t], hbuf[:, t], gates_p[:, t], ALU.mult))
                for s in range(SLOTS):
                    r, w = rows[n % GB], hbuf[:, t, s:s + 1]
                    dve.wait_ge(row_full[n % GB], 16 * (n // GB + 1))
                    if s == 0:
                        step(dve.tensor_scalar(ytok[:, t], r, w, None, ALU.mult))
                    else:
                        step(dve.scalar_tensor_tensor(out=ytok[:, t], in0=r, scalar=w, in1=ytok[:, t],
                                                      op0=ALU.mult, op1=ALU.add))
                    dve.sem_inc(row_free, 1)
                    n += 1

        def pe_peer_out(pe):
            for m in range(DC):
                pe.wait_ge(D_.free, D_.given_back())
                bank = D_.claim()
                for t in range(QT):
                    ins = pe.transpose(bank[:, t * P:(t + 1) * P], ytok[:, t, m * P:(m + 1) * P], ident)
                ins.then_inc(D_.full, 1)

        def dve_peer_out(dve, step):
            for m in range(DC):
                dve.wait_ge(D_.full, D_.filled())
                bank = D_.take()
                step(dve.tensor_tensor(xT[:, m, 0:LAT], xT[:, m, 0:LAT], bank[:, 0:LAT], ALU.add))
                dve.sem_inc(D_.free, 1)

        block = ctx.enter_context(nc.Block())
        FIRST_LOADS = 3
        GATHER_STAGE = 22
        N_STAGES = 13 + 2 * 11 + 1
        last_tile = [0]
        out_done = signal("out_done", 16)

        def want(n):
            return until >= n

        @block.tensor
        def _(pe):
            W = Weights(pe)
            mm = make_mm(pe, W)

            def b_out():
                pe.wait_ge(h_ready.sem, h_ready.due(pe))
                pe_project(pe, W, mm, "b_w_o", 0, range(0, D, P), LAT, lambda _: D_, oB)

            pe.wait_ge(loaded.sem, loaded.due(pe, FIRST_LOADS))
            stages = [
                lambda: pe_ada(pe, W, mm, 0),
                lambda: pe_ffn(pe, W, mm, "pre", 0, TOK),
                lambda: pe_a_qkv(pe, W, mm),
                lambda: pe_a_attend(pe, W, mm),
                lambda: pe_a_out(pe, W, mm),
                lambda: pe_ffn(pe, W, mm, "post", 0, TOK),
                lambda: pe_ada(pe, W, mm, 1),
                lambda: pe_ffn(pe, W, mm, "pre", 1, TOK),
                lambda: pe_b_qkv(pe, W, mm),
                lambda: pe_b_attend(pe, W, mm),
                b_out,
                lambda: pe_ffn(pe, W, mm, "post", 1, LAT),
                lambda: pe_bias(pe, W, mm),
            ]
            for l in range(2):
                stages += [
                    lambda l=l: pe_rwkv_in(pe, W, mm, l),
                    lambda l=l: pe_rwkv_core(pe, W, mm, l),
                    lambda l=l: pe_rwkv_out(pe, W, mm, l),
                    lambda l=l: pe_nsa_in(pe, W, mm, l),
                    lambda: pe_nsa_cmp(pe, W, mm),
                    lambda: pe_nsa_attend(pe, W, mm),
                    lambda l=l: pe_swa_in(pe, W, mm, l),
                    lambda: pe_rel(pe, mm, fS, [dupS], [vS], False),
                    lambda l=l: pe_merge(pe, W, mm, l),
                    lambda l=l: pe_peer(pe, W, mm, l),
                    lambda: pe_peer_out(pe),
                ]
            stages.append(lambda: pe_norm(pe, mm, LAT))
            for n, s in enumerate(stages):
                if want(n):
                    s()
                    end_phase(pe)
            last_tile[0] = -(-W.at // W_TILE)

        @block.scalar
        def _(act):
            step = Stepper(act, act_chain)
            act.wait_ge(loaded.sem, loaded.due(act, FIRST_LOADS))
            stages = [
                lambda: act.activation(silu_cc[:, :, :], v("c", 0, 2 * DC).rearrange("p (k c) -> p k c", c=2),
                                       ACT.Silu).then_inc(silu_done.sem, 1),
                lambda: act_ffn(act, step, 0, 0, TOK),
                lambda: (act_a_qkv(act, step), act_lambda(act, step)),
                lambda: act_a_attend(act, step),
                lambda: act_a_out(act, step),
                lambda: act_ffn(act, step, 0, 2, TOK),
                lambda: None,
                lambda: act_ffn(act, step, 1, 0, TOK),
                lambda: act_b_qkv(act, step),
                lambda: act_b_attend(act, step),
                lambda: None,
                lambda: act_ffn(act, step, 1, 2, LAT),
                lambda: dma_bias(act),
            ]
            for l in range(2):
                stages += [
                    lambda l=l: act_rwkv_in(act, step, l),
                    lambda l=l: act_rwkv_core(act, step, l),
                    lambda l=l: act_rwkv_out(act, step, l),
                    lambda l=l: act_nsa_in(act, step, l),
                    lambda: act_nsa_cmp(act, step),
                    lambda: act_rel(act, step, 2, None),
                    lambda: None,
                    lambda l=l: act_rel(act, step, 1, lambda h: v("swa_sink", l * 8 + h)),
                    lambda: act_merge(act, step),
                    lambda l=l: act_peer(act, step, l),
                    lambda: None,
                ]
            stages.append(lambda: act_norm(act, step, LAT, gained(act, "lnf", 0)))
            for n, s in enumerate(stages):
                if want(n):
                    s()
                    end_phase(act)

        @block.vector
        def _(dve):
            step = Stepper(dve, dve_chain)
            dve.wait_ge(loaded.sem, loaded.due(dve, FIRST_LOADS))

            def b_out():
                for m in range(DC):
                    dve.wait_ge(D_.full, D_.filled())
                    dve_residual(dve, D_.take(), m, 1, 1, LAT)

            stages = [
                lambda: dve_ada(dve, step, 0),
                lambda: dve_ffn(dve, step, 0, 0, TOK),
                lambda: dve_a_qkv(dve, step),
                lambda: dve_a_attend(dve, step),
                lambda: dve_a_out(dve, step),
                lambda: dve_ffn(dve, step, 0, 2, TOK),
                lambda: dve_ada(dve, step, 1),
                lambda: dve_ffn(dve, step, 1, 0, TOK),
                lambda: dve_b_qkv(dve, step),
                lambda: dve_b_attend(dve, step),
                lambda: b_out(),
                lambda: dve_ffn(dve, step, 1, 2, LAT),
                lambda: dve_bias(dve, step),
            ]
            for l in range(2):
                stages += [
                    lambda l=l: dve_rwkv_in(dve, step, l),
                    lambda l=l: dve_rwkv_core(dve, step, l),
                    lambda l=l: dve_rwkv_out(dve, step, l),
                    lambda l=l: dve_nsa_in(dve, step, l),
                    lambda: dve_nsa_cmp(dve, step),
                    lambda: dve_rel(dve, step, 2, 0, None, True, ob),
                    lambda l=l: dve_swa_in(dve, step, l),
                    lambda l=l: dve_rel(dve, step, 1, 8, lambda h: v("swa_sink", l * 8 + h), False, oc),
                    lambda: dve_merge(dve, step),
                    lambda l=l: dve_peer(dve, step, l, l * len(GATHERS)),
                    lambda: dve_peer_out(dve, step),
                ]
            stages.append(lambda: dve_norm(dve, LAT))
            for n, s in enumerate(stages):
                if want(n):
                    s()
                    end_phase(dve)

        @block.gpsimd
        def _(pool):
            step = Stepper(pool, pool_chain)
            for n in range(N_STAGES):
                if want(n):
                    for l in range(2):
                        if n == GATHER_STAGE + l * 11:
                            pool_peer(pool, l * len(GATHERS))
                    end_phase(pool)

        @block.sync
        def _(sp):
            sp.dma_start(vec[:, :], vecs).then_inc(loaded.sem, 16)
            sp.dma_start(cst[:, :], consts).then_inc(loaded.sem, 16)
            sp.dma_start(xT[:, :, :], tokens).then_inc(loaded.sem, 16)
            for n in range(last_tile[0]):
                if n >= W_SLOTS:
                    sp.wait_ge(w_free, n - W_SLOTS + 1)
                sp.dma_start(wt[:, n % W_SLOTS, :], wstream[n]).then_inc(w_full[n % W_SLOTS], 16)
            sp.wait_ge(phase_done, 4 * max(phases.values()))
            sp.dma_start(out, hT[:, :, 0:LAT] if until > 34 else xT[:, :, 0:LAT]).then_inc(out_done.sem, 16)
            sp.wait_ge(out_done.sem, 16)


def pack(inputs):
    def rows(a):
        return np.asarray(a, np.float32).reshape(-1, P).T

    def twice(a):
        return np.tile(np.asarray(a, np.float32).reshape(1, HD), 2).reshape(P, 1)

    def wide(a):
        a = np.asarray(a, np.float32).reshape(1, -1)
        return np.broadcast_to(a, (P, a.shape[1]))

    g = inputs
    vecs = np.zeros((P, N_VEC), np.float32)

    def put(name, a):
        at, w = VEC_AT[name]
        vecs[:, at:at + w] = a.reshape(P, w)

    put("c", np.stack([rows(g["c"]), rows(g["c_ctx"])], 2))
    put("ada_b", rows(g["ada_b"]))
    put("a_q_gain", twice(g["a_q_gain"]))
    put("a_k_gain", twice(g["a_k_gain"]))
    put("a_subln", rows(g["a_subln_gain"]))
    put("b_q_gain", twice(g["b_q_gain"]))
    put("b_k_gain", twice(g["b_k_gain"]))
    for name, key in (("ln1", "ln1_w_2"), ("ln2", "ln2_w_2"), ("lnf", "lnf_w_2"), ("mu", "rwkv_mu_2"),
                      ("w0", "rwkv_w0_2"), ("a0", "rwkv_a0_2"), ("k_k", "rwkv_k_k_2"), ("k_a", "rwkv_k_a_2"),
                      ("r_k", "rwkv_r_k_2"), ("ln_w", "rwkv_ln_w_2"), ("ln_b", "rwkv_ln_b_2")):
        put(name, rows(g[key]))
    for name, key in (("pe_k", "nsa_pe_k_2"), ("pe_v", "nsa_pe_v_2")):
        put(name, np.asarray(g[key]).reshape(2, 16, P).transpose(2, 0, 1))
    put("b_sink", wide(g["b_sink"]))
    put("swa_sink", wide(g["swa_sinks_2"]))
    put("lambda", wide(g["a_lambda"]))
    rel = np.zeros((P, 16), np.float32)
    rel[:32] = g["rel_bias_2"]
    rel[32] = 1
    put("rel", rel)

    arrays = {k.removesuffix("_2"): np.asarray(a) for k, a in g.items()
              if k.removesuffix("_2") in {e[0] for e in PLAN if isinstance(e, tuple)}}
    for k in ("a_w_qkv", "a_w_o", "b_w_qkv", "b_w_o"):
        assert arrays[k].shape[0] == 1
    arrays["rwkv_wa"] = np.concatenate([np.asarray(g["rwkv_w2_2"]), np.asarray(g["rwkv_a2_2"])], 1)
    arrays["peer_subkeys"] = np.asarray(g["peer_subkeys_2"]).transpose(0, 4, 1, 2, 3).reshape(2, P, -1)
    w = np.zeros((W_TILES, P, W_TILE * P), np.float32)
    for n, e in enumerate(PLAN):
        if isinstance(e, tuple):
            name, l, r, c, width = e
            b = arrays[name][l, r:r + P, c:c + width * P]
            t, at = divmod(n, W_TILE)
            w[t, :, at * P:at * P + b.shape[1]] = b
    tok = np.concatenate([np.asarray(g["x"])[0], np.asarray(g["ctx"])[0]], 0)
    tokens = np.ascontiguousarray(tok.T.reshape(DC, P, TOK).transpose(1, 0, 2))
    c, oh = constants()
    return {
        "wstream": w, "vecs": vecs, "consts": c, "onehots": oh, "tokens": tokens,
        "peer_u": np.ascontiguousarray(g["peer_u_2"]).reshape(2 * EXPERTS, D),
        "peer_v": np.ascontiguousarray(g["peer_v_2"]).reshape(2 * EXPERTS, D),
    }


def kernel(**inputs):
    import concourse.bacc as bacc
    from concourse.bass_utils import run_bass_kernel_spmd

    nc = bacc.Bacc("TRN2", target_bir_lowering=False, num_devices=1)
    arrays = pack(inputs)
    aps = [nc.dram_tensor(name, a.shape, mybir.dt.from_np(a.dtype), kind="ExternalInput").ap()
           for name, a in arrays.items()]
    out = nc.dram_tensor("out", (P, DC, LAT), F32, kind="ExternalOutput").ap()
    model_kernel(nc, *aps, out)
    r = run_bass_kernel_spmd(nc, [arrays], core_ids=[0])
    got = r.results[0]["out"]
    return got.transpose(2, 1, 0).reshape(1, LAT, D)
```

```python
import math
from contextlib import ExitStack

import numpy as np
import concourse.bass as bass
from concourse import mybir

P = 128
F32 = mybir.dt.float32
F32R = mybir.dt.float32r
U32 = mybir.dt.uint32
I32 = mybir.dt.int32
ALU = mybir.AluOpType
ACT = mybir.ActivationFunctionType
AX = mybir.AxisListType.X

D = 1024
DC = D // P
LAT, CTX = 256, 256
TOK = LAT + CTX
FF = 2816
FC = FF // P
NMOD = 9
EPS = 1e-6
HD = 64
SCALE = HD ** -0.5
NEG = -1e30
A_HEADS = 8
LAM_INIT = 0.8 - 0.6 * math.exp(0.0)
B_HEADS, B_KV = 16, 4
B_WINDOW = 128
RW = 512
RC = RW // P
CH = 64
GN_EPS = 64e-5
DECAY = -math.exp(-0.5)
N_CMP, CMP_LEN, CMP_STRIDE = 15, 32, 16
PEER_H, PEER_K, NKEYS = 8, 16, 128
EXPERTS = NKEYS * NKEYS
SLOTS = PEER_H * PEER_K
QT = LAT // P
W_TILE = 16
W_SLOTS = 5
GROUP = W_TILE // 2
SPLITS = 4
HALF = FC // 2
HALF_GROUPS = HALF * (2 * DC + DC) // GROUP
GATED_GROUPS = 2 * HALF * DC // GROUP
assert GROUP == DC

IN = dict(rw=0, nq=1792, nkc=2304, nvc=2432, nks=2560, nvs=2688, nkw=2816, nvw=2944, ngate=3072,
          sq=3096, sk=3608, sv=3736, gates=3864)


def weight_plan():
    plan = []

    def add(name, layer, row, col, width=1):
        if len(plan) % W_TILE + width > W_TILE:
            while len(plan) % W_TILE:
                plan.append(None)
        plan.append((name, layer, row, col, width))
        plan.extend(["+"] * (width - 1))

    def align():
        while len(plan) % W_TILE:
            plan.append(None)

    def ffn(which, layer):
        align()
        for part in range(0, FC, HALF):
            for j in range(part, part + HALF):
                for half in range(2):
                    for k in range(DC):
                        add(f"ffn_{which}_wi", layer, k * P, half * FF + j * P)
            for m in range(DC):
                for f in range(part, part + HALF):
                    add(f"ffn_{which}_wo", layer, f * P, m * P)

    def square(name, layer, cols, rows=D):
        for c in cols:
            for k in range(rows // P):
                add(name, layer, k * P, c)

    def ada(layer):
        for c in range(0, NMOD * D, 4 * 512):
            for k in range(DC):
                for q in range(c, min(c + 4 * 512, NMOD * D), 512):
                    add("ada_w", layer, k * P, q, 4)

    ada(0)
    ffn("pre", 0)
    align()
    square("a_w_qkv", 0, range(0, 2 * D, P))
    for half in range(2):
        for k in range(DC):
            add("a_w_qkv", 0, k * P, 2 * D + half * 512, 4)
    align()
    square("a_w_o", 0, range(0, D, P))
    ffn("post", 0)
    ada(1)
    ffn("pre", 1)
    align()
    square("b_w_qkv", 0, range(0, D + 256, P))
    for k in range(DC):
        add("b_w_qkv", 0, k * P, D + 256, 2)
    align()
    square("b_w_o", 0, range(0, D, P))
    ffn("post", 1)
    align()
    for l in range(2):
        square("w_in", l, range(0, IN["nq"], P))
        add("rwkv_wa", l, 0, 0, 4)
        add("rwkv_g2", l, 0, 0, 4)
        square("w_in", l, [*range(IN["nq"], IN["nvs"], P), IN["nkw"]])
        for c, width in ((IN["nvs"], 1), (IN["nvw"], 2)):
            for k in range(DC):
                add("w_in", l, k * P, c, width)
        for name in ("nsa_ck", "nsa_cv"):
            for h in range(2):
                for k in range(16):
                    add(name + "_w1", l, k * P, h * P)
            for k in range(2):
                add(name + "_w2", l, k * P, 0)
        square("w_in", l, range(IN["sq"], IN["sv"], P))
        square("w_in", l, [IN["sv"]])
        align()
        for m in range(DC):
            for i, name in enumerate(("w_br_a", "w_br_b", "w_br_c")):
                square("w_in", l, [IN["gates"] + i * D + m * P])
                square(name, l, [m * P], RW)
        square("w_out", l, range(0, D, P))
        for i in range(2 * PEER_H):
            square("peer_wq", l, [i * P])
            add("peer_subkeys", l, 0, i * P)
    while len(plan) % W_TILE:
        plan.append(None)
    return plan


PLAN = weight_plan()
W_TILES = len(PLAN) // W_TILE


def columns(widths):
    at, out = 0, {}
    for name, w in widths:
        out[name] = (at, w)
        at += w
    return out, at


VEC_AT, N_VEC = columns([
    ("c", DC * 2), ("ada_b", 2 * NMOD * DC), ("a_q_gain", 1), ("a_k_gain", 1), ("a_subln", 1), ("b_q_gain", 1),
    ("b_k_gain", 1), ("ln1", 2 * DC), ("ln2", 2 * DC), ("lnf", DC), ("mu", 2 * 14), ("w0", 2 * RC), ("a0", 2 * RC),
    ("k_k", 2 * RC), ("k_a", 2 * RC), ("r_k", 2 * RC), ("ln_w", 2 * RC), ("ln_b", 2 * RC), ("pe_k", 2 * 16),
    ("pe_v", 2 * 16), ("b_sink", B_HEADS), ("swa_sink", 2 * 8), ("lambda", 4 * HD), ("rel", 16)])
LEVELS = 6
CONST_AT, N_CONST = columns([
    ("ident", P), ("ones", P), ("bones", P), ("rot", P), ("sel", 2 * P), ("cos", LAT), ("sin", LAT),
    ("level", LEVELS * P), ("before", P), ("upto", P), ("window", QT * TOK), ("cmp", QT * N_CMP),
    ("iota", PEER_K), ("carry", LAT), ("flip", P), ("eps", 1), ("gn_eps", 1)])
OH = 512
OH_AT, N_OH = columns([("nsa", OH), ("swa", OH)])


def t5_bucket(dist):
    n = np.maximum(dist, 0)
    nf = np.maximum(n, 16).astype(np.float32)
    large = 16 + (np.log(nf / 16) / math.log(128 / 16) * 16).astype(np.int32)
    return np.where(n < 16, n, np.minimum(large, 31))


def constants():
    c = np.zeros((P, N_CONST), np.float32)

    def put(name, a):
        at, w = CONST_AT[name]
        c[:, at:at + w] = np.asarray(a, np.float32).reshape(P, w)

    i, j = np.arange(P)[:, None], np.arange(P)[None, :]
    put("ident", i == j)
    put("ones", np.ones((P, P)))
    put("bones", i // HD == j // HD)
    rot = np.zeros((P, P))
    for m in range(P):
        if m % 32 < 16:
            rot[m + 16, m] = -1
        else:
            rot[m - 16, m] = 1
    put("rot", rot)
    put("sel", np.stack([(i == g * HD + j % HD) for g in range(2)], 1))
    inv = (10000.0 ** (-np.arange(16, dtype=np.float32) / 16)).astype(np.float32)
    t = np.arange(LAT)
    pos = np.stack([t // 64, t % 64]).astype(np.float32)
    d = np.arange(P) % HD
    ang = (pos[(d // 32)][:, :] * inv[d % 16][:, None]).astype(np.float32)
    put("cos", np.cos(ang))
    put("sin", np.sin(ang))
    put("level", np.stack([(i // (2 << k) == j // (2 << k)) & (i % (2 << k) < (1 << k)) & (j % (2 << k) >= (1 << k))
                           for k in range(LEVELS)], 1))
    put("before", (i // CH == j // CH) & (i < j))
    put("upto", (i // CH == j // CH) & (i <= j))
    w = np.zeros((P, QT, TOK))
    for q in range(QT):
        w[:, q, :LAT] = np.where(np.abs(np.arange(LAT)[None, :] - (q * P + i)) <= B_WINDOW, 0, NEG)
    put("window", w)
    end = np.arange(N_CMP) * CMP_STRIDE + CMP_LEN - 1
    put("cmp", np.stack([np.where(end[None, :] <= q * P + i, 0, NEG) for q in range(QT)], 1))
    put("iota", np.tile(np.arange(PEER_K), (P, 1)))
    put("carry", np.tile(np.arange(LAT) % CH != 0, (P, 1)))
    put("flip", i + j == P - 1)
    put("eps", np.full((P, 1), EPS))
    put("gn_eps", np.full((P, 1), GN_EPS))
    oh = np.zeros((33, 2, OH), np.float32)
    dist = 255 - np.arange(OH)
    for n, last in enumerate((256, 128)):
        oh[t5_bucket(dist), n, np.arange(OH)] = 1
        oh[32, n] = np.where((dist >= 0) & (dist < last), 0, NEG)
    return c, oh.reshape(33, N_OH)


ARENA = 28672


class Signal:

    def __init__(self, sem, unit=1):
        self.sem, self.unit, self.seen = sem, unit, {}

    def due(self, eng, n=1):
        self.seen[id(eng)] = self.seen.get(id(eng), 0) + n
        return self.unit * self.seen[id(eng)]


class Ring:

    def __init__(self, full, free, bufs):
        self.full, self.free, self.bufs = full, free, bufs
        self.claimed, self.taken = 0, 0

    def given_back(self, n=1):
        return max(self.claimed + n - len(self.bufs), 0)

    def filled(self, n=1):
        return self.taken + n

    def claim(self):
        self.claimed += 1
        return self.bufs[(self.claimed - 1) % len(self.bufs)]

    def take(self):
        self.taken += 1
        return self.bufs[(self.taken - 1) % len(self.bufs)]


def model_kernel(nc, wstream, vecs, consts, onehots, tokens, peer_u, peer_v, out):
    ctx = ExitStack()
    with ctx:
        def sem(name):
            return ctx.enter_context(nc.semaphore(name))

        def sb(name, shape, dt=F32):
            return ctx.enter_context(nc.sbuf_tensor(name, shape, dt))

        def signal(name, unit=1):
            return Signal(sem(name), unit)

        def ring(name, bufs):
            return Ring(sem(name + "_full"), sem(name + "_free"), bufs)

        xT = sb("xT", [P, DC, TOK])
        hT = sb("hT", [P, DC, TOK])
        wt = sb("wt", [P, W_SLOTS, W_TILE * P])
        cst = sb("cst", [P, N_CONST])
        vec = sb("vec", [P, N_VEC])
        mod = sb("mod", [P, 2, NMOD * DC, 2])
        silu_cc = sb("silu_cc", [P, DC, 2])
        rstd = sb("rstd", [P, TOK])
        small = sb("small", [P, 64])
        mini = sb("mini", [P, 784])
        with ExitStack() as split:
            def part(name, *shape):
                return split.enter_context(nc.sbuf_tensor(name, [P, *shape], F32R))

            h_hi, h_lo = part("h_hi", DC, TOK), part("h_lo", DC, TOK)
            w_hi, w_lo = part("w_hi", SPLITS, GROUP * P), part("w_lo", SPLITS, GROUP * P)
            hid_hi, hid_lo = part("hid_hi", HALF, TOK), part("hid_lo", HALF, TOK)
        with ExitStack() as split:
            part("under_bias", 16 * 3 * P)
            merged_hi = part("merged_hi", DC, LAT)
            part("under_w", 2 * SPLITS * GROUP * P)
            z_hi, z_lo = part("z_hi", DC, LAT), part("z_lo", DC, LAT)
            o_hi, o_lo = part("o_hi", 3 * RC, LAT), part("o_lo", 3 * RC, LAT)
            merged_lo = part("merged_lo", DC, LAT)
        arena = sb("arena", [P, ARENA])
        ps = ctx.enter_context(nc.psum_tensor("ps", [P, 8, 512], F32))

        def const(name, i=0, w=None):
            at, width = CONST_AT[name]
            w = w or width
            return cst[:, at + i * w:at + (i + 1) * w]

        def v(name, i=0, w=1):
            at = VEC_AT[name][0] + i
            return vec[:, at:at + w]

        ident, ones, bones = const("ident"), const("ones"), const("bones")
        eps = const("eps")

        class Carve:

            def __init__(self, at=0):
                self.at = at

            def __call__(self, *shape):
                n = int(np.prod(shape))
                a = arena[:, self.at:self.at + n]
                self.at += n
                assert self.at <= ARENA, self.at
                if len(shape) == 1:
                    return a
                names = "abcd"[:len(shape)]
                return a.rearrange(f"p ({' '.join(names)}) -> p {' '.join(names)}",
                                   **dict(zip(names[1:], shape[1:])))

        scratch = nc.dram_tensor("bias_by_distance", (16, OH), F32, kind="Internal").ap()

        loaded = signal("loaded", 16)
        w_full = [sem(f"w_full{i}") for i in range(W_SLOTS)]
        w_free = sem("w_free")
        phase_done = sem("phase_done")
        silu_done = signal("silu_done")
        sq_ready = signal("sq_ready")
        rstd_ready = signal("rstd_ready")
        xn_ready = signal("xn_ready")
        h_ready = signal("h_ready")
        hid_ready = signal("hid_ready")
        act_chain, dve_chain, pool_chain = sem("act_chain"), sem("dve_chain"), sem("pool_chain")
        D_ = ring("psd", [ps[:, i, :] for i in range(4)])
        A_ = ring("psa", [ps[:, 4 + i, :] for i in range(4)])

        phases = {}

        def end_phase(eng):
            n = phases[id(eng)] = phases.get(id(eng), 0) + 1
            eng.drain().then_inc(phase_done, 1)
            eng.wait_ge(phase_done, 4 * n)

        class Stepper:

            def __init__(self, eng, chain):
                self.eng, self.chain, self.n = eng, chain, 0

            def __call__(self, ins):
                self.n += 1
                ins.then_inc(self.chain, 1)
                self.eng.wait_ge(self.chain, self.n)

        class Weights:

            def __init__(self, pe):
                self.pe, self.at, self.owed, self.tile = pe, 0, 0, None

            def next(self, *key, width=1):
                while PLAN[self.at] in (None, "+"):
                    self.at += 1
                assert PLAN[self.at] == (*key, width), (PLAN[self.at], key, width)
                tile, b = divmod(self.at, W_TILE)
                if self.tile != tile:
                    self.pe.wait_ge(w_full[tile % W_SLOTS], 16 * (tile // W_SLOTS + 1))
                    if self.tile is not None:
                        self.owed += 1
                    self.tile = tile
                self.at += 1
                return wt[:, tile % W_SLOTS, b * P:(b + width) * P]

            def close(self):
                if self.tile is not None:
                    self.pe.drain()
                    self.pe.sem_inc(w_free, self.owed + 1)
                    self.owed, self.tile = 0, None

        def make_mm(pe, W):
            def mm(o, lhsT, rhs, start=True, stop=True, inc=None, **kw):
                ins = pe.matmul(o, lhsT, rhs, start=start, stop=stop, **kw)
                if inc is not None:
                    ins.then_inc(inc, 1)
                elif W.owed and not start:
                    ins.then_inc(w_free, 1)
                    W.owed -= 1
                return ins
            return mm

        def pe_project(pe, W, mm, name, l, cols, T, ring_of, src, parts_ready=False):
            for n, c in enumerate(cols):
                r = ring_of(n)
                pe.wait_ge(r.free, r.given_back())
                bank = r.claim()
                for k in range(DC):
                    if parts_ready and n == 0:
                        pe.wait_ge(h_ready.sem, h_ready.due(pe))
                    mm(bank[:, 0:T], W.next(name, l, k * P, c), src[:, k, 0:T], k == 0, k == DC - 1,
                       r.full if k == DC - 1 else None)

        def pe_norm(pe, mm, T):
            pe.wait_ge(A_.free, A_.given_back())
            bank = A_.claim()
            for k in range(DC):
                pe.wait_ge(sq_ready.sem, sq_ready.due(pe))
                mm(bank[:, 0:T], ones, hT[:, k, 0:T], k == 0, k == DC - 1, A_.full if k == DC - 1 else None)

        def act_rsqrt(act, step, out_, in_, scale, bias):
            step(act.activation(out_, in_, ACT.Ln, bias=bias, scale=scale))
            step(act.activation(out_, out_, ACT.Exp, scale=-0.5))

        def act_norm(act, step, T, affine):
            for k in range(DC):
                act.activation(hT[:, k, 0:T], xT[:, k, 0:T], ACT.Square).then_inc(sq_ready.sem, 1)
            act.wait_ge(A_.full, A_.filled())
            bank = A_.take()
            act_rsqrt(act, step, rstd[:, 0:T], bank[:, 0:T], 1.0 / D, eps)
            act.sem_inc(A_.free, 1)
            act.sem_inc(rstd_ready.sem, 1)
            for k in range(DC):
                act.wait_ge(xn_ready.sem, xn_ready.due(act))
                affine(k)

        def dve_norm(dve, T):
            dve.wait_ge(rstd_ready.sem, rstd_ready.due(dve))
            for k in range(DC):
                dve.tensor_tensor(hT[:, k, 0:T], xT[:, k, 0:T], rstd[:, 0:T], ALU.mult).then_inc(xn_ready.sem, 1)

        def modulated(act, l, which, T):
            def affine(k):
                modulate(act, l, which, T, k).then_inc(h_ready.sem, 1)
            return affine

        def modulate(act, l, which, T, k):
            for r in range(T // LAT):
                seg = hT[:, k, r * LAT:(r + 1) * LAT]
                ins = act.activation(seg, seg, ACT.Identity, bias=mod[:, l, 3 * which * DC + k, r:r + 1],
                                     scale=mod[:, l, (3 * which + 1) * DC + k, r:r + 1])
            return ins

        def dve_residual(dve, bank, m, l, which, T):
            for r in range(T // LAT):
                seg = xT[:, m, r * LAT:(r + 1) * LAT]
                ins = dve.scalar_tensor_tensor(out=seg, in0=bank[:, r * LAT:(r + 1) * LAT],
                                               scalar=mod[:, l, (3 * which + 2) * DC + m, r:r + 1], in1=seg,
                                               op0=ALU.mult, op1=ALU.add)
            ins.then_inc(D_.free, 1)

        arow = Carve()(NMOD * D)
        arow_ready = signal("arow_ready")

        def pe_ada(pe, W, mm, l):
            if l == 0:
                pe.wait_ge(silu_done.sem, silu_done.due(pe))
            for c in range(0, NMOD * D, 4 * 512):
                cols = range(c, min(c + 4 * 512, NMOD * D), 512)
                pe.wait_ge(D_.free, D_.given_back())
                bank = D_.claim()
                for k in range(DC):
                    for i, q in enumerate(cols):
                        last = k == DC - 1 and i == len(cols) - 1
                        mm(bank[32 * i:32 * i + 2, :], silu_cc[:, k, :], W.next("ada_w", l, k * P, q, width=4),
                           k == 0, k == DC - 1, D_.full if last else None)
            pe.wait_ge(arow_ready.sem, arow_ready.due(pe))
            pe.wait_ge(D_.free, D_.given_back())
            bank = D_.claim()
            for j in range(NMOD * DC):
                ins = pe.transpose(bank[:, 2 * j:2 * j + 2], arow[0:2, j * P:(j + 1) * P], ident[0:2, 0:2])
            ins.then_inc(D_.full, 1)

        def dve_ada(dve, step, l):
            for c in range(0, NMOD * D, 4 * 512):
                dve.wait_ge(D_.full, D_.filled())
                bank = D_.take()
                for i, q in enumerate(range(c, min(c + 4 * 512, NMOD * D), 512)):
                    step(dve.tensor_copy(arow[0:2, q:q + 512], bank[32 * i:32 * i + 2, :]))
                dve.sem_inc(D_.free, 1)
            dve.sem_inc(arow_ready.sem, 1)
            dve.wait_ge(D_.full, D_.filled())
            bank = D_.take()
            n = NMOD * DC
            bias = v("ada_b", l * n, n).unsqueeze(2).to_broadcast([P, n, 2])
            step(dve.tensor_tensor(mod[:, l], bank[:, 0:2 * n].rearrange("p (n c) -> p n c", c=2), bias, ALU.add))
            dve.sem_inc(D_.free, 1)
            for i in (1, 4, 7):
                a = mod[:, l, i * DC:(i + 1) * DC, :]
                step(dve.tensor_scalar(a, a, 1.0, None, ALU.add))
            for i in (2, 8):
                a = mod[:, l, i * DC:(i + 1) * DC, :]
                step(dve.tensor_scalar(a, a, 0.5, None, ALU.mult))

        SPLIT_END = 2 * DC * TOK + 2 * SPLITS * GROUP * P
        split_ring = ring("split", [(w_hi[:, i], w_lo[:, i]) for i in range(SPLITS)])
        w_hi_ready = signal("w_hi_ready")
        h_hi_ready = signal("h_hi_ready")
        raw_ready = signal("raw_ready")

        def groups_of(name, layer, cols, col=0):
            first = PLAN.index((name, layer, 0, col, 1))
            assert first % W_TILE == 0
            return range(first // GROUP, first // GROUP + cols // P * DC // GROUP)

        def raw_group(g):
            return wt[:, (g // 2) % W_SLOTS, (g % 2) * GROUP * P:(g % 2 + 1) * GROUP * P]

        class SplitHi:

            def __init__(self, act, groups):
                self.act, self.left = act, list(groups)
                for _ in range(SPLITS):
                    self.ahead()

            def ahead(self):
                if self.left:
                    g = self.left.pop(0)
                    self.act.wait_ge(w_full[(g // 2) % W_SLOTS], 16 * (g // 2 // W_SLOTS + 1))
                    self.act.wait_ge(split_ring.free, split_ring.given_back())
                    hi, _ = split_ring.claim()
                    self.act.activation(hi, raw_group(g), ACT.Copy).then_inc(w_hi_ready.sem, 1)

        split_done = [0]

        class SplitLo:

            def __init__(self, dve, step, groups):
                self.dve, self.step, self.left = dve, step, list(groups)
                for _ in range(SPLITS):
                    self.ahead()

            def ahead(self):
                if self.left:
                    g = self.left.pop(0)
                    self.dve.wait_ge(w_hi_ready.sem, w_hi_ready.due(self.dve))
                    hi, lo = split_ring.bufs[split_done[0] % SPLITS]
                    split_done[0] += 1
                    self.step(self.dve.tensor_tensor(lo, raw_group(g), hi.bitcast(F32), ALU.subtract))
                    self.dve.sem_inc(split_ring.full, 1)
                    if g % 2:
                        self.dve.sem_inc(w_free, 1)

        class SplitWeights:

            def __init__(self, pe, W):
                self.pe, self.W, self.group, self.owed = pe, W, None, 0

            def next(self, *key, width=1):
                W = self.W
                while PLAN[W.at] in (None, "+"):
                    W.at += 1
                assert PLAN[W.at] == (*key, width), (PLAN[W.at], key)
                group, b = divmod(W.at, GROUP)
                if self.group != group:
                    self.pe.wait_ge(split_ring.full, split_ring.filled())
                    self.bufs = split_ring.take()
                    if self.group is not None:
                        self.owed += 1
                    self.group = group
                W.at += 1
                return [w[:, b * P:(b + width) * P] for w in self.bufs]

            def mm(self, o, pairs, start, stop, inc):
                for i, (a, b) in enumerate(pairs):
                    ins = self.pe.matmul(o, a, b, start=start and i == 0, stop=stop and i == 2)
                if inc is not None:
                    ins.then_inc(inc, 1)
                elif self.owed and not start:
                    ins.then_inc(split_ring.free, 1)
                    self.owed -= 1

            def close(self):
                self.pe.drain()
                self.pe.sem_inc(split_ring.free, self.owed + 1)

        def three(a, b):
            return (a[0], b[0]), (a[0], b[1]), (a[1], b[0])

        def h_parts(k, t0, t1):
            return h_hi[:, k, t0:t1], h_lo[:, k, t0:t1]

        def pe_split_project(pe, SW, name, cols, T, r, parts_ready):
            for c in cols:
                pe.wait_ge(r.free, r.given_back())
                bank = r.claim()
                for k in range(DC):
                    if parts_ready and c == cols[0]:
                        pe.wait_ge(h_ready.sem, h_ready.due(pe))
                    SW.mm(bank[:, 0:T], three(SW.next(name, 0, k * P, c), h_parts(k, 0, T)), k == 0, k == DC - 1,
                          r.full if k == DC - 1 else None)

        def act_split_norm(act, step, groups, l, sub, T):
            for k in range(DC):
                act.activation(hT[:, k, 0:T], xT[:, k, 0:T], ACT.Square).then_inc(sq_ready.sem, 1)
            weights = SplitHi(act, groups)
            act.wait_ge(A_.full, A_.filled())
            bank = A_.take()
            act_rsqrt(act, step, rstd[:, 0:T], bank[:, 0:T], 1.0 / D, eps)
            act.sem_inc(A_.free, 1)
            act.sem_inc(rstd_ready.sem, 1)
            for k in range(DC):
                act.wait_ge(xn_ready.sem, xn_ready.due(act))
                step(modulate(act, l, sub, T, k))
                act.activation(h_hi[:, k, 0:T], hT[:, k, 0:T], ACT.Copy).then_inc(h_hi_ready.sem, 1)
            return weights

        def dve_split_norm(dve, step, groups, T):
            weights = SplitLo(dve, step, groups)
            dve.wait_ge(rstd_ready.sem, rstd_ready.due(dve))
            for k in range(DC + 2):
                if k < DC:
                    dve.tensor_tensor(hT[:, k, 0:T], xT[:, k, 0:T], rstd[:, 0:T], ALU.mult).then_inc(xn_ready.sem, 1)
                if k >= 2:
                    dve.wait_ge(h_hi_ready.sem, h_hi_ready.due(dve))
                    dve.tensor_tensor(h_lo[:, k - 2, 0:T], hT[:, k - 2, 0:T], h_hi[:, k - 2, 0:T].bitcast(F32),
                                      ALU.subtract).then_inc(h_ready.sem, 1)
            return weights

        hid_hi_ready = signal("hid_hi_ready")
        silu_ring = ring("silu", [hT[:, i, :] for i in range(3)])
        hid_raw = hT[:, 3, :]

        def ffn_groups(which, l):
            return groups_of(f"ffn_{which}_wi", l, 3 * FF)

        def pe_ffn(pe, W, mm, which, l, T):
            SW = SplitWeights(pe, W)
            pe_norm(pe, mm, T)
            for part in range(0, FC, HALF):
                for j in range(part, part + HALF):
                    for half, r in ((0, A_), (1, D_)):
                        pe.wait_ge(r.free, r.given_back())
                        bank = r.claim()
                        for k in range(DC):
                            if j == 0 and half == 0:
                                pe.wait_ge(h_ready.sem, h_ready.due(pe))
                            w = SW.next(f"ffn_{which}_wi", l, k * P, half * FF + j * P)
                            SW.mm(bank[:, 0:T], three(w, h_parts(k, 0, T)), k == 0, k == DC - 1,
                                  r.full if k == DC - 1 else None)
                for m in range(DC):
                    pe.wait_ge(D_.free, D_.given_back())
                    bank = D_.claim()
                    for f in range(HALF):
                        if m == 0:
                            pe.wait_ge(hid_ready.sem, hid_ready.due(pe))
                        w = SW.next(f"ffn_{which}_wo", l, (part + f) * P, m * P)
                        SW.mm(bank[:, 0:T], three(w, (hid_hi[:, f, 0:T], hid_lo[:, f, 0:T])), f == 0, f == HALF - 1,
                              D_.full if f == HALF - 1 else None)
            SW.close()

        def act_ffn(act, step, which, l, sub, T):
            weights = act_split_norm(act, step, ffn_groups(which, l), l, sub, T)
            for g in range(2 * HALF_GROUPS):
                i = g % HALF_GROUPS
                if i < GATED_GROUPS and i % 2 == 0:
                    act.wait_ge(A_.full, A_.filled())
                    act.wait_ge(silu_ring.free, silu_ring.given_back())
                    bank, s = A_.take(), silu_ring.claim()
                    step(act.activation(s[:, 0:T], bank[:, 0:T], ACT.Silu))
                    act.sem_inc(A_.free, 1)
                    act.sem_inc(silu_ring.full, 1)
                weights.ahead()
                if i < GATED_GROUPS and i % 2:
                    act.wait_ge(raw_ready.sem, raw_ready.due(act))
                    act.activation(hid_hi[:, i // 2, 0:T], hid_raw[:, 0:T], ACT.Copy).then_inc(hid_hi_ready.sem, 1)

        def dve_ffn(dve, step, which, l, sub, T):
            weights = dve_split_norm(dve, step, ffn_groups(which, l), T)
            for g in range(2 * HALF_GROUPS):
                i = g % HALF_GROUPS
                if i < GATED_GROUPS and i % 2:
                    dve.wait_ge(silu_ring.full, silu_ring.filled())
                    dve.wait_ge(D_.full, D_.filled())
                    s, bank = silu_ring.take(), D_.take()
                    step(dve.tensor_tensor(hid_raw[:, 0:T], s[:, 0:T], bank[:, 0:T], ALU.mult))
                    dve.sem_inc(silu_ring.free, 1)
                    dve.sem_inc(D_.free, 1)
                    dve.sem_inc(raw_ready.sem, 1)
                weights.ahead()
                if i < GATED_GROUPS and i % 2:
                    dve.wait_ge(hid_hi_ready.sem, hid_hi_ready.due(dve))
                    step(dve.tensor_tensor(hid_lo[:, i // 2, 0:T], hid_raw[:, 0:T],
                                           hid_hi[:, i // 2, 0:T].bitcast(F32), ALU.subtract))
                    dve.sem_inc(hid_ready.sem, 1)
                for m in range(DC):
                    if ((m + 1) * HALF - 1) // GROUP == i - GATED_GROUPS:
                        dve.wait_ge(D_.full, D_.filled())
                        dve_residual(dve, D_.take(), m, l, sub, T)

        M = Carve(SPLIT_END)
        qT, kT = M(8, TOK), M(8, TOK)
        vA = M(4, D)
        oT = hT
        raw_ring = ring("raw", [hT[:, i, :] for i in (0, 1)])
        sqh_ring = ring("sqh", [hT[:, i, :] for i in (2, 3)])
        rs_ring = ring("rs", [hT[:, i, :] for i in (4, 5)])
        qn_ring = ring("qn", [hT[:, 6, i * LAT:(i + 1) * LAT] for i in range(2)])
        tmp_a, tmp_b = hT[:, 7, 0:LAT], hT[:, 7, LAT:TOK]
        O_ = Carve(SPLIT_END)
        sqo_ring = ring("sqo", [O_(TOK) for _ in range(2)])
        rso_ring = ring("rso", [O_(TOK) for _ in range(2)])

        def pe_heads(pe, SW, mm, name, cols):
            n = len(cols)
            for i in range(n + 2):
                if i < n:
                    pe_split_project(pe, SW, name, [cols[i]], TOK, A_, i == 0)
                if 1 <= i <= n:
                    pe.wait_ge(sqh_ring.full, sqh_ring.filled())
                    sq = sqh_ring.take()
                    pe.wait_ge(A_.free, A_.given_back())
                    mm(A_.claim(), bones, sq).then_inc(A_.full, 1)
                if i >= 2:
                    pe.wait_ge(qn_ring.full, qn_ring.filled())
                    qn = qn_ring.take()
                    pe.wait_ge(D_.free, D_.given_back())
                    mm(D_.claim()[:, 0:LAT], const("rot"), qn).then_inc(D_.full, 1)

        def act_heads(act, step, n, weights):
            for i in range(n + 1):
                if i < n:
                    act.wait_ge(A_.full, A_.filled())
                    bank = A_.take()
                    act.wait_ge(raw_ring.free, raw_ring.given_back())
                    act.wait_ge(sqh_ring.free, sqh_ring.given_back())
                    raw, sq = raw_ring.claim(), sqh_ring.claim()
                    act.activation(raw, bank, ACT.Copy).then_inc(raw_ring.full, 1)
                    step(act.activation(sq, bank, ACT.Square))
                    act.sem_inc(sqh_ring.full, 1)
                    act.sem_inc(A_.free, 1)
                if i >= 1:
                    act.wait_ge(A_.full, A_.filled())
                    bank = A_.take()
                    act.wait_ge(rs_ring.free, rs_ring.given_back())
                    r = rs_ring.claim()
                    act_rsqrt(act, step, r, bank, 1.0 / HD, eps)
                    act.sem_inc(sqh_ring.free, 1)
                    act.sem_inc(A_.free, 1)
                    act.sem_inc(rs_ring.full, 1)
                if i < n - 1:
                    weights.ahead()

        def dve_heads(dve, step, outs, gains, weights):
            n = len(outs)
            for i in range(n + 1):
                if i < n - 1:
                    weights.ahead()
                if i < n:
                    dve.wait_ge(raw_ring.full, raw_ring.filled())
                    dve.wait_ge(rs_ring.full, rs_ring.filled())
                    dve.wait_ge(qn_ring.free, qn_ring.given_back())
                    raw, r, qn = raw_ring.take(), rs_ring.take(), qn_ring.claim()
                    step(dve.scalar_tensor_tensor(out=outs[i][:, LAT:TOK], in0=raw[:, LAT:TOK], scalar=gains[i],
                                                  in1=r[:, LAT:TOK], op0=ALU.mult, op1=ALU.mult))
                    step(dve.scalar_tensor_tensor(out=qn, in0=raw[:, 0:LAT], scalar=gains[i],
                                                  in1=r[:, 0:LAT], op0=ALU.mult, op1=ALU.mult))
                    dve.sem_inc(raw_ring.free, 1)
                    dve.sem_inc(rs_ring.free, 1)
                    step(dve.tensor_tensor(outs[i][:, 0:LAT], qn, const("cos"), ALU.mult))
                    dve.sem_inc(qn_ring.full, 1)
                if i >= 1:
                    dve.wait_ge(D_.full, D_.filled())
                    bank = D_.take()
                    o = outs[i - 1][:, 0:LAT]
                    step(dve.tensor_tensor(tmp_a[:, 0:LAT], bank[:, 0:LAT], const("sin"), ALU.mult))
                    dve.sem_inc(qn_ring.free, 1)
                    dve.sem_inc(D_.free, 1)
                    step(dve.tensor_tensor(o, o, tmp_a[:, 0:LAT], ALU.add))

        def pe_a_qkv(pe, W, mm):
            SW = SplitWeights(pe, W)
            pe_norm(pe, mm, TOK)
            pe_heads(pe, SW, mm, "a_w_qkv", range(0, 2 * D, P))
            for half in range(2):
                pe.wait_ge(D_.free, D_.given_back(4))
                banks = [D_.claim() for _ in range(4)]
                for k in range(DC):
                    w = SW.next("a_w_qkv", 0, k * P, 2 * D + half * 512, width=4)
                    for t in range(4):
                        SW.mm(banks[t], three(h_parts(k, t * P, (t + 1) * P), w), k == 0, k == DC - 1,
                              D_.full if k == DC - 1 else None)
            SW.close()

        def act_a_qkv(act, step):
            weights = act_split_norm(act, step, groups_of("a_w_qkv", 0, 3 * D), 0, 1, TOK)
            act_heads(act, step, 16, weights)
            for _ in range(2 * DC // 2):
                weights.ahead()

        def dve_a_qkv(dve, step):
            weights = dve_split_norm(dve, step, groups_of("a_w_qkv", 0, 3 * D), TOK)
            dve_heads(dve, step, [qT[:, i] for i in range(8)] + [kT[:, i] for i in range(8)],
                      [v("a_q_gain")] * 8 + [v("a_k_gain")] * 8, weights)
            for half in range(2):
                for _ in range(DC // 2):
                    weights.ahead()
                for t in range(4):
                    dve.wait_ge(D_.full, D_.filled())
                    bank = D_.take()
                    dve.tensor_copy(vA[:, t, half * 512:(half + 1) * 512], bank).then_inc(D_.free, 1)
            prod = tmp_b[:, 0:2 * HD]
            lam4 = v("lambda", 0, 4 * HD).rearrange("p (a b d) -> p a b d", a=2, b=2)
            step(dve.tensor_tensor(prod.rearrange("p (a d) -> p a d", a=2), lam4[:, :, 0, :], lam4[:, :, 1, :], ALU.mult))
            step(dve.tensor_reduce(small[:, 2:4], prod.rearrange("p (a d) -> p a d", a=2), AX, ALU.add))
            dve.sem_inc(lam_sum.sem, 1)
            dve.wait_ge(lam_exp.sem, lam_exp.due(dve))
            step(dve.tensor_scalar(small[:, 0:1], small[:, 5:6], small[:, 4:5], -LAM_INIT, ALU.subtract, ALU.add))

        lam_sum, lam_exp = signal("lam_sum"), signal("lam_exp")

        def act_lambda(act, step):
            act.wait_ge(lam_sum.sem, lam_sum.due(act))
            step(act.activation(small[:, 4:6], small[:, 2:4], ACT.Exp))
            act.sem_inc(lam_exp.sem, 1)

        A_UNITS = [(h, q) for h in range(A_HEADS) for q in range(4)]
        U = Carve()
        p_bufs = [U(2, TOK) for _ in range(2)]
        a_ring = ring("aprob", [U(TOK) for _ in range(2)])
        t_ring = ring("at", [U(4, P) for _ in range(2)])
        nmax = U(8, 2)
        rsum = U(8, 2)
        assert U.at <= SPLIT_END
        s_pair = ring("spair", [ps[:, 0:2], ps[:, 2:4]])
        p_ring = ring("prob", p_bufs)
        nm_ready = signal("nm_ready")
        ot_ring = ring("ot", [ps[:, 6], ps[:, 7]])
        tpr = ring("tpr", [ps[:, 4], ps[:, 5]])

        def keys_of(q):
            return (0, TOK) if q < QT else (LAT, TOK)

        def pe_a_attend(pe, W, mm):
            n = len(A_UNITS)
            for i in range(n + 3):
                if i < n:
                    h, q = A_UNITS[i]
                    k0, k1 = keys_of(q)
                    pe.wait_ge(s_pair.free, s_pair.given_back())
                    s = s_pair.claim()
                    for c in range(2):
                        r = slice(c * HD, (c + 1) * HD)
                        mm(s[:, c, 0:k1 - k0], qT[r, h, q * P:(q + 1) * P], kT[r, h, k0:k1],
                           inc=s_pair.full if c else None)
                if 2 <= i < n + 2:
                    h, q = A_UNITS[i - 2]
                    k0, k1 = keys_of(q)
                    pe.wait_ge(a_ring.full, a_ring.filled())
                    pe.wait_ge(tpr.free, tpr.given_back())
                    a, t = a_ring.take(), tpr.claim()
                    for j in range((k1 - k0) // P):
                        ins = pe.transpose(t[:, j * P:(j + 1) * P], a[:, j * P:(j + 1) * P], ident)
                    ins.then_inc(tpr.full, 1)
                if i >= 3:
                    h, q = A_UNITS[i - 3]
                    k0, k1 = keys_of(q)
                    pe.wait_ge(t_ring.full, t_ring.filled())
                    pe.wait_ge(ot_ring.free, ot_ring.given_back())
                    t, o = t_ring.take(), ot_ring.claim()
                    nk = (k1 - k0) // P
                    for j in range(nk):
                        mm(o[:, 0:P], vA[:, k0 // P + j, h * P:(h + 1) * P], t[:, j, :], j == 0, j == nk - 1,
                           ot_ring.full if j == nk - 1 else None)

        def act_a_attend(act, step):
            n = len(A_UNITS)
            for i in range(n + 2):
                if i < n:
                    h, q = A_UNITS[i]
                    k0, k1 = keys_of(q)
                    w = k1 - k0
                    act.wait_ge(nm_ready.sem, nm_ready.due(act))
                    act.wait_ge(p_ring.free, p_ring.given_back())
                    p = p_ring.claim()
                    s = s_pair.bufs[i % 2]
                    for c in range(2):
                        step(act.activation(p[:, c, 0:w], s[:, c, 0:w], ACT.Exp, bias=nmax[:, i % 8, c:c + 1],
                                            scale=SCALE, accum_out=rsum[:, i % 8, c:c + 1]))
                    act.sem_inc(s_pair.free, 1)
                    act.sem_inc(p_ring.full, 1)
                if i >= 2:
                    h, q = A_UNITS[i - 2]
                    k0, k1 = keys_of(q)
                    w = k1 - k0
                    act.wait_ge(tpr.full, tpr.filled())
                    act.wait_ge(t_ring.free, t_ring.given_back())
                    tp, t = tpr.take(), t_ring.claim()
                    act.sem_inc(a_ring.free, 1)
                    step(act.activation(t[:, 0:w // P, :], tp[:, 0:w].rearrange("p (a b) -> p a b", b=P), ACT.Copy))
                    act.sem_inc(tpr.free, 1)
                    act.sem_inc(t_ring.full, 1)

        def dve_a_attend(dve, step):
            n = len(A_UNITS)
            for i in range(n + 4):
                if i < n:
                    h, q = A_UNITS[i]
                    k0, k1 = keys_of(q)
                    dve.wait_ge(s_pair.full, s_pair.filled())
                    s = s_pair.take()
                    step(dve.tensor_reduce(nmax[:, i % 8, :], s[:, :, 0:k1 - k0], AX, ALU.max))
                    step(dve.tensor_scalar(nmax[:, i % 8, :], nmax[:, i % 8, :], -SCALE, None, ALU.mult))
                    dve.sem_inc(nm_ready.sem, 1)
                if 1 <= i < n + 1:
                    j = i - 1
                    h, q = A_UNITS[j]
                    k0, k1 = keys_of(q)
                    w = k1 - k0
                    dve.wait_ge(p_ring.full, p_ring.filled())
                    p = p_ring.take()
                    dve.wait_ge(a_ring.free, a_ring.given_back())
                    a = a_ring.claim()
                    rs = rsum[:, j % 8, :]
                    step(dve.reciprocal(rs, rs))
                    step(dve.tensor_scalar(p[:, 1, 0:w], p[:, 1, 0:w], rs[:, 1:2], small[:, 0:1], ALU.mult, ALU.mult))
                    step(dve.scalar_tensor_tensor(out=a[:, 0:w], in0=p[:, 0, 0:w], scalar=rs[:, 0:1], in1=p[:, 1, 0:w],
                                                  op0=ALU.mult, op1=ALU.add))
                    dve.sem_inc(p_ring.free, 1)
                    dve.sem_inc(a_ring.full, 1)
                if i >= 4:
                    h, q = A_UNITS[i - 4]
                    dve.wait_ge(ot_ring.full, ot_ring.filled())
                    o = ot_ring.take()
                    step(dve.tensor_copy(oT[:, h, q * P:(q + 1) * P], o[:, 0:P]))
                    dve.sem_inc(ot_ring.free, 1)
                    dve.sem_inc(t_ring.free, 1)

        def pe_a_out(pe, W, mm):
            SW = SplitWeights(pe, W)
            for h in range(A_HEADS):
                pe.wait_ge(A_.free, A_.given_back())
                pe.wait_ge(sqo_ring.full, sqo_ring.filled())
                mm(A_.claim(), ones, sqo_ring.take()).then_inc(A_.full, 1)
            pe_split_project(pe, SW, "a_w_o", range(0, D, P), TOK, D_, True)
            SW.close()

        def act_a_out(act, step):
            weights = SplitHi(act, groups_of("a_w_o", 0, D))
            for h in range(A_HEADS + 2):
                if h < A_HEADS:
                    act.wait_ge(sqo_ring.free, sqo_ring.given_back())
                    sq = sqo_ring.claim()
                    step(act.activation(sq, oT[:, h, :], ACT.Square))
                    act.sem_inc(sqo_ring.full, 1)
                if 1 <= h < A_HEADS + 1:
                    act.wait_ge(A_.full, A_.filled())
                    act.wait_ge(rso_ring.free, rso_ring.given_back())
                    bank, r = A_.take(), rso_ring.claim()
                    act_rsqrt(act, step, r, bank, 1.0 / P, eps)
                    act.sem_inc(sqo_ring.free, 1)
                    act.sem_inc(A_.free, 1)
                    act.sem_inc(rso_ring.full, 1)
                if h >= 2:
                    act.wait_ge(raw_ready.sem, raw_ready.due(act))
                    act.activation(h_hi[:, h - 2, :], oT[:, h - 2, :], ACT.Copy).then_inc(h_hi_ready.sem, 1)
            for _ in range(DC):
                weights.ahead()

        def dve_a_out(dve, step):
            weights = SplitLo(dve, step, groups_of("a_w_o", 0, D))
            step(dve.tensor_scalar(small[:, 1:2], v("a_subln"), 1.0 - LAM_INIT, None, ALU.mult))
            for h in range(A_HEADS + 1):
                if h < A_HEADS:
                    dve.wait_ge(rso_ring.full, rso_ring.filled())
                    r = rso_ring.take()
                    step(dve.scalar_tensor_tensor(out=oT[:, h, :], in0=oT[:, h, :], scalar=small[:, 1:2], in1=r,
                                                  op0=ALU.mult, op1=ALU.mult))
                    dve.sem_inc(rso_ring.free, 1)
                    dve.sem_inc(raw_ready.sem, 1)
                if h >= 1:
                    dve.wait_ge(h_hi_ready.sem, h_hi_ready.due(dve))
                    dve.tensor_tensor(h_lo[:, h - 1, :], oT[:, h - 1, :], h_hi[:, h - 1, :].bitcast(F32),
                                      ALU.subtract).then_inc(h_ready.sem, 1)
            for m in range(DC):
                weights.ahead()
                dve.wait_ge(D_.full, D_.filled())
                dve_residual(dve, D_.take(), m, 0, 1, TOK)

        MB = Carve(SPLIT_END)
        qB = MB(8, TOK)
        kB = MB(2, TOK)
        kD = MB(B_KV, TOK)
        vB = MB(4, 256)
        oB = MB(8, LAT)
        N = Carve(U.at)
        sm_ring_b = ring("sm", [N(TOK) for _ in range(2)])
        pb_ring = ring("pb", [N(TOK) for _ in range(2)])
        sinkv = N(8, 4)
        B_UNITS = [(h, q) for h in range(B_HEADS) for q in range(QT)]

        def pe_b_qkv(pe, W, mm):
            SW = SplitWeights(pe, W)
            pe_norm(pe, mm, TOK)
            pe_heads(pe, SW, mm, "b_w_qkv", range(0, D + 256, P))
            pe.wait_ge(D_.free, D_.given_back(4))
            banks = [D_.claim() for _ in range(4)]
            for k in range(DC):
                w = SW.next("b_w_qkv", 0, k * P, D + 256, width=2)
                for t in range(4):
                    SW.mm(banks[t][:, 0:256], three(h_parts(k, t * P, (t + 1) * P), w), k == 0, k == DC - 1,
                          D_.full if k == DC - 1 else None)
            SW.close()
            pe.wait_ge(kb_ready.sem, kb_ready.due(pe))
            for g in range(B_KV):
                pe.wait_ge(D_.free, D_.given_back())
                mm(D_.claim(), const("sel", g % 2, P), kB[:, g // 2, :]).then_inc(D_.full, 1)

        kb_ready = signal("kb_ready")

        def dve_b_qkv(dve, step):
            weights = dve_split_norm(dve, step, groups_of("b_w_qkv", 0, D + 512), TOK)
            dve_heads(dve, step, [qB[:, i] for i in range(8)] + [kB[:, i] for i in range(2)],
                      [v("b_q_gain")] * 8 + [v("b_k_gain")] * 2, weights)
            dve.sem_inc(kb_ready.sem, 1)
            for t in range(4):
                dve.wait_ge(D_.full, D_.filled())
                bank = D_.take()
                dve.tensor_copy(vB[:, t, :], bank[:, 0:256]).then_inc(D_.free, 1)
            for g in range(B_KV):
                dve.wait_ge(D_.full, D_.filled())
                bank = D_.take()
                dve.tensor_copy(kD[:, g, :], bank).then_inc(D_.free, 1)

        def act_b_qkv(act, step):
            weights = act_split_norm(act, step, groups_of("b_w_qkv", 0, D + 512), 1, 1, TOK)
            act_heads(act, step, 10, weights)

        def pe_b_attend(pe, W, mm):
            n = len(B_UNITS)
            for i in range(n + 3):
                if i < n:
                    h, q = B_UNITS[i]
                    r = slice((h % 2) * HD, (h % 2 + 1) * HD)
                    pe.wait_ge(D_.free, D_.given_back())
                    mm(D_.claim(), qB[r, h // 2, q * P:(q + 1) * P], kD[r, h // 4, :]).then_inc(D_.full, 1)
                if 2 <= i < n + 2:
                    pe.wait_ge(a_ring.full, a_ring.filled())
                    pe.wait_ge(tpr.free, tpr.given_back())
                    a, t = a_ring.take(), tpr.claim()
                    for j in range(4):
                        ins = pe.transpose(t[:, j * P:(j + 1) * P], a[:, j * P:(j + 1) * P], ident)
                    ins.then_inc(tpr.full, 1)
                if i >= 3:
                    h, q = B_UNITS[i - 3]
                    g = h // 4
                    r = slice((h % 2) * HD, (h % 2 + 1) * HD)
                    pe.wait_ge(t_ring.full, t_ring.filled())
                    pe.wait_ge(ot_ring.free, ot_ring.given_back())
                    t, o = t_ring.take(), ot_ring.claim()
                    for j in range(4):
                        mm(o[r, 0:P], vB[:, j, g * HD:(g + 1) * HD], t[:, j, :], j == 0, j == 3,
                           ot_ring.full if j == 3 else None)

        def act_b_attend(act, step):
            n = len(B_UNITS)
            for i in range(n + 2):
                if i < n:
                    h, q = B_UNITS[i]
                    act.wait_ge(sm_ring_b.full, sm_ring_b.filled())
                    act.wait_ge(pb_ring.free, pb_ring.given_back())
                    s, p = sm_ring_b.take(), pb_ring.claim()
                    sv = sinkv[:, i % 8, :]
                    step(act.activation(p, s, ACT.Exp, bias=sv[:, 0:1], accum_out=sv[:, 1:2]))
                    act.sem_inc(sm_ring_b.free, 1)
                    step(act.activation(sv[:, 2:3], v("b_sink", h), ACT.Exp, bias=sv[:, 0:1]))
                    act.sem_inc(pb_ring.full, 1)
                if i >= 2:
                    act.wait_ge(tpr.full, tpr.filled())
                    act.wait_ge(t_ring.free, t_ring.given_back())
                    tp, t = tpr.take(), t_ring.claim()
                    act.sem_inc(a_ring.free, 1)
                    step(act.activation(t, tp.rearrange("p (a b) -> p a b", b=P), ACT.Copy))
                    act.sem_inc(tpr.free, 1)
                    act.sem_inc(t_ring.full, 1)

        def dve_b_attend(dve, step):
            n = len(B_UNITS)
            for i in range(n + 4):
                if i < n:
                    h, q = B_UNITS[i]
                    dve.wait_ge(D_.full, D_.filled())
                    dve.wait_ge(sm_ring_b.free, sm_ring_b.given_back())
                    bank, s = D_.take(), sm_ring_b.claim()
                    sv = sinkv[:, i % 8, :]
                    step(dve.scalar_tensor_tensor(out=s, in0=bank, scalar=SCALE, in1=const("window", q, TOK),
                                                  op0=ALU.mult, op1=ALU.add))
                    dve.sem_inc(D_.free, 1)
                    step(dve.tensor_reduce(sv[:, 0:1], s, AX, ALU.max))
                    step(dve.tensor_scalar(sv[:, 0:1], sv[:, 0:1], v("b_sink", h), -1.0, ALU.max, ALU.mult))
                    dve.sem_inc(sm_ring_b.full, 1)
                if 1 <= i < n + 1:
                    dve.wait_ge(pb_ring.full, pb_ring.filled())
                    dve.wait_ge(a_ring.free, a_ring.given_back())
                    p, a = pb_ring.take(), a_ring.claim()
                    sv = sinkv[:, (i - 1) % 8, :]
                    step(dve.tensor_tensor(sv[:, 3:4], sv[:, 1:2], sv[:, 2:3], ALU.add))
                    step(dve.reciprocal(sv[:, 3:4], sv[:, 3:4]))
                    step(dve.tensor_scalar(a, p, sv[:, 3:4], None, ALU.mult))
                    dve.sem_inc(pb_ring.free, 1)
                    dve.sem_inc(a_ring.full, 1)
                if i >= 4:
                    h, q = B_UNITS[i - 4]
                    r = slice((h % 2) * HD, (h % 2 + 1) * HD)
                    dve.wait_ge(ot_ring.full, ot_ring.filled())
                    o = ot_ring.take()
                    step(dve.tensor_copy(oB[r, h // 2, q * P:(q + 1) * P], o[r, 0:P]))
                    dve.sem_inc(ot_ring.free, 1)
                    dve.sem_inc(t_ring.free, 1)

        biasT = Carve()(16, 3 * P)
        B0 = 16 * 3 * P
        xU, hU = xT[:, :, LAT:TOK], hT[:, :, LAT:TOK]
        oa, ob, oc = xU[:, 0:4], xU[:, 4:8], hU[:, 0:4]

        X_ = Carve(B0)
        oh_sb = X_(N_OH)
        f_sb = X_(2 * OH)
        toep = X_(16, 3 * P)
        oh_loaded, f_ready, f_stored, toep_loaded = (signal(n, u) for n, u in (
            ("oh_loaded", 16), ("f_ready", 1), ("f_stored", 16), ("toep_loaded", 16)))

        def pe_bias(pe, W, mm):
            pe.wait_ge(oh_loaded.sem, oh_loaded.due(pe))
            for i in range(2):
                pe.wait_ge(D_.free, D_.given_back())
                mm(D_.claim()[0:8, 0:OH], v("rel", i * 8, 8)[0:33, :], oh_sb[0:33, i * OH:(i + 1) * OH]).then_inc(D_.full, 1)
            pe.wait_ge(toep_loaded.sem, toep_loaded.due(pe))
            for h in range(16):
                pe.wait_ge(D_.free, D_.given_back())
                mm(D_.claim()[:, 0:3 * P], const("flip"), toep[:, h, :]).then_inc(D_.full, 1)

        def dve_bias(dve, step):
            for i in range(2):
                dve.wait_ge(D_.full, D_.filled())
                bank = D_.take()
                step(dve.tensor_copy(f_sb[0:8, i * OH:(i + 1) * OH], bank[0:8, 0:OH]))
                dve.sem_inc(D_.free, 1)
            dve.sem_inc(f_ready.sem, 1)
            for h in range(16):
                dve.wait_ge(D_.full, D_.filled())
                bank = D_.take()
                step(dve.tensor_copy(biasT[:, h, :], bank[:, 0:3 * P]))
                dve.sem_inc(D_.free, 1)

        def dma_bias(act):
            act.dma_start(oh_sb[0:33, :], onehots).then_inc(oh_loaded.sem, 16)
            act.wait_ge(f_ready.sem, f_ready.due(act))
            act.dma_start(scratch.rearrange("(i h) x -> h i x", i=2),
                         f_sb[0:8, :].rearrange("p (i x) -> p i x", i=2)).then_inc(f_stored.sem, 16)
            act.wait_ge(f_stored.sem, f_stored.due(act))
            shifted = bass.AP(scratch.tensor, 0, [[1, P], [OH, 16], [1, 3 * P]])
            act.dma_start(toep, shifted).then_inc(toep_loaded.sem, 16)

        def gained(act, name, l):
            def affine(k):
                act.activation(hT[:, k, 0:LAT], hT[:, k, 0:LAT], ACT.Copy,
                               scale=v(name, l * DC + k)).then_inc(h_ready.sem, 1)
            return affine

        def copy_out(dve, dst, w):
            dve.wait_ge(D_.full, D_.filled())
            bank = D_.take()
            dve.tensor_copy(dst, bank[:, 0:w]).then_inc(D_.free, 1)

        def slot(n, k=1):
            return arena[:, B0 + n * 1024:B0 + (n + k) * 1024]

        def fm(n):
            return slot(n).rearrange("p (m t) -> p m t", t=LAT)

        zraw = arena[:, B0:B0 + 14 * (LAT + 1)].rearrange("p (m t) -> p m t", t=LAT + 1)
        zs = arena[:, B0 + 4096:B0 + 4096 + 14 * LAT].rearrange("p (m t) -> p m t", t=LAT)
        zr, zk, zv = zs[:, 0:4], zs[:, 4:8], zs[:, 8:12]
        ld, lcum, pcum, pinv = fm(0), fm(1), fm(2), fm(3)
        pprev, iclr, gate, kk, bonus, sqk, kmod = fm(8), fm(9), fm(10), fm(11), fm(12), fm(13), fm(14)
        rt, kt, at_, bt = pcum, pinv, pprev, iclr
        vtok, atok, btok, ktok = (slot(n).rearrange("p (t f) -> p t f", t=2) for n in (15, 11, 0, 1))
        utok = slot(7).rearrange("p (t f) -> p t f", t=2)
        xat = slot(4).rearrange("p (m t f) -> p m t f", m=4, t=2)
        lrb, lrk = (slot(n, 2).rearrange("p (t h f) -> p t h f", t=2, h=8) for n in (5, 13))
        B4 = [slot(16 + n // 2)[:, (n % 2) * 512:(n % 2 + 1) * 512].rearrange("p (a b) -> p a b", b=P)
              for n in range(8)]
        B4 += [u[:, 4:8, i * P:(i + 1) * P] for u in (xU, hU) for i in range(2)]
        LT, LAK, X, XT, LTL, Y = (B4[2 * i:2 * i + 2] for i in range(6))
        W1 = [a[:, :, 0:HD] for a in LTL]
        state = [mini[:, c * 256:(c + 1) * 256].rearrange("p (m i) -> p m i", i=HD) for c in range(3)]
        p_end = mini[:, 768:784].rearrange("p (m c) -> p m c", c=4)
        y_ = at_
        mix_ready = signal("mix_ready")
        act_ready = signal("act_ready")
        to_act = signal("to_act")
        to_dve = signal("to_dve")

        def by_group(tok, t):
            return tok[:, t].rearrange("p (u g f) -> p u g f", g=2, f=HD)

        def pe_rwkv_in(pe, W, mm, l):
            pe_norm(pe, mm, LAT)
            pe_project(pe, W, mm, "w_in", l, range(0, IN["nq"], P), LAT, lambda _: D_, hT, parts_ready=True)
            pe.wait_ge(act_ready.sem, act_ready.due(pe))
            w = W.next("rwkv_wa", l, 0, 0, width=4)
            for m in range(RC):
                pe.wait_ge(A_.free, A_.given_back())
                mm(A_.claim()[:, 0:LAT], w[0:64, m * P:(m + 1) * P], zs[0:64, 12, :]).then_inc(A_.full, 1)
            for m in range(RC):
                pe.wait_ge(A_.free, A_.given_back())
                mm(A_.claim()[:, 0:LAT], w[64:128, m * P:(m + 1) * P], zs[64:128, 12, :]).then_inc(A_.full, 1)
            w = W.next("rwkv_g2", l, 0, 0, width=4)
            for m in range(RC):
                pe.wait_ge(A_.free, A_.given_back())
                mm(A_.claim()[:, 0:LAT], w[:, m * P:(m + 1) * P], zs[:, 13, :]).then_inc(A_.full, 1)
            pe.wait_ge(mix_ready.sem, mix_ready.due(pe))
            for m in range(RC):
                pe.wait_ge(A_.free, A_.given_back())
                mm(A_.claim()[:, 0:LAT], bones, sqk[:, m]).then_inc(A_.full, 1)
            pe.wait_ge(mix_ready.sem, mix_ready.due(pe))
            for m in range(RC):
                pe.wait_ge(D_.free, D_.given_back())
                mm(D_.claim()[:, 0:LAT], bones, sqk[:, m]).then_inc(D_.full, 1)

        def act_rwkv_in(act, step, l):
            act_norm(act, step, LAT, gained(act, "ln1", l))
            act.wait_ge(to_act.sem, to_act.due(act))
            step(act.activation(zs[0:64, 12, :], zs[0:64, 12, :], ACT.Tanh))
            step(act.activation(zs[:, 13, :], zs[:, 13, :], ACT.Sigmoid))
            act.sem_inc(act_ready.sem, 1)
            for m in range(RC):
                act.wait_ge(A_.full, A_.filled())
                bank = A_.take()
                act.activation(ld[:, m], bank[:, 0:LAT], ACT.Sigmoid, bias=v("w0", l * RC + m)).then_inc(A_.free, 1)
            for m in range(RC):
                act.wait_ge(A_.full, A_.filled())
                bank = A_.take()
                act.activation(iclr[:, m], bank[:, 0:LAT], ACT.Sigmoid, bias=v("a0", l * RC + m)).then_inc(A_.free, 1)
            for m in range(RC):
                act.wait_ge(A_.full, A_.filled())
                bank = A_.take()
                act.activation(gate[:, m], bank[:, 0:LAT], ACT.Copy).then_inc(A_.free, 1)
            act.drain().then_inc(to_dve.sem, 1)
            act.wait_ge(to_act.sem, to_act.due(act))
            act.activation(pprev, pprev, ACT.Exp)
            act.activation(pcum, lcum, ACT.Exp)
            step(act.activation(pinv, lcum, ACT.Exp, scale=-1.0))
            act.sem_inc(to_dve.sem, 1)
            for m in range(RC):
                act.wait_ge(A_.full, A_.filled())
                bank = A_.take()
                step(act.activation(lcum[:, m], bank[:, 0:LAT], ACT.Copy))
                act.sem_inc(A_.free, 1)
            act.sem_inc(to_dve.sem, 1)
            act.wait_ge(to_act.sem, to_act.due(act))
            act_rsqrt(act, step, lcum, lcum, 1.0, 0.0)
            act.sem_inc(to_dve.sem, 1)

        def dve_rwkv_in(dve, step, l):
            dve_norm(dve, LAT)
            step(dve.memset(zraw[:, :, 0:1], 0.0))
            for n in [*range(14)]:
                dve.wait_ge(D_.full, D_.filled())
                bank = D_.take()
                step(dve.tensor_copy(zraw[:, n, 1:], bank[:, 0:LAT]))
                dve.sem_inc(D_.free, 1)
                z = zs[:, n, :]
                step(dve.tensor_tensor(z, zraw[:, n, 0:LAT], zraw[:, n, 1:], ALU.subtract))
                step(dve.scalar_tensor_tensor(out=z, in0=z, scalar=v("mu", l * 14 + n), in1=zraw[:, n, 1:],
                                              op0=ALU.mult, op1=ALU.add))
            dve.sem_inc(to_act.sem, 1)
            for m in range(RC):
                step(dve.tensor_scalar(kk[:, m], zk[:, m], v("k_k", l * RC + m), None, ALU.mult))
            step(dve.tensor_tensor(sqk, kk, kk, ALU.mult))
            dve.sem_inc(mix_ready.sem, 1)
            dve.wait_ge(to_dve.sem, to_dve.due(dve))
            step(dve.tensor_scalar(ld, ld, DECAY, None, ALU.mult))
            for m in range(RC):
                step(dve.tensor_tensor_scan(lcum[:, m], const("carry"), ld[:, m], 0.0, ALU.mult, ALU.add))
            step(dve.tensor_tensor(pprev, lcum, ld, ALU.subtract))
            dve.sem_inc(to_act.sem, 1)
            for m in range(RC):
                step(dve.tensor_scalar(kmod[:, m], iclr[:, m], -1.0, v("k_a", l * RC + m), ALU.add, ALU.mult))
            step(dve.scalar_tensor_tensor(out=kmod, in0=kmod, scalar=1.0, in1=zk, op0=ALU.add, op1=ALU.mult))
            dve.wait_ge(to_dve.sem, to_dve.due(dve))
            dve.wait_ge(to_dve.sem, to_dve.due(dve))
            step(dve.tensor_scalar(lcum, lcum, 1e-12, None, ALU.max))
            dve.sem_inc(to_act.sem, 1)
            for m in range(RC):
                step(dve.scalar_tensor_tensor(out=sqk[:, m], in0=zr[:, m], scalar=v("r_k", l * RC + m), in1=kmod[:, m],
                                              op0=ALU.mult, op1=ALU.mult))
            dve.sem_inc(mix_ready.sem, 1)
            dve.wait_ge(to_dve.sem, to_dve.due(dve))
            step(dve.tensor_tensor(kk, kk, lcum, ALU.mult))
            step(dve.tensor_tensor(iclr, iclr, kk, ALU.mult))
            step(dve.tensor_tensor(bt, iclr, pinv, ALU.mult))
            step(dve.scalar_tensor_tensor(out=at_, in0=kk, scalar=-1.0, in1=pprev, op0=ALU.mult, op1=ALU.mult))
            step(dve.tensor_tensor(kt, kmod, pinv, ALU.mult))
            step(dve.tensor_copy(p_end, pcum[:, :, CH - 1::CH]))
            step(dve.tensor_tensor(rt, zr, pcum, ALU.mult))
            for m in range(RC):
                dve.wait_ge(D_.full, D_.filled())
                bank = D_.take()
                dve.tensor_tensor(bonus[:, m], bank[:, 0:LAT], zv[:, m], ALU.mult).then_inc(D_.free, 1)

        def pe_rwkv_core(pe, W, mm, l):
            for src in (zv, at_, bt, kt):
                for t in range(2):
                    pe.wait_ge(A_.free, A_.given_back())
                    bank = A_.claim()
                    for m in range(RC):
                        ins = pe.transpose(bank[:, m * P:(m + 1) * P], src[:, m, t * P:(t + 1) * P], ident)
                    ins.then_inc(A_.full, 1)

            def gram(t, g, a, b):
                pe.wait_ge(D_.free, D_.given_back())
                bank = D_.claim()
                r = slice(g * HD, (g + 1) * HD)
                for u in range(4):
                    mm(bank[:, u * P:(u + 1) * P], a[r, u, t * P:(t + 1) * P], b[r, u, t * P:(t + 1) * P],
                       inc=D_.full if u == 3 else None)

            for t in range(2):
                for g in range(2):
                    gram(t, g, bt, at_)
                for g in range(2):
                    gram(t, g, kt, at_)
                for g in range(2):
                    gram(t, g, bt, rt)
                    gram(t, g, kt, rt)
                for g in range(2):
                    pe.wait_ge(mix_ready.sem, mix_ready.due(pe))
                    pe.wait_ge(A_.free, A_.given_back())
                    bank = A_.claim()
                    for u in range(4):
                        mm(bank[:, u * P:(u + 1) * P], LTL[g][:, u, :], ident, inc=A_.full if u == 3 else None)
                for level in range(1, LEVELS):
                    for g in range(2):
                        pe.wait_ge(mix_ready.sem, mix_ready.due(pe))
                        pe.wait_ge(A_.free, A_.given_back())
                        bank = A_.claim()
                        for u in range(4):
                            mm(bank[:, u * P:(u + 1) * P], LTL[g][:, u, :], X[g][:, u, :],
                               inc=A_.full if u == 3 else None)
                    for g in range(2):
                        pe.wait_ge(act_ready.sem, act_ready.due(pe))
                        for a, b in (((XT, Y), (Y, XT)) if level < LEVELS - 1 else ((Y, XT),)):
                            pe.wait_ge(D_.free, D_.given_back())
                            bank = D_.claim()
                            for u in range(4):
                                mm(bank[:, u * P:(u + 1) * P], a[g][:, u, :], b[g][:, u, :],
                                   inc=D_.full if u == 3 else None)
                for g in range(2):
                    pe.wait_ge(mix_ready.sem, mix_ready.due(pe))
                    pe.wait_ge(A_.free, A_.given_back())
                    bank = A_.claim()
                    for u in range(4):
                        h = 2 * u + g
                        mm(bank[:, u * HD:(u + 1) * HD], LAK[g][:, u, :], vtok[:, t, h * HD:(h + 1) * HD],
                           inc=A_.full if u == 3 else None)
                    pe.wait_ge(A_.free, A_.given_back())
                    bank = A_.claim()
                    for u in range(4):
                        h = 2 * u + g
                        mm(bank[g * HD:(g + 1) * HD, u * P:(u + 1) * P], atok[:, t, h * HD:(h + 1) * HD], XT[g][:, u, :],
                           inc=A_.full if u == 3 else None)
                    pe.wait_ge(act_ready.sem, act_ready.due(pe))
                    pe.wait_ge(A_.free, A_.given_back())
                    bank = A_.claim()
                    for u in range(4):
                        mm(bank[:, u * HD:(u + 1) * HD], XT[g][:, u, :], W1[g][:, u, :], inc=A_.full if u == 3 else None)

        def act_rwkv_core(act, step, l):
            for dst in (vtok, atok, btok, ktok):
                for t in range(2):
                    act.wait_ge(A_.full, A_.filled())
                    bank = A_.take()
                    act.activation(dst[:, t], bank, ACT.Copy).then_inc(A_.free, 1)
            for t in range(2):
                for g in range(2):
                    act.wait_ge(A_.full, A_.filled())
                    bank = A_.take()
                    step(act.activation(X[g], bank.rearrange("p (a b) -> p a b", b=P), ACT.Copy))
                    act.sem_inc(A_.free, 1)
                    act.sem_inc(to_dve.sem, 1)
                for level in range(1, LEVELS):
                    for g in range(2):
                        act.wait_ge(A_.full, A_.filled())
                        bank = A_.take()
                        step(act.activation(Y[g], bank.rearrange("p (a b) -> p a b", b=P), ACT.Copy))
                        act.sem_inc(A_.free, 1)
                        act.sem_inc(act_ready.sem, 1)
                for g in range(2):
                    act.wait_ge(A_.full, A_.filled())
                    bank = A_.take()
                    step(act.activation(W1[g], bank[:, 0:4 * HD].rearrange("p (a b) -> p a b", b=HD), ACT.Copy))
                    act.sem_inc(A_.free, 1)
                    act.sem_inc(act_ready.sem, 1)
                    act.wait_ge(A_.full, A_.filled())
                    bank = A_.take()
                    r = slice(g * HD, (g + 1) * HD)
                    act.activation(xat[r, :, t, :], bank[r, :].rearrange("p (a b) -> p a b", b=P),
                                   ACT.Copy).then_inc(A_.free, 1)
                    act.wait_ge(A_.full, A_.filled())
                    bank = A_.take()
                    act.activation(by_group(utok, t)[:, :, g, :], bank[:, 0:256].rearrange("p (a b) -> p a b", b=HD),
                                   ACT.Copy).then_inc(A_.free, 1)

        def dve_rwkv_core(dve, step, l):
            def four(ap):
                return ap.unsqueeze(1).to_broadcast([P, 4, P])

            def bank4(bank):
                return bank.rearrange("p (a b) -> p a b", b=P)

            for t in range(2):
                for dst, mask in ((LT, "before"), (LAK, "before")):
                    for g in range(2):
                        dve.wait_ge(D_.full, D_.filled())
                        bank = D_.take()
                        step(dve.tensor_tensor(dst[g], bank4(bank), four(const(mask)), ALU.mult))
                        dve.sem_inc(D_.free, 1)
                for g in range(2):
                    for dst in (lrb, lrk):
                        dve.wait_ge(D_.full, D_.filled())
                        bank = D_.take()
                        dve.tensor_tensor(dst[:, t, g::2], bank4(bank), four(const("upto")),
                                          ALU.mult).then_inc(D_.free, 1)
                for g in range(2):
                    step(dve.tensor_tensor(LTL[g], LT[g], four(const("level", 0, P)), ALU.mult))
                    dve.sem_inc(mix_ready.sem, 1)
                    step(dve.tensor_tensor(XT[g], LTL[g], four(ident), ALU.add))
                for g in range(2):
                    dve.wait_ge(to_dve.sem, to_dve.due(dve))
                    step(dve.tensor_tensor(X[g], X[g], four(ident), ALU.add))
                    step(dve.tensor_tensor(LTL[g], LT[g], four(const("level", 1, P)), ALU.mult))
                    dve.sem_inc(mix_ready.sem, 1)
                for level in range(1, LEVELS):
                    for g in range(2):
                        if level < LEVELS - 1:
                            dve.wait_ge(D_.full, D_.filled())
                            bank = D_.take()
                            step(dve.tensor_tensor(X[g], X[g], bank4(bank), ALU.add))
                            dve.sem_inc(D_.free, 1)
                        dve.wait_ge(D_.full, D_.filled())
                        bank = D_.take()
                        step(dve.tensor_tensor(XT[g], XT[g], bank4(bank), ALU.add))
                        dve.sem_inc(D_.free, 1)
                        if level < LEVELS - 1:
                            step(dve.tensor_tensor(LTL[g], LT[g], four(const("level", level + 1, P)), ALU.mult))
                        dve.sem_inc(mix_ready.sem, 1)

        def pe_rwkv_out(pe, W, mm, l):
            for c in range(LAT // CH):
                t, r = c // 2, slice((c % 2) * CH, (c % 2 + 1) * CH)
                if c:
                    pe.wait_ge(mix_ready.sem, mix_ready.due(pe))
                    for g in range(2):
                        pe.wait_ge(D_.free, D_.given_back())
                        bank = D_.claim()
                        q = slice(g * HD, (g + 1) * HD)
                        for u in range(4):
                            mm(bank[r, u * HD:(u + 1) * HD], xat[q, u, t, r], state[c - 1][q, u, :],
                               inc=D_.full if u == 3 else None)
                if c < LAT // CH - 1:
                    if c:
                        pe.wait_ge(mix_ready.sem, mix_ready.due(pe))
                    pe.wait_ge(D_.free, D_.given_back())
                    bank = D_.claim()
                    for h in range(8):
                        q = slice((h % 2) * HD, (h % 2 + 1) * HD)
                        o = bank[q, (h // 2) * HD:(h // 2 + 1) * HD]
                        f = slice(h * HD, (h + 1) * HD)
                        mm(o, btok[r, t, f], utok[r, t, f], True, False)
                        mm(o, ktok[r, t, f], vtok[r, t, f], False, True, D_.full if h == 7 else None)
            pe.wait_ge(mix_ready.sem, mix_ready.due(pe))
            for m in range(RC):
                for hh in range(2):
                    pe.wait_ge(D_.free, D_.given_back())
                    bank = D_.claim()
                    h = 2 * m + hh
                    q = slice(hh * HD, (hh + 1) * HD)
                    f = slice(h * HD, (h + 1) * HD)
                    for t in range(2):
                        o = bank[q, t * P:(t + 1) * P]
                        mm(o, vtok[:, t, f], lrk[:, t, h, :], True, False)
                        mm(o, utok[:, t, f], lrb[:, t, h, :], False, False)
                        for c in range(max(2 * t, 1), 2 * t + 2):
                            last = c == 2 * t + 1
                            mm(bank[q, c * CH:(c + 1) * CH], state[c - 1][q, m, :], rt[q, m, c * CH:(c + 1) * CH],
                               False, last, D_.full if last and t else None)
            pe.wait_ge(mix_ready.sem, mix_ready.due(pe))
            for m in range(RC):
                pe.wait_ge(D_.free, D_.given_back())
                mm(D_.claim()[:, 0:LAT], bones, y_[:, m]).then_inc(D_.full, 1)
            pe.wait_ge(act_ready.sem, act_ready.due(pe))
            for m in range(RC):
                pe.wait_ge(A_.free, A_.given_back())
                mm(A_.claim()[:, 0:LAT], bones, sqk_y[:, m]).then_inc(A_.full, 1)

        sqk_y = fm(8 + 1)
        rstd_y = fm(3)

        def dve_rwkv_out(dve, step, l):
            for c in range(LAT // CH):
                t, r = c // 2, slice((c % 2) * CH, (c % 2 + 1) * CH)
                if c:
                    for g in range(2):
                        dve.wait_ge(D_.full, D_.filled())
                        bank = D_.take()
                        o = by_group(utok, t)[r, :, g, :]
                        step(dve.tensor_tensor(o, o, bank[r, 0:256].rearrange("p (u f) -> p u f", f=HD), ALU.add))
                        dve.sem_inc(D_.free, 1)
                    dve.sem_inc(mix_ready.sem, 1)
                if c < LAT // CH - 1:
                    dve.wait_ge(D_.full, D_.filled())
                    bank = D_.take()
                    s = state[c]
                    pe_bc = p_end[:, :, c:c + 1].to_broadcast([P, RC, HD])
                    b4 = bank[:, 0:RC * HD].rearrange("p (m i) -> p m i", i=HD)
                    if c:
                        step(dve.tensor_tensor(s, state[c - 1], b4, ALU.add))
                        step(dve.tensor_tensor(s, s, pe_bc, ALU.mult))
                    else:
                        step(dve.tensor_tensor(s, b4, pe_bc, ALU.mult))
                    dve.sem_inc(D_.free, 1)
                    dve.sem_inc(mix_ready.sem, 1)
            for h in range(8):
                dve.wait_ge(D_.full, D_.filled())
                bank = D_.take()
                q = slice((h % 2) * HD, (h % 2 + 1) * HD)
                step(dve.tensor_copy(y_[q, h // 2], bank[q, 0:LAT]))
                dve.sem_inc(D_.free, 1)
            dve.sem_inc(mix_ready.sem, 1)
            for m in range(RC):
                dve.wait_ge(D_.full, D_.filled())
                bank = D_.take()
                step(dve.scalar_tensor_tensor(out=y_[:, m], in0=bank[:, 0:LAT], scalar=-1.0 / HD, in1=y_[:, m],
                                              op0=ALU.mult, op1=ALU.add))
                dve.sem_inc(D_.free, 1)
            dve.sem_inc(to_act.sem, 1)
            dve.wait_ge(to_dve.sem, to_dve.due(dve))
            step(dve.tensor_tensor(y_, y_, rstd_y, ALU.mult))
            for m in range(RC):
                step(dve.tensor_scalar(y_[:, m], y_[:, m], v("ln_w", l * RC + m), v("ln_b", l * RC + m),
                                       ALU.mult, ALU.add))
            step(dve.tensor_tensor(y_, y_, bonus, ALU.add))
            step(dve.tensor_tensor(oa, y_, gate, ALU.mult))

        def act_rwkv_out(act, step, l):
            act.wait_ge(to_act.sem, to_act.due(act))
            step(act.activation(sqk_y, y_, ACT.Square))
            act.sem_inc(act_ready.sem, 1)
            for m in range(RC):
                act.wait_ge(A_.full, A_.filled())
                bank = A_.take()
                act_rsqrt(act, step, rstd_y[:, m], bank[:, 0:LAT], 1.0 / HD, const("gn_eps"))
                act.sem_inc(A_.free, 1)
            act.sem_inc(to_dve.sem, 1)

        Q_ = Carve(B0)
        fN = Q_(8, LAT)
        dup = Q_(4, 2, LAT)
        vsw = Q_(2, 3, P)
        ngate = Q_(2, 24)
        zpe = Q_(2, 16, 2, 15)
        hidc = Q_(2, 2, 30)
        kcmp = Q_(30)
        vcmp = Q_(2, HD)
        sc = Q_(8, N_CMP)
        pcT = Q_(QT, 8, P)
        mx8 = Q_(8)
        fS = Q_(5, LAT)
        dupS = Q_(2, LAT)
        vS = Q_(2, P)
        s_ring = ring("s2", [Q_(2, LAT) for _ in range(3)])
        e_ring = ring("e2", [Q_(2, LAT) for _ in range(3)])
        n_ring = ring("n2", [Q_(2, LAT) for _ in range(2)])
        nt_ring = ring("nt2", [Q_(4, P) for _ in range(2)])
        st2 = Q_(8, 8)

        def pe_nsa_in(pe, W, mm, l):
            pe_project(pe, W, mm, "w_in", l, [*range(IN["nq"], IN["nvs"], P), IN["nkw"]], LAT, lambda _: D_, hT)
            for c, width in ((IN["nvs"], 1), (IN["nvw"], 2)):
                pe.wait_ge(D_.free, D_.given_back(2))
                banks = [D_.claim() for _ in range(2)]
                for k in range(DC):
                    w = W.next("w_in", l, k * P, c, width=width)
                    for t in range(2):
                        mm(banks[t][:, 0:width * P], hT[:, k, t * P:(t + 1) * P], w, k == 0, k == DC - 1,
                           D_.full if k == DC - 1 else None)
            pe.wait_ge(mix_ready.sem, mix_ready.due(pe))
            for i in range(4):
                for g in range(2):
                    pe.wait_ge(D_.free, D_.given_back())
                    mm(D_.claim()[:, 0:LAT], const("sel", g, P), fN[:, 4 + i, :]).then_inc(D_.full, 1)
            pe.wait_ge(mix_ready.sem, mix_ready.due(pe))
            for n, name in enumerate(("nsa_ck", "nsa_cv")):
                for h in range(2):
                    pe.wait_ge(A_.free, A_.given_back())
                    bank = A_.claim()
                    for k in range(16):
                        mm(bank[:, 0:30], W.next(name + "_w1", l, k * P, h * P),
                           zpe[:, n, k].rearrange("p g c -> p (g c)"), k == 0, k == 15, A_.full if k == 15 else None)
                pe.wait_ge(act_ready.sem, act_ready.due(pe))
                if n == 0:
                    pe.wait_ge(D_.free, D_.given_back())
                    bank = D_.claim()
                    for k in range(2):
                        w = W.next(name + "_w2", l, k * P, 0)
                        for half in range(2):
                            mm(bank[half * HD:(half + 1) * HD, 0:30], w[:, 0:HD], hidc[:, n, k, :], k == 0, k == 1,
                               D_.full if k and half else None)
                else:
                    pe.wait_ge(D_.free, D_.given_back(2))
                    banks = [D_.claim() for _ in range(2)]
                    for k in range(2):
                        w = W.next(name + "_w2", l, k * P, 0)
                        for g in range(2):
                            mm(banks[g][0:N_CMP, 0:HD], hidc[:, n, k, g * N_CMP:(g + 1) * N_CMP], w[:, 0:HD],
                               k == 0, k == 1, D_.full if k else None)

        def act_nsa_in(act, step, l):
            act.wait_ge(to_act.sem, to_act.due(act))
            step(act.activation(ngate, vsw[:, :, 2, 0:24], ACT.Sigmoid))
            for n in range(2):
                for h in range(2):
                    act.wait_ge(A_.full, A_.filled())
                    bank = A_.take()
                    step(act.activation(hidc[:, n, h, :], bank[:, 0:30], ACT.Gelu))
                    act.sem_inc(A_.free, 1)
                act.sem_inc(act_ready.sem, 1)

        def dve_nsa_in(dve, step, l):
            for i in range(8):
                copy_out(dve, fN[:, i, :], LAT)
            for t in range(2):
                copy_out(dve, vsw[:, t, 0, :], P)
            for t in range(2):
                copy_out(dve, vsw[:, t, 1:3, :].rearrange("p a b -> p (a b)"), 2 * P)
            dve.drain().then_inc(mix_ready.sem, 1)
            dve.sem_inc(to_act.sem, 1)
            for i in range(4):
                for g in range(2):
                    dve.wait_ge(D_.full, D_.filled())
                    bank = D_.take()
                    step(dve.tensor_copy(dup[:, i, g, :], bank[:, 0:LAT]))
                    dve.sem_inc(D_.free, 1)
            for n, name in enumerate(("pe_k", "pe_v")):
                for par in range(2):
                    r = slice(par * HD, (par + 1) * HD)
                    tokens16 = dup[r, n].rearrange("p g (c l x) -> p g c l x", l=8, x=2)
                    for a in range(2):
                        pos = v(name, l * 16 + a * 8, 8)[r, :]
                        for g in range(2):
                            o = zpe[r, n, a * 8:(a + 1) * 8, g, :].rearrange("p l c -> p c l")
                            step(dve.tensor_tensor(o, tokens16[:, g, a:a + N_CMP, :, par],
                                                   pos.unsqueeze(1).to_broadcast([HD, N_CMP, 8]), ALU.add))
            dve.sem_inc(mix_ready.sem, 1)
            dve.wait_ge(D_.full, D_.filled())
            bank = D_.take()
            dve.tensor_copy(kcmp, bank[:, 0:30]).then_inc(D_.free, 1)
            for g in range(2):
                dve.wait_ge(D_.full, D_.filled())
                bank = D_.take()
                dve.tensor_copy(vcmp[0:N_CMP, g, :], bank[0:N_CMP, 0:HD]).then_inc(D_.free, 1)

        def pe_nsa_cmp(pe, W, mm):
            for q in range(QT):
                for half in range(2):
                    pe.wait_ge(D_.free, D_.given_back())
                    bank = D_.claim()
                    r = slice(half * HD, (half + 1) * HD)
                    for u in range(4):
                        mm(bank[:, u * N_CMP:(u + 1) * N_CMP], fN[r, u, q * P:(q + 1) * P],
                           kcmp[r, (u // 2) * N_CMP:(u // 2 + 1) * N_CMP], inc=D_.full if u == 3 else None)
                pe.wait_ge(mix_ready.sem, mix_ready.due(pe))
                for half in range(2):
                    pe.wait_ge(A_.free, A_.given_back())
                    bank = A_.claim()
                    for u in range(4):
                        ins = pe.transpose(bank[0:N_CMP, u * P:(u + 1) * P], sc[:, 4 * half + u, :], ident)
                    ins.then_inc(A_.full, 1)

        def act_nsa_cmp(act, step):
            for q in range(QT):
                act.wait_ge(to_act.sem, to_act.due(act))
                step(act.activation(sc, sc, ACT.Exp))
                act.sem_inc(to_dve.sem, 1)
                for half in range(2):
                    act.wait_ge(A_.full, A_.filled())
                    bank = A_.take()
                    step(act.activation(pcT[0:N_CMP, q, 4 * half:4 * half + 4, :],
                                        bank[0:N_CMP, :].rearrange("p (a b) -> p a b", b=P), ACT.Copy))
                    act.sem_inc(A_.free, 1)
                act.sem_inc(to_dve.sem, 1)

        def dve_nsa_cmp(dve, step):
            def wide(a):
                return a.unsqueeze(2).to_broadcast([P, 8, N_CMP])

            for q in range(QT):
                mask = const("cmp", q, N_CMP).unsqueeze(1).to_broadcast([P, 4, N_CMP])
                for half in range(2):
                    dve.wait_ge(D_.full, D_.filled())
                    bank = D_.take()
                    step(dve.scalar_tensor_tensor(out=sc[:, half::2, :],
                                                  in0=bank[:, 0:4 * N_CMP].rearrange("p (a b) -> p a b", b=N_CMP),
                                                  scalar=SCALE, in1=mask, op0=ALU.mult, op1=ALU.add))
                    dve.sem_inc(D_.free, 1)
                step(dve.tensor_reduce(mx8, sc, AX, ALU.max))
                step(dve.tensor_scalar(mx8, mx8, NEG / 10, None, ALU.max))
                step(dve.tensor_tensor(sc, sc, wide(mx8), ALU.subtract))
                dve.sem_inc(to_act.sem, 1)
                dve.wait_ge(to_dve.sem, to_dve.due(dve))
                step(dve.tensor_reduce(mx8, sc, AX, ALU.add))
                step(dve.tensor_scalar(mx8, mx8, 1e-30, None, ALU.max))
                step(dve.reciprocal(mx8, mx8))
                step(dve.tensor_tensor(mx8, mx8, ngate[:, q].rearrange("p (h i) -> p h i", i=3)[:, :, 0], ALU.mult))
                step(dve.tensor_tensor(sc, sc, wide(mx8), ALU.mult))
                dve.sem_inc(mix_ready.sem, 1)
                dve.wait_ge(to_dve.sem, to_dve.due(dve))

        N_UNITS = [(h, q) for h in range(8) for q in range(QT)]

        def bias_of(base, h, q):
            return biasT[:, base + h, P * (1 - q):2 * P] if q == 0 else biasT[:, base + h, 0:2 * P]

        def pe_rel(pe, mm, qsrc, keys, values, cmp):
            n, parts = len(N_UNITS), len(keys)
            for i in range(n + 3):
                if i < n:
                    h, q = N_UNITS[i]
                    r = slice((h % 2) * HD, (h % 2 + 1) * HD)
                    nk = (q + 1) * P
                    pe.wait_ge(D_.free, D_.given_back())
                    bank = D_.claim()
                    for j, key in enumerate(keys):
                        mm(bank[:, j * LAT:j * LAT + nk], qsrc[r, h // 2, q * P:(q + 1) * P], key[r, h // 4, 0:nk],
                           inc=D_.full if j == parts - 1 else None)
                if 2 <= i < n + 2:
                    h, q = N_UNITS[i - 2]
                    pe.wait_ge(n_ring.full, n_ring.filled())
                    pe.wait_ge(tpr.free, tpr.given_back())
                    a, t = n_ring.take(), tpr.claim()
                    for j in range(parts):
                        for k in range(q + 1):
                            ins = pe.transpose(t[:, (2 * j + k) * P:(2 * j + k + 1) * P], a[:, j, k * P:(k + 1) * P], ident)
                    ins.then_inc(tpr.full, 1)
                if i >= 3:
                    h, q = N_UNITS[i - 3]
                    r = slice((h % 2) * HD, (h % 2 + 1) * HD)
                    f = slice((h // 4) * HD, (h // 4 + 1) * HD)
                    pe.wait_ge(nt_ring.full, nt_ring.filled())
                    pe.wait_ge(ot_ring.free, ot_ring.given_back())
                    t, o = nt_ring.take(), ot_ring.claim()
                    if cmp:
                        mm(o[r, 0:P], vcmp[0:N_CMP, h // 4, :], pcT[0:N_CMP, q, h, :], True, False)
                    steps = [(j, k) for j in range(parts) for k in range(q + 1)]
                    for x, (j, k) in enumerate(steps):
                        last = x == len(steps) - 1
                        mm(o[r, 0:P], values[j][:, k, f], t[:, 2 * j + k, :], not cmp and x == 0, last,
                           ot_ring.full if last else None)

        def act_rel(act, step, parts, sink):
            n = len(N_UNITS)
            for i in range(n + 2):
                if i < n:
                    h, q = N_UNITS[i]
                    nk = (q + 1) * P
                    act.wait_ge(s_ring.full, s_ring.filled())
                    act.wait_ge(e_ring.free, e_ring.given_back())
                    s, e, st = s_ring.take(), e_ring.claim(), st2[:, i % 8, :]
                    for j in range(parts):
                        step(act.activation(e[:, j, 0:nk], s[:, j, 0:nk], ACT.Exp, bias=st[:, j:j + 1],
                                            accum_out=st[:, 2 + j:3 + j]))
                    act.sem_inc(s_ring.free, 1)
                    if sink is not None:
                        step(act.activation(st[:, 6:7], sink(h), ACT.Exp, bias=st[:, 0:1]))
                    act.sem_inc(e_ring.full, 1)
                if i >= 2:
                    h, q = N_UNITS[i - 2]
                    act.wait_ge(tpr.full, tpr.filled())
                    act.wait_ge(nt_ring.free, nt_ring.given_back())
                    tp, t = tpr.take(), nt_ring.claim()
                    act.sem_inc(n_ring.free, 1)
                    src = tp.rearrange("p (j k b) -> p j k b", j=2, b=P)[:, 0:parts, 0:q + 1, :]
                    dst = t.rearrange("p (j k) b -> p j k b", j=2)[:, 0:parts, 0:q + 1, :]
                    step(act.activation(dst, src, ACT.Copy))
                    act.sem_inc(tpr.free, 1)
                    act.sem_inc(nt_ring.full, 1)

        def dve_rel(dve, step, parts, base, sink, gates, out_):
            n = len(N_UNITS)
            for i in range(n + 4):
                if i < n:
                    h, q = N_UNITS[i]
                    nk = (q + 1) * P
                    dve.wait_ge(D_.full, D_.filled())
                    dve.wait_ge(s_ring.free, s_ring.given_back())
                    bank, s, st = D_.take(), s_ring.claim(), st2[:, i % 8, :]
                    b = bank.rearrange("p (j k) -> p j k", j=2)[:, 0:parts, 0:nk]
                    bias = bias_of(base, h, q).unsqueeze(1).to_broadcast([P, parts, nk])
                    step(dve.scalar_tensor_tensor(out=s[:, 0:parts, 0:nk], in0=b, scalar=SCALE, in1=bias,
                                                  op0=ALU.mult, op1=ALU.add))
                    dve.sem_inc(D_.free, 1)
                    step(dve.tensor_reduce(st[:, 0:parts], s[:, 0:parts, 0:nk], AX, ALU.max))
                    if sink is not None:
                        step(dve.tensor_scalar(st[:, 0:1], st[:, 0:1], sink(h), -1.0, ALU.max, ALU.mult))
                    else:
                        step(dve.tensor_scalar(st[:, 0:parts], st[:, 0:parts], -1.0, None, ALU.mult))
                    dve.sem_inc(s_ring.full, 1)
                if 1 <= i < n + 1:
                    h, q = N_UNITS[i - 1]
                    nk = (q + 1) * P
                    dve.wait_ge(e_ring.full, e_ring.filled())
                    dve.wait_ge(n_ring.free, n_ring.given_back())
                    e, a, st = e_ring.take(), n_ring.claim(), st2[:, (i - 1) % 8, :]
                    if sink is not None:
                        step(dve.tensor_tensor(st[:, 2:3], st[:, 2:3], st[:, 6:7], ALU.add))
                    step(dve.reciprocal(st[:, 4:4 + parts], st[:, 2:2 + parts]))
                    if gates:
                        step(dve.tensor_tensor(st[:, 4:6], st[:, 4:6], ngate[:, q, 3 * h + 1:3 * h + 3], ALU.mult))
                    for j in range(parts):
                        step(dve.tensor_scalar(a[:, j, 0:nk], e[:, j, 0:nk], st[:, 4 + j:5 + j], None, ALU.mult))
                    dve.sem_inc(e_ring.free, 1)
                    dve.sem_inc(n_ring.full, 1)
                if i >= 4:
                    h, q = N_UNITS[i - 4]
                    r = slice((h % 2) * HD, (h % 2 + 1) * HD)
                    dve.wait_ge(ot_ring.full, ot_ring.filled())
                    o = ot_ring.take()
                    step(dve.tensor_copy(out_[r, h // 2, q * P:(q + 1) * P], o[r, 0:P]))
                    dve.sem_inc(ot_ring.free, 1)
                    dve.sem_inc(nt_ring.free, 1)

        def pe_nsa_attend(pe, W, mm):
            pe_rel(pe, mm, fN, [dup[:, 2], dup[:, 3]], [vsw[:, :, 0, :], vsw[:, :, 1, :]], True)

        def pe_swa_in(pe, W, mm, l):
            pe_project(pe, W, mm, "w_in", l, range(IN["sq"], IN["sv"], P), LAT, lambda _: D_, hT)
            pe.wait_ge(D_.free, D_.given_back(2))
            banks = [D_.claim() for _ in range(2)]
            for k in range(DC):
                w = W.next("w_in", l, k * P, IN["sv"])
                for t in range(2):
                    mm(banks[t][:, 0:P], hT[:, k, t * P:(t + 1) * P], w, k == 0, k == DC - 1,
                       D_.full if k == DC - 1 else None)
            pe.wait_ge(mix_ready.sem, mix_ready.due(pe))
            for g in range(2):
                pe.wait_ge(D_.free, D_.given_back())
                mm(D_.claim()[:, 0:LAT], const("sel", g, P), fS[:, 4, :]).then_inc(D_.full, 1)

        def dve_swa_in(dve, step, l):
            for i in range(5):
                copy_out(dve, fS[:, i, :], LAT)
            for t in range(2):
                copy_out(dve, vS[:, t, :], P)
            dve.drain().then_inc(mix_ready.sem, 1)
            for g in range(2):
                copy_out(dve, dupS[:, g, :], LAT)

        assert 2 * DC * TOK == B0 + DC * LAT
        merged = hT[:, :, 0:LAT]
        g_ring = ring("gate", [hU[:, 4 + i, :] for i in range(3)])
        mtmp = hU[:, 7, :]
        TO_SPLIT = [(hT[:, k, 0:LAT], z_hi[:, k], z_lo[:, k]) for k in range(DC)]
        TO_SPLIT += [(o[:, k], o_hi[:, i * RC + k], o_lo[:, i * RC + k]) for i, o in enumerate((oa, ob, oc))
                     for k in range(RC)]
        PRODUCT = DC + RC
        N_MERGE = 3 * DC

        def merge_groups(l):
            return groups_of("w_in", l, (N_MERGE * PRODUCT // DC + DC) * P, IN["gates"])

        def groups_due(n):
            return (PRODUCT * n + DC) // GROUP - ((PRODUCT * (n - 1) + DC) // GROUP if n else 0)

        def pe_merge(pe, W, mm, l):
            SW = SplitWeights(pe, W)
            for m in range(DC):
                for i, name in enumerate(("w_br_a", "w_br_b", "w_br_c")):
                    pe.wait_ge(A_.free, A_.given_back())
                    bank = A_.claim()
                    for k in range(DC):
                        if m == i == 0:
                            pe.wait_ge(h_ready.sem, h_ready.due(pe))
                        w = SW.next("w_in", l, k * P, IN["gates"] + i * D + m * P)
                        SW.mm(bank[:, 0:LAT], three(w, (z_hi[:, k], z_lo[:, k])), k == 0, k == DC - 1,
                              A_.full if k == DC - 1 else None)
                    pe.wait_ge(D_.free, D_.given_back())
                    bank = D_.claim()
                    for k in range(RC):
                        if m == 0:
                            pe.wait_ge(h_ready.sem, h_ready.due(pe))
                        o = o_hi[:, i * RC + k], o_lo[:, i * RC + k]
                        SW.mm(bank[:, 0:LAT], three(SW.next(name, l, k * P, m * P), o), k == 0, k == RC - 1,
                              D_.full if k == RC - 1 else None)
            for m in range(DC):
                pe.wait_ge(D_.free, D_.given_back())
                bank = D_.claim()
                for k in range(DC):
                    if m == 0:
                        pe.wait_ge(h_ready.sem, h_ready.due(pe))
                    w = SW.next("w_out", l, k * P, m * P)
                    SW.mm(bank[:, 0:LAT], three(w, (merged_hi[:, k], merged_lo[:, k])), k == 0, k == DC - 1,
                          D_.full if k == DC - 1 else None)
            SW.close()

        def act_merge(act, step, l):
            weights = SplitHi(act, merge_groups(l))
            for whole, hi, _ in TO_SPLIT:
                act.activation(hi, whole, ACT.Copy).then_inc(h_hi_ready.sem, 1)
            for n in range(N_MERGE + 1):
                if n < N_MERGE:
                    act.wait_ge(A_.full, A_.filled())
                    act.wait_ge(g_ring.free, g_ring.given_back())
                    bank, g = A_.take(), g_ring.claim()
                    step(act.activation(g, bank[:, 0:LAT], ACT.Sigmoid))
                    act.sem_inc(A_.free, 1)
                    act.sem_inc(g_ring.full, 1)
                    for _ in range(groups_due(n)):
                        weights.ahead()
                if n and n % 3 == 0:
                    m = n // 3 - 1
                    act.wait_ge(raw_ready.sem, raw_ready.due(act))
                    act.activation(merged_hi[:, m], merged[:, m], ACT.Copy).then_inc(h_hi_ready.sem, 1)
            for _ in range(DC):
                weights.ahead()

        def dve_merge(dve, step, l):
            weights = SplitLo(dve, step, merge_groups(l))
            for whole, hi, lo in TO_SPLIT:
                dve.wait_ge(h_hi_ready.sem, h_hi_ready.due(dve))
                dve.tensor_tensor(lo, whole, hi.bitcast(F32), ALU.subtract).then_inc(h_ready.sem, 1)
            for n in range(N_MERGE + 1):
                if n < N_MERGE:
                    for _ in range(groups_due(n)):
                        weights.ahead()
                if n and n % 3 == 0:
                    m = n // 3 - 1
                    dve.wait_ge(h_hi_ready.sem, h_hi_ready.due(dve))
                    dve.tensor_tensor(merged_lo[:, m], merged[:, m], merged_hi[:, m].bitcast(F32),
                                      ALU.subtract).then_inc(h_ready.sem, 1)
                if n < N_MERGE:
                    m, i = divmod(n, 3)
                    dve.wait_ge(D_.full, D_.filled())
                    dve.wait_ge(g_ring.full, g_ring.filled())
                    bank, g = D_.take(), g_ring.take()
                    dst = mtmp if i else merged[:, m]
                    step(dve.tensor_tensor(dst, g, bank[:, 0:LAT], ALU.mult))
                    dve.sem_inc(D_.free, 1)
                    dve.sem_inc(g_ring.free, 1)
                    if i:
                        step(dve.tensor_tensor(merged[:, m], merged[:, m], mtmp, ALU.add))
                    if i == 2:
                        dve.sem_inc(raw_ready.sem, 1)
            for m in range(DC):
                weights.ahead()
                dve.wait_ge(D_.full, D_.filled())
                bank = D_.take()
                step(dve.tensor_tensor(xT[:, m, 0:LAT], xT[:, m, 0:LAT], bank[:, 0:LAT], ALU.add))
                dve.sem_inc(D_.free, 1)

        E_ = Carve(B0)
        ztok = E_(QT, D)
        ytok = E_(QT, D)
        experts = E_(QT, SLOTS).bitcast(U32)
        gates_p = E_(QT, SLOTS)
        hbuf = E_(QT, SLOTS)
        subs = E_(QT, 2 * PEER_H, NKEYS)
        q_ring = ring("pq", [E_(LAT) for _ in range(2)])
        top_s = E_(2, PEER_K)
        top_i = E_(2, PEER_K)
        top_u = E_(2, PEER_K).bitcast(U32)
        cand = E_(PEER_K, PEER_K)
        pick = E_(2, PEER_K, PEER_K)
        best = E_(PEER_H, PEER_K)
        flat_u = E_(PEER_K).bitcast(U32)
        digit_u = E_(2, PEER_K).bitcast(U32)
        digit = E_(2, PEER_K)
        hsum = E_(PEER_H)
        GB = (ARENA - E_.at) // D
        rows = [E_(D) for _ in range(GB)]
        row_full = [sem(f"row_full{i}") for i in range(GB)]
        row_free = sem("row_free")
        ztok_ready = signal("ztok_ready")
        subs_ready = signal("subs_ready")
        experts_ready = signal("experts_ready")
        GATHERS = [(t, x, s) for t in range(QT) for x in range(2) for s in range(SLOTS)]

        def pe_peer(pe, W, mm, l):
            pe_norm(pe, mm, LAT)
            pe.wait_ge(h_ready.sem, h_ready.due(pe, DC))
            for t in range(QT):
                for half in range(2):
                    pe.wait_ge(A_.free, A_.given_back())
                    bank = A_.claim()
                    for k in range(4):
                        ins = pe.transpose(bank[:, k * P:(k + 1) * P], hT[:, 4 * half + k, t * P:(t + 1) * P], ident)
                    ins.then_inc(A_.full, 1)
            for i in range(2 * PEER_H):
                pe_project(pe, W, mm, "peer_wq", l, [i * P], LAT, lambda _: A_, hT)
                w = W.next("peer_subkeys", l, 0, i * P)
                pe.wait_ge(q_ring.full, q_ring.filled())
                qc = q_ring.take()
                pe.wait_ge(A_.free, A_.given_back())
                bank = A_.claim()
                for t in range(QT):
                    mm(bank[:, t * P:(t + 1) * P], qc[:, t * P:(t + 1) * P], w, inc=A_.full if t else None)

        def act_peer(act, step, l):
            act_norm(act, step, LAT, gained(act, "ln2", l))
            for t in range(QT):
                for half in range(2):
                    act.wait_ge(A_.full, A_.filled())
                    bank = A_.take()
                    step(act.activation(ztok[:, t, half * 512:(half + 1) * 512], bank, ACT.Copy))
                    act.sem_inc(A_.free, 1)
            act.sem_inc(ztok_ready.sem, 1)
            for i in range(2 * PEER_H):
                act.wait_ge(A_.full, A_.filled())
                bank = A_.take()
                act.wait_ge(q_ring.free, q_ring.given_back())
                qc = q_ring.claim()
                step(act.activation(qc, bank[:, 0:LAT], ACT.Copy))
                act.sem_inc(A_.free, 1)
                act.sem_inc(q_ring.full, 1)
                act.wait_ge(A_.full, A_.filled())
                bank = A_.take()
                act.sem_inc(q_ring.free, 1)
                step(act.activation(subs[:, :, i, :], bank[:, 0:2 * P].rearrange("p (t n) -> p t n", t=2), ACT.Copy))
                act.sem_inc(A_.free, 1)
                act.sem_inc(subs_ready.sem, 1)
            for t in range(QT):
                act.wait_ge(to_act.sem, to_act.due(act))
                step(act.activation(gates_p[:, t], gates_p[:, t], ACT.Exp))
                step(act.activation(hbuf[:, t], hbuf[:, t], ACT.Gelu))
                act.sem_inc(to_dve.sem, 1)

        def dve_top16(dve, step, src, vals, idx):
            step(dve.max(vals[:, 0:8], src))
            step(dve.max_index(idx[:, 0:8], vals[:, 0:8], src))
            step(dve.match_replace(src, vals[:, 0:8], src, -3.0e38))
            step(dve.max(vals[:, 8:16], src))
            step(dve.max_index(idx[:, 8:16], vals[:, 8:16], src))

        def dve_experts(dve, step, l, t, h):
            sq = [P, PEER_K, PEER_K]
            for x in range(2):
                if t == 0:
                    dve.wait_ge(subs_ready.sem, subs_ready.due(dve))
                dve_top16(dve, step, subs[:, t, 2 * h + x, :], top_s[:, x, :], top_u[:, x, :])
            step(dve.tensor_copy(top_i, top_u))
            step(dve.tensor_tensor(cand, top_s[:, 0, :].unsqueeze(2).to_broadcast(sq),
                                   top_s[:, 1, :].unsqueeze(1).to_broadcast(sq), ALU.add))
            dve_top16(dve, step, cand.rearrange("p a b -> p (a b)"), best[:, h, :], flat_u)
            dve.tensor_scalar(digit_u[:, 0], flat_u, 4, None, ALU.logical_shift_right)
            step(dve.tensor_scalar(digit_u[:, 1], flat_u, PEER_K - 1, None, ALU.bitwise_and))
            step(dve.tensor_copy(digit, digit_u))
            for x in range(2):
                step(dve.tensor_tensor(pick[:, x], digit[:, x].unsqueeze(2).to_broadcast(sq),
                                       const("iota").unsqueeze(1).to_broadcast(sq), ALU.is_equal))
                step(dve.tensor_tensor(pick[:, x], pick[:, x], top_i[:, x].unsqueeze(1).to_broadcast(sq), ALU.mult))
            step(dve.tensor_reduce(digit, pick, AX, ALU.add))
            step(dve.tensor_scalar(digit[:, 0], digit[:, 0], float(NKEYS), float(l * EXPERTS), ALU.mult, ALU.add))
            step(dve.tensor_tensor(experts[:, t, h * PEER_K:(h + 1) * PEER_K], digit[:, 0], digit[:, 1], ALU.add))
            dve.sem_inc(experts_ready.sem, 1)

        def pool_peer(pool, base):
            for n, (t, x, s) in enumerate(GATHERS):
                n += base
                if x == 0 and s % PEER_K == 0:
                    pool.wait_ge(experts_ready.sem, experts_ready.due(pool))
                if n >= GB:
                    pool.wait_ge(row_free, n - GB + 1)
                pool.indirect_dma_start(out=rows[n % GB], out_offset=None, in_=(peer_u, peer_v)[x],
                                        in_offset=bass.IndirectOffsetOnAxis(ap=experts[:, t, s:s + 1], axis=0)
                                        ).then_inc(row_full[n % GB], 16)

        def dve_peer(dve, step, l, base):
            dve_norm(dve, LAT)
            n = base
            for t in range(QT):
                dve_experts(dve, step, l, t, 0)
                if t == 0:
                    dve.wait_ge(ztok_ready.sem, ztok_ready.due(dve))
                for h in range(PEER_H):
                    if h + 1 < PEER_H:
                        dve_experts(dve, step, l, t, h + 1)
                    for s in range(h * PEER_K, (h + 1) * PEER_K):
                        r = rows[n % GB]
                        dve.wait_ge(row_full[n % GB], 16 * (n // GB + 1))
                        dve.tensor_tensor_reduce(r, r, ztok[:, t], 1.0, 0.0, ALU.mult, ALU.add,
                                                 hbuf[:, t, s:s + 1]).then_inc(row_free, 1)
                        n += 1
                gp = gates_p[:, t].rearrange("p (h j) -> p h j", h=PEER_H)
                dve.tensor_tensor(gp, best, best[:, :, 0:1].to_broadcast([P, PEER_H, PEER_K]), ALU.subtract)
                dve.drain().then_inc(to_act.sem, 1)
                dve.wait_ge(to_dve.sem, to_dve.due(dve))
                step(dve.tensor_reduce(hsum, gp, AX, ALU.add))
                step(dve.reciprocal(hsum, hsum))
                step(dve.tensor_tensor(gp, gp, hsum.unsqueeze(2).to_broadcast([P, PEER_H, PEER_K]), ALU.mult))
                step(dve.tensor_tensor(hbuf[:, t], hbuf[:, t], gates_p[:, t], ALU.mult))
                for s in range(SLOTS):
                    r, w = rows[n % GB], hbuf[:, t, s:s + 1]
                    dve.wait_ge(row_full[n % GB], 16 * (n // GB + 1))
                    if s == 0:
                        step(dve.tensor_scalar(ytok[:, t], r, w, None, ALU.mult))
                    else:
                        step(dve.scalar_tensor_tensor(out=ytok[:, t], in0=r, scalar=w, in1=ytok[:, t],
                                                      op0=ALU.mult, op1=ALU.add))
                    dve.sem_inc(row_free, 1)
                    n += 1

        def pe_peer_out(pe):
            for m in range(DC):
                pe.wait_ge(D_.free, D_.given_back())
                bank = D_.claim()
                for t in range(QT):
                    ins = pe.transpose(bank[:, t * P:(t + 1) * P], ytok[:, t, m * P:(m + 1) * P], ident)
                ins.then_inc(D_.full, 1)

        def dve_peer_out(dve, step):
            for m in range(DC):
                dve.wait_ge(D_.full, D_.filled())
                bank = D_.take()
                step(dve.tensor_tensor(xT[:, m, 0:LAT], xT[:, m, 0:LAT], bank[:, 0:LAT], ALU.add))
                dve.sem_inc(D_.free, 1)

        block = ctx.enter_context(nc.Block())
        FIRST_LOADS = 3
        GATHER_STAGE = 22
        SPLIT_STAGES = (1, 2, 4, 5, 7, 8, 10, 11, 21, 32)
        N_STAGES = 13 + 2 * 11 + 1
        out_done = signal("out_done", 16)

        @block.tensor
        def _(pe):
            W = Weights(pe)
            mm = make_mm(pe, W)

            def b_out():
                SW = SplitWeights(pe, W)
                pe_split_project(pe, SW, "b_w_o", range(0, D, P), LAT, D_, True)
                SW.close()

            pe.wait_ge(loaded.sem, loaded.due(pe, FIRST_LOADS))
            stages = [
                lambda: pe_ada(pe, W, mm, 0),
                lambda: pe_ffn(pe, W, mm, "pre", 0, TOK),
                lambda: pe_a_qkv(pe, W, mm),
                lambda: pe_a_attend(pe, W, mm),
                lambda: pe_a_out(pe, W, mm),
                lambda: pe_ffn(pe, W, mm, "post", 0, TOK),
                lambda: pe_ada(pe, W, mm, 1),
                lambda: pe_ffn(pe, W, mm, "pre", 1, TOK),
                lambda: pe_b_qkv(pe, W, mm),
                lambda: pe_b_attend(pe, W, mm),
                b_out,
                lambda: pe_ffn(pe, W, mm, "post", 1, LAT),
                lambda: pe_bias(pe, W, mm),
            ]
            for l in range(2):
                stages += [
                    lambda l=l: pe_rwkv_in(pe, W, mm, l),
                    lambda l=l: pe_rwkv_core(pe, W, mm, l),
                    lambda l=l: pe_rwkv_out(pe, W, mm, l),
                    lambda l=l: pe_nsa_in(pe, W, mm, l),
                    lambda: pe_nsa_cmp(pe, W, mm),
                    lambda: pe_nsa_attend(pe, W, mm),
                    lambda l=l: pe_swa_in(pe, W, mm, l),
                    lambda: pe_rel(pe, mm, fS, [dupS], [vS], False),
                    lambda l=l: pe_merge(pe, W, mm, l),
                    lambda l=l: pe_peer(pe, W, mm, l),
                    lambda: pe_peer_out(pe),
                ]
            stages.append(lambda: pe_norm(pe, mm, LAT))
            for n, s in enumerate(stages):
                s()
                if n + 1 in SPLIT_STAGES:
                    W.close()
                end_phase(pe)

        @block.scalar
        def _(act):
            step = Stepper(act, act_chain)

            def b_out():
                weights = SplitHi(act, groups_of("b_w_o", 0, D))
                for k in range(DC):
                    act.activation(h_hi[:, k, 0:LAT], oB[:, k, :], ACT.Copy).then_inc(h_hi_ready.sem, 1)
                for _ in range(DC):
                    weights.ahead()

            act.wait_ge(loaded.sem, loaded.due(act, FIRST_LOADS))
            stages = [
                lambda: act.activation(silu_cc[:, :, :], v("c", 0, 2 * DC).rearrange("p (k c) -> p k c", c=2),
                                       ACT.Silu).then_inc(silu_done.sem, 1),
                lambda: act_ffn(act, step, "pre", 0, 0, TOK),
                lambda: (act_a_qkv(act, step), act_lambda(act, step)),
                lambda: act_a_attend(act, step),
                lambda: act_a_out(act, step),
                lambda: act_ffn(act, step, "post", 0, 2, TOK),
                lambda: None,
                lambda: act_ffn(act, step, "pre", 1, 0, TOK),
                lambda: act_b_qkv(act, step),
                lambda: act_b_attend(act, step),
                b_out,
                lambda: act_ffn(act, step, "post", 1, 2, LAT),
                lambda: dma_bias(act),
            ]
            for l in range(2):
                stages += [
                    lambda l=l: act_rwkv_in(act, step, l),
                    lambda l=l: act_rwkv_core(act, step, l),
                    lambda l=l: act_rwkv_out(act, step, l),
                    lambda l=l: act_nsa_in(act, step, l),
                    lambda: act_nsa_cmp(act, step),
                    lambda: act_rel(act, step, 2, None),
                    lambda: None,
                    lambda l=l: act_rel(act, step, 1, lambda h: v("swa_sink", l * 8 + h)),
                    lambda l=l: act_merge(act, step, l),
                    lambda l=l: act_peer(act, step, l),
                    lambda: None,
                ]
            stages.append(lambda: act_norm(act, step, LAT, gained(act, "lnf", 0)))
            for n, s in enumerate(stages):
                s()
                end_phase(act)

        @block.vector
        def _(dve):
            step = Stepper(dve, dve_chain)
            dve.wait_ge(loaded.sem, loaded.due(dve, FIRST_LOADS))

            def b_out():
                weights = SplitLo(dve, step, groups_of("b_w_o", 0, D))
                for k in range(DC):
                    dve.wait_ge(h_hi_ready.sem, h_hi_ready.due(dve))
                    dve.tensor_tensor(h_lo[:, k, 0:LAT], oB[:, k, :], h_hi[:, k, 0:LAT].bitcast(F32),
                                      ALU.subtract).then_inc(h_ready.sem, 1)
                for m in range(DC):
                    weights.ahead()
                    dve.wait_ge(D_.full, D_.filled())
                    dve_residual(dve, D_.take(), m, 1, 1, LAT)

            stages = [
                lambda: dve_ada(dve, step, 0),
                lambda: dve_ffn(dve, step, "pre", 0, 0, TOK),
                lambda: dve_a_qkv(dve, step),
                lambda: dve_a_attend(dve, step),
                lambda: dve_a_out(dve, step),
                lambda: dve_ffn(dve, step, "post", 0, 2, TOK),
                lambda: dve_ada(dve, step, 1),
                lambda: dve_ffn(dve, step, "pre", 1, 0, TOK),
                lambda: dve_b_qkv(dve, step),
                lambda: dve_b_attend(dve, step),
                lambda: b_out(),
                lambda: dve_ffn(dve, step, "post", 1, 2, LAT),
                lambda: dve_bias(dve, step),
            ]
            for l in range(2):
                stages += [
                    lambda l=l: dve_rwkv_in(dve, step, l),
                    lambda l=l: dve_rwkv_core(dve, step, l),
                    lambda l=l: dve_rwkv_out(dve, step, l),
                    lambda l=l: dve_nsa_in(dve, step, l),
                    lambda: dve_nsa_cmp(dve, step),
                    lambda: dve_rel(dve, step, 2, 0, None, True, ob),
                    lambda l=l: dve_swa_in(dve, step, l),
                    lambda l=l: dve_rel(dve, step, 1, 8, lambda h: v("swa_sink", l * 8 + h), False, oc),
                    lambda l=l: dve_merge(dve, step, l),
                    lambda l=l: dve_peer(dve, step, l, l * len(GATHERS)),
                    lambda: dve_peer_out(dve, step),
                ]
            stages.append(lambda: dve_norm(dve, LAT))
            for n, s in enumerate(stages):
                s()
                end_phase(dve)

        @block.gpsimd
        def _(pool):
            step = Stepper(pool, pool_chain)
            for n in range(N_STAGES):
                for l in range(2):
                    if n == GATHER_STAGE + l * 11:
                        pool_peer(pool, l * len(GATHERS))
                end_phase(pool)

        @block.sync
        def _(sp):
            sp.dma_start(vec[:, :], vecs).then_inc(loaded.sem, 16)
            sp.dma_start(cst[:, :], consts).then_inc(loaded.sem, 16)
            sp.dma_start(xT[:, :, :], tokens).then_inc(loaded.sem, 16)
            for n in range(W_TILES):
                if n >= W_SLOTS:
                    sp.wait_ge(w_free, n - W_SLOTS + 1)
                sp.dma_start(wt[:, n % W_SLOTS, :], wstream[n]).then_inc(w_full[n % W_SLOTS], 16)
            sp.wait_ge(phase_done, 4 * max(phases.values()))
            sp.dma_start(out, hT[:, :, 0:LAT]).then_inc(out_done.sem, 16)
            sp.wait_ge(out_done.sem, 16)


def pack(inputs):
    def rows(a):
        return np.asarray(a, np.float32).reshape(-1, P).T

    def twice(a):
        return np.tile(np.asarray(a, np.float32).reshape(1, HD), 2).reshape(P, 1)

    def wide(a):
        a = np.asarray(a, np.float32).reshape(1, -1)
        return np.broadcast_to(a, (P, a.shape[1]))

    g = inputs
    vecs = np.zeros((P, N_VEC), np.float32)

    def put(name, a):
        at, w = VEC_AT[name]
        vecs[:, at:at + w] = a.reshape(P, w)

    put("c", np.stack([rows(g["c"]), rows(g["c_ctx"])], 2))
    put("ada_b", rows(g["ada_b"]))
    put("a_q_gain", twice(g["a_q_gain"]))
    put("a_k_gain", twice(g["a_k_gain"]))
    put("a_subln", rows(g["a_subln_gain"]))
    put("b_q_gain", twice(g["b_q_gain"]))
    put("b_k_gain", twice(g["b_k_gain"]))
    for name, key in (("ln1", "ln1_w_2"), ("ln2", "ln2_w_2"), ("lnf", "lnf_w_2"), ("mu", "rwkv_mu_2"),
                      ("w0", "rwkv_w0_2"), ("a0", "rwkv_a0_2"), ("k_k", "rwkv_k_k_2"), ("k_a", "rwkv_k_a_2"),
                      ("r_k", "rwkv_r_k_2"), ("ln_w", "rwkv_ln_w_2"), ("ln_b", "rwkv_ln_b_2")):
        put(name, rows(g[key]))
    for name, key in (("pe_k", "nsa_pe_k_2"), ("pe_v", "nsa_pe_v_2")):
        put(name, np.asarray(g[key]).reshape(2, 16, P).transpose(2, 0, 1))
    put("b_sink", wide(g["b_sink"]))
    put("swa_sink", wide(g["swa_sinks_2"]))
    put("lambda", wide(g["a_lambda"]))
    rel = np.zeros((P, 16), np.float32)
    rel[:32] = g["rel_bias_2"]
    rel[32] = 1
    put("rel", rel)

    arrays = {k.removesuffix("_2"): np.asarray(a) for k, a in g.items()
              if k.removesuffix("_2") in {e[0] for e in PLAN if isinstance(e, tuple)}}
    for k in ("a_w_qkv", "a_w_o", "b_w_qkv", "b_w_o"):
        assert arrays[k].shape[0] == 1
    arrays["rwkv_wa"] = np.concatenate([np.asarray(g["rwkv_w2_2"]), np.asarray(g["rwkv_a2_2"])], 1)
    arrays["peer_subkeys"] = np.asarray(g["peer_subkeys_2"]).transpose(0, 4, 1, 2, 3).reshape(2, P, -1)
    w = np.zeros((W_TILES, P, W_TILE * P), np.float32)
    for n, e in enumerate(PLAN):
        if isinstance(e, tuple):
            name, l, r, c, width = e
            b = arrays[name][l, r:r + P, c:c + width * P]
            t, at = divmod(n, W_TILE)
            w[t, :, at * P:at * P + b.shape[1]] = b
    tok = np.concatenate([np.asarray(g["x"])[0], np.asarray(g["ctx"])[0]], 0)
    tokens = np.ascontiguousarray(tok.T.reshape(DC, P, TOK).transpose(1, 0, 2))
    c, oh = constants()
    return {
        "wstream": w, "vecs": vecs, "consts": c, "onehots": oh, "tokens": tokens,
        "peer_u": np.ascontiguousarray(g["peer_u_2"]).reshape(2 * EXPERTS, D),
        "peer_v": np.ascontiguousarray(g["peer_v_2"]).reshape(2 * EXPERTS, D),
    }


def kernel(**inputs):
    import concourse.bacc as bacc
    from concourse.bass_utils import run_bass_kernel_spmd

    nc = bacc.Bacc("TRN2", target_bir_lowering=False, num_devices=1)
    arrays = pack(inputs)
    aps = [nc.dram_tensor(name, a.shape, mybir.dt.from_np(a.dtype), kind="ExternalInput").ap()
           for name, a in arrays.items()]
    out = nc.dram_tensor("out", (P, DC, LAT), F32, kind="ExternalOutput").ap()
    model_kernel(nc, *aps, out)
    r = run_bass_kernel_spmd(nc, [arrays], core_ids=[0])
    got = r.results[0]["out"]
    return got.transpose(2, 1, 0).reshape(1, LAT, D)
```
